# Optimizing a Trainium2 kernel written in Bass

```python
import jax, jax.numpy as jnp
from jax import lax
import numpy as np

D_MODEL = 1024
BATCH = 1
SEQ = 1024
DEPTH = 1
DEC_BATCH = 8
DEC_SEQ = 8
PAST_LEN = 1024
PAGE_SIZE = 128

ATT_HEADS = 8
HEAD_DIM = 64
ATT_W = ATT_HEADS * HEAD_DIM
CONV_W = D_MODEL // 2
CONV_K = 3
POOL_WINDOWS = (2, 4, 8, 16)
POOL_GROUPS = len(POOL_WINDOWS)
POOL_GW = D_MODEL // 8
POOL_W = POOL_GROUPS * POOL_GW
POOL_STATE = max(POOL_WINDOWS) - 1
N_BRANCH = 3
FF = -(-8 * D_MODEL // (3 * 256)) * 256
Q_BLOCK = 128
ALPHA = (2 * DEPTH) ** 0.25
BETA = (8 * DEPTH) ** -0.25
LN_EPS = 1e-5
FORGET_BIAS = 3.0

OFF_Q = 0
OFF_K = OFF_Q + ATT_W
OFF_V = OFF_K + ATT_W
OFF_F = OFF_V + ATT_W
OFF_CB = OFF_F + ATT_HEADS
OFF_CC = OFF_CB + CONV_W
OFF_CH = OFF_CC + CONV_W
OFF_P = OFF_CH + CONV_W
OFF_G = OFF_P + POOL_W
IN_W = OFF_G + N_BRANCH * D_MODEL

kernel_name = "hybrid_conv_pool_forgetting_attn_decoder_step"

def layer_norm(x, g, b):
    xf = x.astype(jnp.float32)
    mu = jnp.mean(xf, axis=-1, keepdims=True)
    var = jnp.mean(jnp.square(xf - mu), axis=-1, keepdims=True)
    return ((xf - mu) * lax.rsqrt(var + LN_EPS) * g + b).astype(x.dtype)

def forget_attention(q, k, v, dq, dk, q_pos, k_pos):
    s = jnp.einsum('bqhd,bkhd->bhqk', q, k).astype(jnp.float32) * (HEAD_DIM ** -0.5)
    s = s + jnp.transpose(dq, (0, 2, 1))[..., None] - jnp.transpose(dk, (0, 2, 1))[:, :, None, :]
    mask = k_pos[None, :] <= q_pos[:, None]
    s = jnp.where(mask, s, -jnp.inf)
    p = jax.nn.softmax(s, axis=-1)
    return jnp.einsum('bhqk,bkhd->bqhd', p.astype(v.dtype), v)

def causal_forget_attention(q, k, v, dq, dk, q_pos, k_pos):
    B, T = q.shape[0], q.shape[1]
    if T <= Q_BLOCK or T % Q_BLOCK:
        return forget_attention(q, k, v, dq, dk, q_pos, k_pos)
    nb = T // Q_BLOCK
    qb = q.reshape(B, nb, Q_BLOCK, ATT_HEADS, HEAD_DIM).swapaxes(0, 1)
    dqb = dq.reshape(B, nb, Q_BLOCK, ATT_HEADS).swapaxes(0, 1)
    pb = q_pos.reshape(nb, Q_BLOCK)
    out = lax.map(lambda a: forget_attention(a[0], k, v, a[1], dk, a[2], k_pos), (qb, dqb, pb))
    return out.swapaxes(0, 1).reshape(B, T, ATT_HEADS, HEAD_DIM)

def token_mixers(h, conv_prev, pool_prev, k_past, v_past, lf_past, lp):
    B, T, _ = h.shape
    P = k_past.shape[1]
    z = h @ lp['w_in']
    pos = P + jnp.arange(T)

    q = z[..., OFF_Q:OFF_K].reshape(B, T, ATT_HEADS, HEAD_DIM)
    k = z[..., OFF_K:OFF_V].reshape(B, T, ATT_HEADS, HEAD_DIM)
    v = z[..., OFF_V:OFF_F].reshape(B, T, ATT_HEADS, HEAD_DIM)
    lf = jax.nn.log_sigmoid((z[..., OFF_F:OFF_CB] + lp['b_forget']).astype(jnp.float32))
    k_all = jnp.concatenate([k_past.astype(k.dtype), k], axis=1)
    v_all = jnp.concatenate([v_past.astype(v.dtype), v], axis=1)
    d_all = jnp.cumsum(jnp.concatenate([lf_past.astype(jnp.float32), lf], axis=1), axis=1)
    k_pos = jnp.arange(P + T)
    att = causal_forget_attention(q, k_all, v_all, d_all[:, P:], d_all, pos, k_pos).reshape(B, T, ATT_W)

    gb = z[..., OFF_CB:OFF_CC]
    gc = z[..., OFF_CC:OFF_CH]
    u = gc * z[..., OFF_CH:OFF_P]
    u_ext = jnp.concatenate([conv_prev.astype(u.dtype), u], axis=1)
    cw = lp['conv_w']
    y = cw[0] * u_ext[:, 0:T]
    for j in range(1, CONV_K):
        y = y + cw[j] * u_ext[:, j:j + T]
    conv_out = gb * y

    p = z[..., OFF_P:OFF_G]
    p_ext = jnp.concatenate([pool_prev.astype(p.dtype), p], axis=1)
    cs = jnp.cumsum(jnp.pad(p_ext.astype(jnp.float32), ((0, 0), (1, 0), (0, 0))), axis=1)
    end = cs[:, POOL_STATE + 1:]
    means = []
    for g, w in enumerate(POOL_WINDOWS):
        sl = slice(g * POOL_GW, (g + 1) * POOL_GW)
        start = cs[:, POOL_STATE + 1 - w:POOL_STATE + 1 - w + T, sl]
        cnt = jnp.minimum(pos + 1, w).astype(jnp.float32)[None, :, None]
        means.append((end[..., sl] - start) / cnt)
    pooled = jnp.concatenate(means, axis=-1) - p.astype(jnp.float32)
    pooled = pooled.reshape(B, T, POOL_GROUPS, POOL_GW).astype(h.dtype)
    pool_out = jnp.einsum('btgc,gcd->btgd', pooled, lp['pool_w']).reshape(B, T, POOL_W) * lp['pool_scale']

    gates = jax.nn.sigmoid(z[..., OFF_G:].astype(jnp.float32)).astype(h.dtype).reshape(B, T, N_BRANCH, D_MODEL)
    merged = (gates[:, :, 0] * (att @ lp['w_br_attn'])
              + gates[:, :, 1] * (conv_out @ lp['w_br_conv'])
              + gates[:, :, 2] * (pool_out @ lp['w_br_pool']))
    out = merged @ lp['w_o']
    new_state = (k, v, lf, u_ext[:, -(CONV_K - 1):], p_ext[:, -POOL_STATE:])
    return out, new_state

def decoder_layer(x, c, conv_prev, pool_prev, k_past, v_past, lf_past, lp):
    mod = (jax.nn.silu(c) @ lp['ada_w'] + lp['ada_b'])[:, None, :]
    sh1, sc1, g1, sh2, sc2, g2 = jnp.split(mod, 6, axis=-1)
    mix, st = token_mixers(x * (1 + sc1) + sh1, conv_prev, pool_prev, k_past, v_past, lf_past, lp)
    x = layer_norm(ALPHA * x + g1 * mix, lp['ln1_g'], lp['ln1_b'])
    h2 = x * (1 + sc2) + sh2
    a, b = jnp.split(h2 @ lp['w_gate_up'], 2, axis=-1)
    f = (jax.nn.silu(a) * b) @ lp['w_down']
    x = layer_norm(ALPHA * x + g2 * f, lp['ln2_g'], lp['ln2_b'])
    return x, st

def setup_inputs(seed: int = 0) -> dict:
    key = jax.random.key(seed)
    ks = jax.random.split(key, 32)

    def nrm(i, shape, scale):
        return jax.random.normal(ks[i], shape, jnp.float32) * scale

    n_pages = PAST_LEN // PAGE_SIZE
    n_used = DEC_BATCH * n_pages
    n_pool = n_used + max(1, n_used // 4)
    D = D_MODEL
    return {
        'x_prompt': nrm(0, (BATCH, SEQ, D), 1.0),
        'x_sample': nrm(1, (DEC_BATCH, DEC_SEQ, D), 1.0),
        'cache_k': nrm(2, (DEPTH, n_pool, PAGE_SIZE, ATT_HEADS, HEAD_DIM), 1.0),
        'cache_v': nrm(3, (DEPTH, n_pool, PAGE_SIZE, ATT_HEADS, HEAD_DIM), 1.0),
        'cache_logf': jax.nn.log_sigmoid(FORGET_BIAS + nrm(4, (DEPTH, n_pool, PAGE_SIZE, ATT_HEADS), 1.0)),
        'state_conv': nrm(5, (DEPTH, DEC_BATCH, CONV_K - 1, CONV_W), 1.0),
        'state_pool': nrm(6, (DEPTH, DEC_BATCH, POOL_STATE, POOL_W), 1.0),
        'page_table': jax.random.permutation(ks[7], n_pool)[:n_used].reshape(DEC_BATCH, n_pages).astype(jnp.int32),
        'c_prompt': nrm(8, (BATCH, D), 1.0),
        'c_sample': nrm(9, (DEC_BATCH, D), 1.0),
        'ada_w': nrm(10, (DEPTH, D, 6 * D), 0.5 * D ** -0.5),
        'ada_b': nrm(11, (DEPTH, 6 * D), 0.02),
        'w_in': nrm(12, (DEPTH, D, IN_W), D ** -0.5),
        'b_forget': FORGET_BIAS + nrm(13, (DEPTH, ATT_HEADS), 0.1),
        'conv_w': nrm(14, (DEPTH, CONV_K, CONV_W), CONV_K ** -0.5),
        'pool_w': nrm(15, (DEPTH, POOL_GROUPS, POOL_GW, POOL_GW), POOL_GW ** -0.5),
        'pool_scale': 1.0 + nrm(16, (DEPTH, POOL_W), 0.1),
        'w_br_attn': nrm(17, (DEPTH, ATT_W, D), ATT_W ** -0.5),
        'w_br_conv': nrm(18, (DEPTH, CONV_W, D), CONV_W ** -0.5),
        'w_br_pool': nrm(19, (DEPTH, POOL_W, D), POOL_W ** -0.5),
        'w_o': nrm(20, (DEPTH, D, D), BETA * D ** -0.5),
        'ln1_g': 1.0 + nrm(21, (DEPTH, D), 0.05),
        'ln1_b': nrm(22, (DEPTH, D), 0.02),
        'w_gate_up': nrm(23, (DEPTH, D, 2 * FF), D ** -0.5),
        'w_down': nrm(24, (DEPTH, FF, D), BETA * FF ** -0.5),
        'ln2_g': 1.0 + nrm(25, (DEPTH, D), 0.05),
        'ln2_b': nrm(26, (DEPTH, D), 0.02),
    }

def reference(x_prompt, x_sample, cache_k, cache_v, cache_logf, state_conv, state_pool, page_table,
              c_prompt, c_sample, ada_w, ada_b, w_in, b_forget, conv_w, pool_w, pool_scale,
              w_br_attn, w_br_conv, w_br_pool, w_o, ln1_g, ln1_b, w_gate_up, w_down, ln2_g, ln2_b):
    xp, xs = x_prompt, x_sample
    Bp, Bs = xp.shape[0], xs.shape[0]
    empty_kv = jnp.zeros((Bp, 0, ATT_HEADS, HEAD_DIM), xp.dtype)
    empty_lf = jnp.zeros((Bp, 0, ATT_HEADS), jnp.float32)
    conv0 = jnp.zeros((Bp, CONV_K - 1, CONV_W), xp.dtype)
    pool0 = jnp.zeros((Bp, POOL_STATE, POOL_W), xp.dtype)
    sp = ([], [], [], [], [])
    ss = ([], [], [], [], [])
    for l in range(DEPTH):
        lp = dict(ada_w=ada_w[l], ada_b=ada_b[l], w_in=w_in[l], b_forget=b_forget[l], conv_w=conv_w[l],
                  pool_w=pool_w[l], pool_scale=pool_scale[l], w_br_attn=w_br_attn[l], w_br_conv=w_br_conv[l],
                  w_br_pool=w_br_pool[l], w_o=w_o[l], ln1_g=ln1_g[l], ln1_b=ln1_b[l],
                  w_gate_up=w_gate_up[l], w_down=w_down[l], ln2_g=ln2_g[l], ln2_b=ln2_b[l])
        xp, st_p = decoder_layer(xp, c_prompt, conv0, pool0, empty_kv, empty_kv, empty_lf, lp)
        k_past = cache_k[l][page_table].reshape(Bs, -1, ATT_HEADS, HEAD_DIM)
        v_past = cache_v[l][page_table].reshape(Bs, -1, ATT_HEADS, HEAD_DIM)
        lf_past = cache_logf[l][page_table].reshape(Bs, -1, ATT_HEADS)
        xs, st_s = decoder_layer(xs, c_sample, state_conv[l], state_pool[l], k_past, v_past, lf_past, lp)
        for i in range(5):
            sp[i].append(st_p[i])
            ss[i].append(st_s[i])
    k_p, v_p, lf_p, conv_p, pool_p = [jnp.stack(a) for a in sp]
    k_s, v_s, lf_s, conv_s, pool_s = [jnp.stack(a) for a in ss]
    return (xp, xs, k_p, v_p, lf_p, conv_p, pool_p, k_s, v_s, lf_s, conv_s, pool_s)


_drawn_inputs = setup_inputs


def setup_inputs(seed=0):
    import zlib

    import numpy as np

    out = dict(_drawn_inputs(seed))
    spreads = {}
    factors = {'cache_k': 4.057,
     'cache_v': 3.306,
     'cache_logf': 8.0,
     'pool_scale': 7.658,
     'ln1_b': 2.821,
     'ln2_b': 2.805}
    for name, (base, spread) in spreads.items():
        noise = np.random.default_rng([zlib.crc32(name.encode()), seed]).standard_normal(out[name].shape)
        drawn = base * np.exp(spread * noise) if base else spread * noise
        out[name] = __import__('jax').numpy.asarray(drawn.astype(out[name].dtype))
    for name, factor in factors.items():
        out[name] = (out[name] * factor).astype(out[name].dtype)
    return out
```

```python
from contextlib import ExitStack

import numpy as np

import concourse.bass as bass
from concourse import mybir

F32 = mybir.dt.float32
F32R = mybir.dt.float32r
I32 = mybir.dt.int32
ALU = mybir.AluOpType
ACT = mybir.ActivationFunctionType

P = 128
D = 1024
KD = D // P
NP = 1024
QT = NP // P
DB, DS = 8, 8
NS = DB * DS
T = 1092
TU = NP + NS
CH = T // 3
SC = NP - 2 * CH
H, HD = 8, 64
HP = H // 2
PAST, PAGE = 1024, 128
NPG = PAST // PAGE
LK = PAST + DS
HALF = 512
NT = HALF // P
POOL_WIN = (2, 4, 8, 16)
PST = 15
LEAD = 16
FF = 2816
FFIT = FF // (2 * P)
OFF_Q, OFF_K, OFF_V, OFF_F = 0, HALF, 2 * HALF, 3 * HALF
OFF_CB = OFF_F + H
OFF_CC, OFF_CH, OFF_P, OFF_G = (OFF_CB + i * HALF for i in (1, 2, 3, 4))
ALPHA = 2 ** 0.25
EPS = 1e-5
NEG = -1.0e30
NCOND = 1 + DB
SH1, SC1, G1, SH2, SC2, G2 = (KD * i for i in range(6))
ADAC = 6 * D // 512
V_ADA, V_L1G, V_L1B, V_CW, V_PS, NVEC = 0, 48, 56, 64, 76, 80
U_F, U_QKV, U_BRA, U_CONV, U_BRC, U_POOL, U_BRP, U_WO, U_FF0, U_FF, U_FFE, U_END = (
    0, 1, 13, 25, 37, 49, 54, 66, 74, 78, 138, 140)
RING = 3
NTILE = 2 * QT
GROUPS = [(r * QT + i, list(range(j, min(j + 4, i + 1))))
          for r in range(2) for i in range(QT) for j in range(0, i + 1, 4)]
NG = len(GROUPS)
LAST_GROUP = [max(g for g, (n, _) in enumerate(GROUPS) if n == t) for t in range(NTILE)]


class Links:

    def __init__(self, eng, sem):
        self.eng, self.sem, self.n, self.off = eng, sem, 0, 0

    def __call__(self, ins):
        ins.then_inc(self.sem, 1)
        self.n += 1
        self.eng.wait_ge(self.sem, self.off + self.n)

    def enter(self, turn, per):
        self.base, self.per, self.off, self.n = self.n, per, turn * per + self.n, 0

    def leave(self, turns):
        assert self.n == self.per, f"{self.n} links in the loop's body, not {self.per}"
        self.off, self.n = 0, self.base + turns * self.per


def build(nc, a, out):
    with ExitStack() as ctx:
        def sem(name):
            return ctx.enter_context(nc.semaphore(name))

        size = (nc.sbuf_bytes_remaining - 64) // 128 * 128
        ctx.enter_context(nc.sbuf_tensor("arena", [P, size // 4], F32))
        base = (nc.sbuf_base - size + 31) // 32 * 32

        class Region:
            def __init__(self, off, size):
                self.off, self.end = off, off + size

            def __call__(self, name, shape, dt=F32):
                o = self.off
                self.off += (4 * int(np.prod(shape[1:])) + 31) // 32 * 32
                assert self.off <= self.end, (name, self.off - self.end)
                return nc.alloc_sbuf_tensor_at(name, shape, dt, offset=o)

        HSZ, MSZ = 4 * 2 * KD * T, 4 * KD * T
        r_h, r_a = base, base + HSZ
        r_m = r_a + MSZ
        r_w = r_m + MSZ
        keep = Region(r_w, base + size - r_w)

        raw = [keep(f"raw{i}", [P, 8, P]) for i in range(RING)]
        whi = [keep(f"whi{i}", [P, 8, P], F32R) for i in range(RING)]
        wlo = [keep(f"wlo{i}", [P, 8, P], F32R) for i in range(RING)]
        ident = keep("ident", [P, P])
        identr = keep("identr", [P, P], F32R)
        maskr = keep("maskr", [P, P], F32R)
        mod = keep("mod", [P, 6 * KD, NCOND])
        vecs = keep("vecs", [P, NVEC])
        q_s = keep("q_s", [P, HP, NS])
        k_s = keep("k_s", [P, HP, NS])
        pst = keep("pst", [P, NT, DB * PST])
        cst = keep("cst", [P, NT, DB * 2])
        recip = keep("recip", [P, LEAD])
        zeros = keep("zeros", [P, 16])
        ones = keep("ones", [P, 1])
        stat = keep("stat", [P, 16])
        rowmax, negmax, rowsum, rowinv = (stat[:, 2 * i:2 * i + 2] for i in range(4))
        bfor = keep("bfor", [H, 1])
        ptab = keep("ptab", [1, DB * NPG], I32)
        maskn = keep("maskn", [NS, DS])
        fold = keep("fold", [NS, DS])
        blockmask = keep("blockmask", [NS, H])
        r_s, r_end = keep.off, base + size

        hhi = Region(r_h, HSZ)("hhi", [P, KD, T], F32R)
        hlo = Region(r_h + HSZ // 2, HSZ // 2)("hlo", [P, KD, T], F32R)
        merged = Region(r_m, MSZ)("merged", [P, KD, T])
        ahi = Region(r_a, MSZ // 2)("ahi", [P, NT, T], F32R)
        alo = Region(r_a + MSZ // 2, MSZ // 2)("alo", [P, NT, T], F32R)

        R = Region(r_h, HSZ)
        xtok = R("xtok", [P, QT + 1, D])
        c9 = R("c9", [NCOND, D])
        c9s = R("c9s", [NCOND, D])
        vtab = R("vtab", [NVEC, P])
        stok = R("stok", [DB * PST, HALF])
        ctok = R("ctok", [DB * 2, HALF])
        lfpast = R("lfpast", [P, NPG, DB, H])
        fill = R("fill", [P, P])
        foldh, maskh = R("foldh", [NS, H, DS]), R("maskh", [NS, H, DS])
        R = Region(r_a, MSZ)
        ada = [R("ada0", [P, KD, 512]), R("ada1", [P, KD, 512])]
        S = Region(r_s, r_end - r_s)
        ada.append(S("ada2", [P, KD, 512]))
        modrow = S("modrow", [NCOND, 2, 512])
        ct = S("ct", [P, KD, NCOND])
        lfall = S("lfall", [NS, LK])
        xt = Region(r_m, MSZ)("xt", [P, KD, T])
        R = Region(r_m, MSZ)
        z8, nl8, e8 = R("z8", [H, T]), R("nl8", [H, T]), R("e8", [H, T])
        dsamp = R("dsamp", [NS, LK])
        lfo = R("lfo", [P, QT, H])
        lfs = R("lfs", [NS, H])
        R = Region(r_m, MSZ)
        qhi, qlo = R("qhi", [P, T], F32R), R("qlo", [P, T], F32R)
        khi, klo = R("khi", [P, T], F32R), R("klo", [P, T], F32R)
        kv = R("kv", [P, T])
        vhi, vlo = R("vhi", [P, QT, P], F32R), R("vlo", [P, QT, P], F32R)
        S = Region(r_s, r_end - r_s)
        decay = S("decay", [P, 2, NP])
        tok = R("tok", [P, QT + 1, P])
        pthi = [S(f"pthi{i}", [P, 4, P], F32R) for i in range(3)]
        ptlo = [S(f"ptlo{i}", [P, 4, P], F32R) for i in range(3)]
        prob = [S("prob0", [P, NP]), S("prob1", [P, NP])]
        R = Region(r_m, MSZ)
        kpage = R("kpage", [P, NPG, HALF])
        kt_s = R("kt_s", [P, HP, LK])
        S = Region(r_s, r_end - r_s)
        vpage = S("vpage", [P, NPG + 1, HALF])
        decs = S("decs", [NS, LK])
        ptrs = S("ptrs", [P, NPG + 1, NS])
        qbd = S("qbd", [P, 320])
        om = R("om", [NS, HALF])
        S = Region(r_s, r_end - r_s)
        sg = [S("sg0", [P, T]), S("sg1", [P, T])]
        part = [S("part0", [P, T]), S("part1", [P, T])]
        S = Region(r_s, r_end - r_s)
        cc = S("cc", [P, T])
        u = S("u", [P, 2 + T])
        us = S("us", [P, DB, 2 + DS])
        yc = S("yc", [P, T])
        ulast = S("ulast", [P, 18])
        utok = S("utok", [18, P])
        S = Region(r_s, r_end - r_s)
        pb = S("pb", [P, LEAD + T])
        w1, w2 = S("w1", [P, LEAD + NP]), S("w2", [P, LEAD + NP])
        ps0, ps1, ps2 = (S(f"ps{i}", [P, DB, LEAD + DS]) for i in range(3))
        yp = S("yp", [P, T])
        ptok = S("ptok", [NS, 2, P])
        S = Region(r_s, r_end - r_s)
        xr = [S("xr0", [P, T]), S("xr1", [P, T])]
        tmp = [S("tmp0", [P, T]), S("tmp1", [P, T])]
        rstd = S("rstd", [P, T])
        mean1 = S("mean1", [P, P])
        S = Region(r_s, r_end - r_s)
        sil = [S("sil0", [P, T]), S("sil1", [P, T])]
        ft = [S("ft0", [P, T]), S("ft1", [P, T])]
        t64 = S("t64", [P, 2, NS])
        R = Region(r_h, HSZ)
        gb = R("gb", [P, 2, D])
        yo = [R(f"yo{i}", [P, D]) for i in range(3)]
        bst = R("bst", [P, 2, 2, 6])
        mv = R("mv", [P, 2, 4])

        def pst_(name, shape):
            return ctx.enter_context(nc.psum_tensor(name, shape, F32))

        psA, psB = pst_("psA", [P, 3, 512]), pst_("psB", [P, 3, 512])
        mi = [pst_("ps6", [P, 512]), pst_("ps7", [P, 512])]
        GP = [psA, psB]

        def cols(ps, n=P):
            return ps[0:n, :, 0:CH]

        def c3(x):
            return x.rearrange("p (c n) -> p c n", c=3)

        def flat(ps):
            return ps[:, :, :].rearrange("p a b -> p (a b)")

        def scratch(name, shape):
            return nc.dram_tensor(name, shape, F32).ap()

        x_keep = scratch("x_keep", [P, KD, T])
        nd_p = scratch("nd_p", [H, NP])
        nd_s = scratch("nd_s", [NS, LK])

        w_in, w_gu, w_dn, w_o = a["w_in"][0], a["w_gate_up"][0], a["w_down"][0], a["w_o"][0]

        names = """c_in vec_in x_in st_in lfp_in bf_in pt_in ada0_in ada1_in ada2_in copied
            consts eye idle c_silu       lfp_tr lfp_copied
            x_tr x_dve x_act x_stored xt_done xt_mod ada_used modrow_done mod_tr mod_done hhi_done hlo_done
            raw0 raw1 raw2 w_split w_used dve_link act_link pool_link
            gemm_done z_done setup_tr setup_copied e_done lf_done lf_tr  lfs_out lfnew_in scan_done nd_out lfo_out
            q_done k_done v_done qhi_done ql_done kv_done kl_done vf_done tok_tr tok_copied
            kst vst vl_done decay_in
            s_done mx_done p_done pn_done tr_done pth_done ptl_done o_done ah_done al_done
            kpg_in vpg_in dec_in vnew_in kt_tr kt_act kt_dve  qbd_done ss_done sm_done se_done sp_done
            pt_tr pt_act pt_dve ov_done om_done fold_done sah_done sal_done pad_done sconst qbd_zero
            cb_done cc_done ch_done cc_copied u_done y_done chi_done clo_done ul_done ul_tr ul_copied ul_out
             pcopied pf_done phi_done plo_done pt2_tr pt2_copied pt2_out  mhi_done mlo_done
               wo_ev xr0_in xr1_in mean_done d_done sq_done var_done ve_done sd_done 
            xn_done x1_done h2_done   xa_done 
            fg_done fu_done sil_done ft_done fhi_done flo_done dn_done dn_ev dn_part
            gb_in yt_done yv_done ysd_done yn_done yg_done y0_out y1_out y2_out""".split()
        s = {n: sem(n) for n in names}
        for n in ("gA", "gB", "bA", "bB", "sgA", "sgB", "mA", "mB"):
            s[n] = sem(n)
        raw_in = [s["raw0"], s["raw1"], s["raw2"]]
        ada_in = [s["ada0_in"], s["ada1_in"], s["ada2_in"]]

        def x_group(g):
            if g < 2 * KD:
                return xt[:, g // 2, 512 * (g % 2):512 * (g % 2) + 512]
            return xt[:, 4 * (g - 2 * KD):4 * (g - 2 * KD) + 4, NP:TU]

        def x_bank(g):
            ps = psB[:, g % 3, 0:512 if g < 2 * KD else 4 * NS]
            return ps if g < 2 * KD else ps.rearrange("p (a b) -> p a b", b=NS)

        def modrow_copy(act, j):
            act.wait_ge(s["ada_used"], j + 1)
            if j >= 2:
                act.wait_ge(s["mod_tr"], j - 1)
            nc.scalar.copy(modrow[:, j % 2, :], psA[0:NCOND, j % 2, :]).then_inc(s["modrow_done"], 1)

        def h2_high(act, k):
            act.wait_ge(s["h2_done"], k + 1)
            nc.scalar.copy(hhi[:, k, :], tmp[k % 2][:, :]).then_inc(s["hhi_done"], 1)

        def apart(eng):
            eng.sem_inc(s["idle"], 1)

        block = ctx.enter_context(nc.Block())

        @block.sync
        def _(sp):
            def wunit(u, slot, src, shape=None):
                if not isinstance(u, int) or u >= RING:
                    sp.wait_ge(s["w_split"], u - RING + 1)
                    if not isinstance(u, int):
                        apart(sp)
                dst = raw[slot][:, :, :]
                if shape:
                    dst = dst.rearrange("p (k j) n -> p k (j n)", k=shape)
                sp.dma_start(dst, src).then_inc(raw_in[slot], 16)

            def tiles(w, c, n=P):
                return w.rearrange("(k p) n -> p k n", p=P)[:, :, bass.ds(c, n)]

            sp.dma_start(c9[0:1, :], a["c_prompt"]).then_inc(s["c_in"], 16)
            sp.dma_start(c9[1:NCOND, :], a["c_sample"]).then_inc(s["c_in"], 16)
            sp.dma_start(ptab[:, :], a["page_table"].rearrange("b (o n) -> o (b n)", o=1)).then_inc(s["pt_in"], 16)
            sp.dma_start(stok[:, :], a["state_pool"].rearrange("o b t c -> (o b t) c")).then_inc(s["st_in"], 16)
            sp.dma_start(ctok[:, :], a["state_conv"].rearrange("o b t c -> (o b t) c")).then_inc(s["st_in"], 16)
            sp.dma_start(bfor[:, :], a["b_forget"].rearrange("o h -> h o")).then_inc(s["bf_in"], 16)
            xv = a["x_prompt"][0].rearrange("(n p) d -> p n d", p=P)
            for j in range(2):
                sp.dma_start(xtok[:, 4 * j:4 * j + 4, :], xv[:, 4 * j:4 * j + 4, :]).then_inc(s["x_in"], 16)
            sp.dma_start(xtok[0:NS, QT, :], a["x_sample"].rearrange("b t d -> (b t) d")).then_inc(s["x_in"], 16)
            for row, src in ((V_ADA, a["ada_b"].rearrange("o (t p) -> (o t) p", p=P)),
                             (V_L1G, a["ln1_g"].rearrange("o (t p) -> (o t) p", p=P)),
                             (V_L1B, a["ln1_b"].rearrange("o (t p) -> (o t) p", p=P)),
                             (V_CW, a["conv_w"].rearrange("o k (t p) -> (o k t) p", p=P)),
                             (V_PS, a["pool_scale"].rearrange("o (t p) -> (o t) p", p=P))):
                sp.dma_start(vtab[row:row + src.shape[0], :], src).then_inc(s["vec_in"], 16)
            adav = a["ada_w"][0].rearrange("(k p) n -> p k n", p=P)

            def ada_chunk(j):
                if j >= 3:
                    sp.wait_ge(s["ada_used"], j - 2)
                sp.dma_start(ada[j % 3][:, :, :], adav[:, :, 512 * j:512 * j + 512]).then_inc(ada_in[j % 3], 16)

            for j in range(4):
                ada_chunk(j)
            sp.dma_start(out["pool_sample"][0, :, 0:PST - DS, :], a["state_pool"][0, :, DS:PST, :]).then_inc(s["copied"], 16)
            sp.wait_ge(s["pt_in"], 16)
            with sp.Fori(0, DB) as b:
                for g in range(NPG):
                    page = sp.value_load(ptab[0:1, bass.ds(b * NPG + g, 1)], min_val=0, max_val=a["cache_logf"].shape[1] - 1)
                    sp.dma_start(lfpast[:, g, bass.ds(b, 1), :],
                                 a["cache_logf"][0, bass.ds(page, 1), :, :].rearrange("o p h -> p o h")).then_inc(s["lfp_in"], 16)
            for j in range(4, 7):
                ada_chunk(j)
            sp.wait_ge(s["xt_done"], 1)
            sp.wait_ge(s["x_dve"], 9)
            sp.wait_ge(s["x_act"], 9)
            sp.dma_start(x_keep, xt[:, :, :]).then_inc(s["x_stored"], 16)
            for j in range(7, ADAC):
                ada_chunk(j)
            wunit(0, 0, tiles(w_in, OFF_F))
            for j in range(2):
                wunit(1 + j, 1 + j, tiles(w_in, (OFF_Q, OFF_K)[j]))
            wunit(3, 0, tiles(w_in, OFF_V))
            with sp.Fori(1, HP) as p:
                for j, off in enumerate((OFF_Q, OFF_K, OFF_V)):
                    wunit(p * 3 + (U_QKV + j), (U_QKV + j) % RING, tiles(w_in, p * P + off))
            sp.wait_ge(s["al_done"], NTILE * HP)
            sp.wait_ge(s["vl_done"], HP)
            sp.wait_ge(s["vst"], 32 * HP)
            sp.wait_ge(s["kst"], 32 * HP)
            sp.wait_ge(s["o_done"], NTILE * HP)

            def sample_loads(b):
                for g in range(NPG):
                    page = sp.value_load(ptab[0:1, bass.ds(b * NPG + g, 1)], min_val=0, max_val=a["cache_k"].shape[1] - 1)
                    for buf, name, si in ((kpage, "cache_k", "kpg_in"), (vpage, "cache_v", "vpg_in")):
                        sp.dma_start(buf[:, g, :], a[name][0, bass.ds(page, 1)].rearrange("o p h d -> p (o h d)")).then_inc(s[si], 16)
                sp.dma_start(vpage[0:DS, NPG, :],
                             out["v_sample"][0, bass.ds(b, 1)].rearrange("o t h d -> t (o h d)")).then_inc(s["vnew_in"], 16)
                for h in range(H):
                    sp.dma_start(decs[h * DS:(h + 1) * DS, :],
                                 nd_s[bass.ds(b * H + h, 1), :].to_broadcast([DS, LK])).then_inc(s["dec_in"], 16)

            sample_loads(0)
            with sp.Fori(1, DB) as b:
                sp.wait_ge(s["kt_tr"], b * 2 * HP)
                sp.wait_ge(s["ov_done"], b)
                apart(sp)
                sample_loads(b)

            def branch_loads(u0, gate, w):
                with sp.Fori(0, 4) as i:
                    for j in range(2):
                        wunit(i * 3 + (u0 + j), (u0 + j) % RING, tiles(w_in, i * 256 + (OFF_G + gate * D + j * P)))
                    wunit(i * 3 + (u0 + 2), (u0 + 2) % RING, tiles(w, i * 256, 256), 4)

            branch_loads(U_BRA, 0, a["w_br_attn"][0])
            with sp.Fori(0, NT) as i:
                for j, off in enumerate((OFF_CC, OFF_CH, OFF_CB)):
                    wunit(i * 3 + (U_CONV + j), (U_CONV + j) % RING, tiles(w_in, i * P + off))
            branch_loads(U_BRC, 1, a["w_br_conv"][0])
            for j in range(4):
                wunit(U_POOL + j, (U_POOL + j) % RING, tiles(w_in, OFF_P + j * P))
            sp.wait_ge(s["w_split"], U_POOL + 4 - RING + 1)
            sp.dma_start(raw[(U_POOL + 4) % RING][:, 0:NT, :],
                         a["pool_w"][0].rearrange("g c d -> c g d")).then_inc(raw_in[(U_POOL + 4) % RING], 16)
            branch_loads(U_BRP, 2, a["w_br_pool"][0])
            for j in range(KD):
                wunit(U_WO + j, (U_WO + j) % RING, tiles(w_o, j * P))

            def ff_cols(u0, slot, i, f):
                for j in range(2):
                    wunit(u0 + j, (slot + j) % RING, tiles(w_gu, i * 256 + (j * FF + f * P)))

            def dn_rows(u0, slot, i):
                rows = w_dn.rearrange("(i k p) n -> i p k n", k=2, p=P)
                for j in range(2):
                    src = rows[bass.ds(i, 1), :, :, j * 512:j * 512 + 512].rearrange("o p k n -> p (o k) n")
                    wunit(u0 + j, (slot + j) % RING, src, 2)

            ff_cols(U_FF0, U_FF0, 0, 0)
            ff_cols(U_FF0 + 2, U_FF0 + 2, 0, 1)
            with sp.Fori(1, FFIT) as i:
                u0 = i * 6 + (U_FF - 6)
                ff_cols(u0, U_FF, i, 0)
                dn_rows(u0 + 2, U_FF + 2, i - 1)
                ff_cols(u0 + 4, U_FF + 4, i, 1)
            dn_rows(U_FFE, U_FFE, FFIT - 1)
            sp.wait_ge(s["fg_done"], 2 * FFIT)
            sp.wait_ge(s["fu_done"], 2 * FFIT)
            sp.dma_start(gb[:, 0, :], a["ln2_g"].to_broadcast([P, D])).then_inc(s["gb_in"], 16)
            sp.dma_start(gb[:, 1, :], a["ln2_b"].to_broadcast([P, D])).then_inc(s["gb_in"], 16)
            outs = (s["y0_out"], s["y1_out"], s["y2_out"])
            for t in range(QT + 1):
                sp.wait_ge(s["yg_done"], 2 * (t + 1))
                if t < QT:
                    sp.dma_start(out["y_prompt"][0, t * P:(t + 1) * P, :], yo[t % 3][:, :]).then_inc(outs[t % 3], 16)
                else:
                    sp.dma_start(out["y_sample"].rearrange("b t d -> (b t) d"), yo[t % 3][0:NS, :]).then_inc(outs[t % 3], 16)
            for o in outs:
                sp.wait_ge(o, 48)
            sp.wait_ge(s["copied"], 16)
            sp.wait_ge(s["lfo_out"], 16)
            sp.wait_ge(s["lfs_out"], 16)
            sp.wait_ge(s["kst"], 32 * HP)
            sp.wait_ge(s["vst"], 32 * HP)
            sp.wait_ge(s["ul_out"], 32 * NT)
            sp.wait_ge(s["pt2_out"], 32 * NT)

        @block.gpsimd
        def _(pool):
            link = Links(pool, s["pool_link"])
            link(nc.gpsimd.memset(ident[:, :], 0.0))
            link(nc.gpsimd.affine_select(out=ident[:, :], in_=ident[:, :], compare_op=ALU.not_equal, fill=1.0,
                                         base=0, pattern=[[-1, P]], channel_multiplier=1))
            nc.gpsimd.tensor_copy(identr[:, :], ident[:, :]).then_inc(s["eye"], 1)
            link(nc.gpsimd.memset(fill[:, :], 0.0))
            link(nc.gpsimd.affine_select(out=fill[:, :], in_=fill[:, :], compare_op=ALU.is_ge, fill=NEG,
                                         base=0, pattern=[[-1, P]], channel_multiplier=1))
            nc.gpsimd.tensor_copy(maskr[:, :], fill[:, :]).then_inc(s["eye"], 1)
            nc.gpsimd.memset(zeros[:, :], 0.0).then_inc(s["consts"], 1)
            nc.gpsimd.memset(ones[:, :], 1.0).then_inc(s["consts"], 1)
            def band(x, fill_, lo):
                return nc.gpsimd.affine_select(
                    out=x, in_=x, compare_op=ALU.is_ge, fill=fill_, base=0 if lo else DS - 1,
                    pattern=[[-DS if lo else DS, H]] + ([[0, DS]] if len(x.shape) == 3 else []),
                    channel_multiplier=1 if lo else -1)

            link(nc.gpsimd.memset(blockmask[:, :], 1.0))
            link(band(blockmask[:, :], 0.0, True))
            link(band(blockmask[:, :], 0.0, False))
            link(nc.gpsimd.memset(foldh[:, :, :], 0.0))
            link(nc.gpsimd.affine_select(out=foldh[:, :, :], in_=foldh[:, :, :], compare_op=ALU.not_equal, fill=1.0,
                                         base=0, pattern=[[-DS, H], [-1, DS]], channel_multiplier=1))
            link(nc.gpsimd.memset(maskh[:, :, :], NEG))
            link(band(maskh[:, :, :], 0.0, True))
            link(band(maskh[:, :, :], 0.0, False))
            nc.gpsimd.affine_select(out=maskh[:, :, :], in_=maskh[:, :, :], compare_op=ALU.is_gt, fill=0.0,
                                    base=0, pattern=[[DS, H], [1, DS]], channel_multiplier=-1).then_inc(s["sconst"], 1)
            for t in range(LEAD):
                nc.gpsimd.memset(recip[:, t:t + 1], 1.0 / (t + 1)).then_inc(s["consts"], 1)

            def parts(slot, n=8):
                apart(pool)
                link(nc.gpsimd.tensor_copy(whi[slot][:, 0:n, :], raw[slot][:, 0:n, :]))
                nc.gpsimd.tensor_tensor(wlo[slot][:, 0:n, :], raw[slot][:, 0:n, :],
                                        whi[slot][:, 0:n, :].bitcast(F32), ALU.subtract).then_inc(s["w_split"], 1)

            def one(u, n=8):
                pool.wait_ge(raw_in[u % RING], 16 * (u // RING + 1))
                if u >= RING:
                    pool.wait_ge(s["w_used"], u - RING + 1)
                parts(u % RING, n)

            def three(first, turns, extra=None, per=3):
                with pool.Fori(0, turns) as i:
                    link.enter(i, per)
                    for j in range(3):
                        u = first + j
                        pool.wait_ge(raw_in[u % RING], i * 16 + 16 * (u // RING + 1))
                        pool.wait_ge(s["w_used"], i * 3 + (u - RING + 1))
                        parts(u % RING)
                    if extra:
                        extra(i)
                link.leave(turns)

            def values(p):
                pool.wait_ge(s["tok_copied"], p * 2 + 2)
                if not isinstance(p, int):
                    pool.wait_ge(s["o_done"], p * NTILE)
                apart(pool)
                link(nc.gpsimd.tensor_copy(vhi[:, :, :], tok[:, 0:QT, :]))
                nc.gpsimd.tensor_tensor(vlo[:, :, :], tok[:, 0:QT, :], vhi[:, :, :].bitcast(F32),
                                        ALU.subtract).then_inc(s["vl_done"], 1)

            for u_ in range(4):
                one(u_)
            values(0)
            with pool.Fori(1, HP) as p:
                link.enter(p - 1, 4)
                for j in range(3):
                    u_ = U_QKV + j
                    pool.wait_ge(raw_in[u_ % RING], p * 16 + 16 * (u_ // RING + 1))
                    pool.wait_ge(s["w_used"], p * 3 + (u_ - RING + 1))
                    parts(u_ % RING)
                values(p)
            link.leave(HP - 1)
            pool.wait_ge(s["al_done"], NTILE * HP)
            pool.wait_ge(s["kst"], 32 * HP)
            pool.wait_ge(s["vst"], 32 * HP)
            nc.gpsimd.memset(qbd[:, :], 0.0).then_inc(s["qbd_zero"], 1)
            three(U_BRA, 36 // 3)
            for u_ in range(U_POOL, U_POOL + 4):
                one(u_)
            one(U_POOL + 4, NT)
            three(U_BRP, 4)
            for u_ in range(U_WO, U_FF):
                one(u_)
            three(U_FF, 2 * (FFIT - 1))
            for u_ in range(U_FFE, U_END):
                one(u_)
            pool.wait_ge(s["gb_in"], 32)
            for t in range(QT + 1):
                n = P if t < QT else NS
                pool.wait_ge(s["yn_done"], t + 1)
                y = yo[t % 3][0:n, :]
                nc.gpsimd.tensor_tensor(y, y, gb[0:n, 0, :], ALU.mult).then_inc(s["yg_done"], 1)
                pool.wait_ge(s["yg_done"], 2 * t + 1)
                nc.gpsimd.tensor_tensor(y, y, gb[0:n, 1, :], ALU.add).then_inc(s["yg_done"], 1)

        @block.scalar
        def _(act):
            link = Links(act, s["act_link"])
            act.wait_ge(s["c_in"], 32)
            nc.scalar.activation(c9s[:, :], c9[:, :], ACT.Silu).then_inc(s["c_silu"], 1)
            for g in range(1, 18, 2):
                act.wait_ge(s["x_tr"], g + 1)
                nc.scalar.copy(x_group(g), x_bank(g)).then_inc(s["x_act"], 1)
            for j in range(4):
                modrow_copy(act, j)
            act.wait_ge(s["lfp_tr"], 2)
            nc.scalar.copy(lfall[:, 0:PAST], flat(psB)[0:NS, 0:PAST]).then_inc(s["lfp_copied"], 1)
            for k in range(KD):
                act.wait_ge(s["xt_mod"], k + 1)
                nc.scalar.copy(hhi[:, k, :], xt[:, k, :]).then_inc(s["hhi_done"], 1)
            for j in range(4, ADAC):
                modrow_copy(act, j)
            act.wait_ge(s["z_done"], 1)
            link(nc.scalar.activation(e8[:, :], e8[:, :], ACT.Exp))
            nc.scalar.activation(e8[:, :], e8[:, :], ACT.Ln, bias=1.0).then_inc(s["e_done"], 1)
            act.wait_ge(s["lf_tr"], 2)
            link(nc.scalar.copy(lfo[:, :, :], mi[0][:, 0:QT * H].rearrange("p (a b) -> p a b", b=H)))
            link(nc.scalar.copy(lfs[:, :], mi[1][0:NS, 0:H]))
            act.dma_start(out["logf_prompt"][0, 0].rearrange("(n p) h -> p n h", p=P), lfo[:, :, :]).then_inc(s["lfo_out"], 16)
            act.dma_start(out["logf_sample"][0].rearrange("b t h -> (b t) h"), lfs[:, :]).then_inc(s["lfs_out"], 16)
            act.wait_ge(s["lfs_out"], 16)
            for b in range(DB):
                act.dma_start(lfall[b * H:(b + 1) * H, PAST:LK], out["logf_sample"][0, b].rearrange("t h -> h t"),
                              allow_slow_non_contiguous=True).then_inc(s["lfnew_in"], 16)
            act.wait_ge(s["scan_done"], 2)
            act.dma_start(nd_p, z8[:, 0:NP]).then_inc(s["nd_out"], 16)
            act.dma_start(nd_s, dsamp[:, :]).then_inc(s["nd_out"], 16)
            act.wait_ge(s["nd_out"], 32)
            act.wait_ge(s["lfo_out"], 16)

            def token_major(p, ps, which, dram_p, dram_s, stored):
                act.wait_ge(s["tok_tr"], p * 4 + (2 * which + 1))
                link(nc.scalar.copy(tok[:, 0:QT, :].rearrange("p (a b) c -> p a (b c)", a=2), ps[:, 0:2, :]))
                act.wait_ge(s["tok_tr"], p * 4 + (2 * which + 2))
                nc.scalar.copy(tok[0:NS, QT, :], ps[0:NS, 2, 0:P]).then_inc(s["tok_copied"], 1)
                act.wait_ge(s["tok_copied"], p * 2 + (which + 1))
                dp = out[dram_p][0, 0].rearrange("(n p) h d -> p n (h d)", p=P)
                act.dma_start(dp[:, :, bass.ds(p * P, P)], tok[:, 0:QT, :]).then_inc(s[stored], 16)
                ds_ = out[dram_s][0].rearrange("b t h d -> (b t) (h d)")
                act.dma_start(ds_[:, bass.ds(p * P, P)], tok[0:NS, QT, :]).then_inc(s[stored], 16)

            for first, last in ((0, 1), (1, HP)):
                with act.Fori(first, last) as p:
                    link.enter(p - first, 2)
                    act.wait_ge(s["mx_done"], p * NTILE) if first else None
                    for r in range(2):
                        act.dma_start(decay[:, r, :], nd_p[bass.ds(2 * p + r, 1), :].to_broadcast([P, NP])).then_inc(s["decay_in"], 16)
                    act.wait_ge(s["q_done"], p + 1)
                    if first:
                        act.wait_ge(s["s_done"], p * NTILE)
                    nc.scalar.activation(c3(qhi[:, :]), cols(psA), ACT.Copy, scale=HD ** -0.5).then_inc(s["qhi_done"], 1)
                    act.wait_ge(s["k_done"], p + 1)
                    if first:
                        act.wait_ge(s["tok_tr"], p * 4)
                    nc.scalar.copy(c3(kv[:, :]), cols(psB)).then_inc(s["kv_done"], 1)
                    if first:
                        act.wait_ge(s["vst"], p * 32)
                        act.wait_ge(s["vl_done"], p)
                    token_major(p, psB, 0, "k_prompt", "k_sample", "kst")
                    act.wait_ge(s["v_done"], p + 1)
                    act.wait_ge(s["kl_done"], p + 1)
                    nc.scalar.copy(c3(kv[:, :]), cols(psA)).then_inc(s["vf_done"], 1)
                    act.wait_ge(s["kst"], p * 32 + 32)
                    token_major(p, psA, 1, "v_prompt", "v_sample", "vst")

                    def exp(n):
                        w = (n % QT + 1) * P
                        act.wait_ge(s["mx_done"], p * NTILE + (n + 1))
                        nc.scalar.activation(prob[n % 2][:, 0:w], prob[n % 2][:, 0:w], ACT.Exp, bias=negmax[:, n % 2:n % 2 + 1],
                                             accum_out=rowsum[:, n % 2:n % 2 + 1]).then_inc(s["p_done"], 1)

                    def pt_hi(n):
                        for g, (t, blocks) in enumerate(GROUPS):
                            if t != n:
                                continue
                            w = len(blocks) * P
                            act.wait_ge(s["tr_done"], p * NG + (g + 1))
                            if g >= 3:
                                act.wait_ge(s["o_done"], p * NTILE + (GROUPS[g - 3][0] + 1))
                            elif first:
                                act.wait_ge(s["o_done"], p * NTILE)
                            nc.scalar.copy(pthi[g % 3][:, 0:len(blocks), :].rearrange("p a b -> p (a b)"),
                                           mi[g % 2][:, 0:w]).then_inc(s["pth_done"], 1)

                    def a_hi(n):
                        r, i = n // QT, n % QT
                        act.wait_ge(s["o_done"], p * NTILE + (n + 1))
                        rows = slice(HD * r, HD * r + HD)
                        nc.scalar.copy(ahi[rows, bass.ds(p, 1), i * P:(i + 1) * P], GP[n % 2][rows, 2:3, 0:P]).then_inc(s["ah_done"], 1)

                    exp(0)
                    for n in range(NTILE):
                        if n >= 1:
                            pt_hi(n - 1)
                        if n + 1 < NTILE:
                            exp(n + 1)
                        if n >= 2:
                            a_hi(n - 2)
                    pt_hi(NTILE - 1)
                    a_hi(NTILE - 2)
                    a_hi(NTILE - 1)
                link.leave(last - first)

            nc.scalar.copy(ahi[:, :, TU:T], zeros[:, :].rearrange("p (a b) -> p a b", a=NT)).then_inc(s["pad_done"], 1)
            with act.Fori(0, DB) as b:
                for g in range(0, 2 * HP, 2):
                    act.wait_ge(s["kt_tr"], b * 2 * HP + (g + 1))
                    nc.scalar.copy(kt_s[:, g // 2, 0:512], mi[0][:, :]).then_inc(s["kt_act"], 1)
                act.wait_ge(s["sm_done"], b + 1)
                nc.scalar.activation(decs[:, :], decs[:, :], ACT.Exp, bias=negmax[0:NS, 0:1],
                                     accum_out=rowsum[0:NS, 0:1]).then_inc(s["se_done"], 1)
                act.wait_ge(s["pt_tr"], b * 2 + 1)
                nc.scalar.copy(ptrs[:, 0:NPG, :].rearrange("p a b -> p (a b)"), psB[:, 0, :]).then_inc(s["pt_act"], 1)
                act.wait_ge(s["fold_done"], b + 1)
                nc.scalar.copy(ahi[:, :, bass.ds(b * DS + NP, DS)],
                               psB[:, 1, 128:128 + HP * DS].rearrange("p (a b) -> p a b", a=HP)).then_inc(s["sah_done"], 1)

            def gates(j):
                with act.Fori(0, 4) as i:
                    for x, ps in (("A", psA), ("B", psB)):
                        act.wait_ge(s[f"g{x}"], i + (4 * j + 1))
                        k = "AB".index(x)
                        nc.scalar.activation(c3(sg[k][:, :]), cols(ps), ACT.Sigmoid).then_inc(s[f"sg{x}"], 1)

            gates(0)
            act.wait_ge(s["mA"], 4)
            act.wait_ge(s["mB"], 4)
            with act.Fori(0, NT) as i:
                act.wait_ge(s["cc_done"], i + 1)
                nc.scalar.copy(c3(cc[:, :]), cols(psA)).then_inc(s["cc_copied"], 1)
                act.wait_ge(s["ul_tr"], i + 1)
                nc.scalar.copy(utok[:, :], mi[0][0:18, 0:P]).then_inc(s["ul_copied"], 1)
                act.wait_ge(s["ul_copied"], i + 1)
                act.dma_start(out["conv_prompt"][0, 0][:, bass.ds(i * P, P)], utok[0:2, :]).then_inc(s["ul_out"], 16)
                act.dma_start(out["conv_sample"][0].rearrange("b t c -> (b t) c")[:, bass.ds(i * P, P)], utok[2:18, :]).then_inc(s["ul_out"], 16)
                act.wait_ge(s["y_done"], i + 1)
                nc.scalar.copy(ahi[:, bass.ds(i, 1), :], yc[:, None, :]).then_inc(s["chi_done"], 1)
                act.wait_ge(s["ul_out"], i * 32 + 32)
            act.wait_ge(s["clo_done"], NT)
            gates(1)
            act.wait_ge(s["mA"], 8)
            act.wait_ge(s["mB"], 8)
            for g in range(NT):
                act.wait_ge(s["gemm_done"], 1 + g + 1)
                if g:
                    act.wait_ge(s["pf_done"], g)
                    act.wait_ge(s["pt2_tr"], g)
                nc.scalar.copy(c3(pb[:, LEAD:LEAD + T]), cols(GP[g % 2])).then_inc(s["pcopied"], 1)
                act.wait_ge(s["pt2_tr"], g + 1)
                if g:
                    act.wait_ge(s["pt2_out"], 32 * g)
                link(nc.scalar.copy(ptok[0:PST, 0, :], mi[0][0:PST, 0:P]))
                nc.scalar.copy(ptok[:, 1, :], mi[0][0:NS, P:2 * P]).then_inc(s["pt2_copied"], 1)
                act.wait_ge(s["pt2_copied"], g + 1)
                act.dma_start(out["pool_prompt"][0, 0][:, g * P:(g + 1) * P], ptok[0:PST, 0, :]).then_inc(s["pt2_out"], 16)
                act.dma_start(out["pool_sample"][0, :, PST - DS:PST, g * P:(g + 1) * P], ptok[:, 1, :]).then_inc(s["pt2_out"], 16)
                act.wait_ge(s["pf_done"], g + 1)
                nc.scalar.copy(ahi[:, g, :], yp[:, :]).then_inc(s["phi_done"], 1)
            for g in range(NT):
                act.wait_ge(s["gemm_done"], 5 + g + 1)
                nc.scalar.activation(c3(ahi[:, g, :]), cols(GP[g % 2]), ACT.Copy,
                                     scale=vecs[:, V_PS + g:V_PS + g + 1]).then_inc(s["mhi_done"], 1)
            act.wait_ge(s["plo_done"], NT)
            gates(2)
            act.wait_ge(s["gA"], 12)
            act.wait_ge(s["gB"], 12)
            for k in range(KD):
                act.wait_ge(s["mB" if k % 2 else "mA"], 8 + k // 2 + 1)
                nc.scalar.copy(hhi[:, k, :], merged[:, k, :]).then_inc(s["hhi_done"], 1)
            act.wait_ge(s["mB"], 12)
            act.wait_ge(s["mA"], 12)
            for k in range(KD):
                if k >= 2:
                    act.wait_ge(s["wo_ev"], k - 1)
                act.dma_start(xr[k % 2][:, :], x_keep[:, k, :]).then_inc(s[f"xr{k % 2}_in"], 16)
            for k in range(KD):
                act.wait_ge(s["d_done"], k + 1)
                if k >= 2:
                    act.wait_ge(s["var_done"], k - 1)
                nc.scalar.activation(tmp[k % 2][:, :], merged[:, k, :], ACT.Square).then_inc(s["sq_done"], 1)
            act.wait_ge(s["ve_done"], 1)
            nc.scalar.activation(rstd[:, :], rstd[:, :], ACT.Sqrt).then_inc(s["sd_done"], 1)
            for k in range(KD):
                act.wait_ge(s["xn_done"], k + 1)
                nc.scalar.activation(merged[:, k, :], merged[:, k, :], ACT.Identity, bias=vecs[:, V_L1B + k:V_L1B + k + 1],
                                     scale=vecs[:, V_L1G + k:V_L1G + k + 1]).then_inc(s["x1_done"], 1)
                if k >= 1:
                    h2_high(act, k - 1)
            h2_high(act, KD - 1)

            def silu(i, k):
                n = 2 * i + (k + 1)
                act.wait_ge(s["fg_done"], n)
                if not isinstance(i, int) or i:
                    act.wait_ge(s["ft_done"], n - 2)
                nc.scalar.activation(c3(sil[k][:, :]), cols(psA), ACT.Silu).then_inc(s["sil_done"], 1)

            def f_high(i, k):
                n = 2 * i + (k + 1)
                act.wait_ge(s["ft_done"], n)
                if not isinstance(i, int) or i:
                    act.wait_ge(s["dn_done"], KD * i)
                nc.scalar.copy(ahi[:, k, :], ft[k][:, :]).then_inc(s["fhi_done"], 1)

            silu(0, 0)
            f_high(0, 0)
            silu(0, 1)
            f_high(0, 1)
            with act.Fori(1, FFIT) as i:
                silu(i, 0)
                f_high(i, 0)
                silu(i, 1)
                f_high(i, 1)
            for t in range(QT + 1):
                n = P if t < QT else NS
                act.wait_ge(s["yv_done"], t + 1)
                nc.scalar.activation(mv[0:n, t % 2, 2:3], mv[0:n, t % 2, 2:3], ACT.Sqrt).then_inc(s["ysd_done"], 1)

        @block.vector
        def _(dve):
            link = Links(dve, s["dve_link"])
            V = nc.vector

            def per_batch(m):
                return m[:, :, 1:NCOND, None].to_broadcast([P, m.shape[1], DB, DS])

            def modulate(k, x, y, shift, scale):
                link(V.tensor_tensor(y[:, NP:TU].rearrange("p (b t) -> p b t", b=DB),
                                     x[:, NP:TU].rearrange("p (b t) -> p b t", b=DB),
                                     mod[:, scale + k, 1:NCOND, None].to_broadcast([P, DB, DS]), ALU.mult))
                link(V.tensor_tensor(y[:, NP:TU].rearrange("p (b t) -> p b t", b=DB),
                                     y[:, NP:TU].rearrange("p (b t) -> p b t", b=DB),
                                     mod[:, shift + k, 1:NCOND, None].to_broadcast([P, DB, DS]), ALU.add))
                return V.tensor_scalar(y[:, 0:NP], x[:, 0:NP], mod[:, scale + k, 0:1], mod[:, shift + k, 0:1],
                                       ALU.mult, ALU.add)

            V.memset(xt[:, :, TU:T], 0.0).then_inc(s["xt_done"], 1)
            dve.wait_ge(s["setup_tr"], 1)
            V.tensor_copy(ct[:, :, :].rearrange("p a b -> p (a b)"), mi[0][:, 0:KD * NCOND]).then_inc(s["setup_copied"], 1)
            dve.wait_ge(s["setup_tr"], 2)
            link(V.tensor_copy(vecs[:, :], mi[1][:, 0:NVEC]))
            dve.wait_ge(s["setup_tr"], 3)
            V.tensor_copy(pst[:, :, :].rearrange("p a b -> p (a b)"), psA[:, 0, 0:NT * DB * PST]).then_inc(s["setup_copied"], 1)
            dve.wait_ge(s["setup_tr"], 4)
            V.tensor_copy(cst[:, :, :].rearrange("p a b -> p (a b)"), psA[:, 1, 0:NT * DB * 2]).then_inc(s["setup_copied"], 1)
            dve.wait_ge(s["sconst"], 1)
            link(V.tensor_reduce(fold[:, :], foldh[:, :, :].rearrange("p h t -> p t h"), mybir.AxisListType.X, ALU.add))
            link(V.tensor_reduce(maskn[:, :], maskh[:, :, :].rearrange("p h t -> p t h"), mybir.AxisListType.X, ALU.add))
            for g in range(0, 18, 2):
                dve.wait_ge(s["x_tr"], g + 1)
                V.tensor_copy(x_group(g), x_bank(g)).then_inc(s["x_dve"], 1)

            def mod_chunk(j):
                dve.wait_ge(s["mod_tr"], j + 1)
                V.tensor_tensor(mod[:, 4 * j:4 * j + 4, :], mi[j % 2][:, 0:4 * NCOND].rearrange("p (a b) -> p a b", a=4),
                                vecs[:, V_ADA + 4 * j:V_ADA + 4 * j + 4, None].to_broadcast([P, 4, NCOND]),
                                ALU.add).then_inc(s["mod_done"], 1)

            for j in range(4):
                mod_chunk(j)
            dve.wait_ge(s["mod_done"], 4)
            link(V.tensor_scalar(mod[:, SC1:SC1 + KD, :], mod[:, SC1:SC1 + KD, :], 1.0, None, ALU.add))
            dve.wait_ge(s["x_stored"], 16)
            dve.wait_ge(s["x_act"], 9)
            dve.wait_ge(s["x_dve"], 9)
            dve.wait_ge(s["eye"], 2)
            dve.wait_ge(s["lfp_copied"], 1)
            for k in range(KD):
                modulate(k, xt[:, k, :], xt[:, k, :], SH1, SC1).then_inc(s["xt_mod"], 1)
                if k:
                    dve.wait_ge(s["hhi_done"], k)
                    V.tensor_tensor(hlo[:, k - 1, :], xt[:, k - 1, :], hhi[:, k - 1, :].bitcast(F32), ALU.subtract).then_inc(s["hlo_done"], 1)
            dve.wait_ge(s["hhi_done"], KD)
            V.tensor_tensor(hlo[:, KD - 1, :], xt[:, KD - 1, :], hhi[:, KD - 1, :].bitcast(F32), ALU.subtract).then_inc(s["hlo_done"], 1)
            for j in range(4, ADAC):
                mod_chunk(j)
            dve.wait_ge(s["mod_done"], ADAC)
            link(V.tensor_scalar(mod[:, SC2:SC2 + KD, :], mod[:, SC2:SC2 + KD, :], 1.0, None, ALU.add))
            dve.wait_ge(s["gemm_done"], 1)
            dve.wait_ge(s["bf_in"], 16)
            dve.wait_ge(s["hlo_done"], KD)
            link(V.tensor_scalar(c3(z8[:, :]), cols(psA, H), bfor[:, 0:1], None, ALU.add))
            V.scalar_tensor_tensor(out=e8[:, :], in0=z8[:, :], scalar=-1.0, in1=z8[:, :], op0=ALU.mult, op1=ALU.min).then_inc(s["z_done"], 1)
            link(V.tensor_scalar(nl8[:, :], z8[:, :], 0.0, None, ALU.min))
            dve.wait_ge(s["e_done"], 1)
            V.tensor_tensor(nl8[:, :], nl8[:, :], e8[:, :], ALU.subtract).then_inc(s["lf_done"], 1)
            dve.wait_ge(s["lf_done"], 1)
            dve.wait_ge(s["consts"], 2)
            V.tensor_tensor_scan(z8[:, 0:NP], ones[0:H, 0:1].to_broadcast([H, NP]), nl8[:, 0:NP], 0.0,
                                 ALU.mult, ALU.subtract).then_inc(s["scan_done"], 1)
            dve.wait_ge(s["lfnew_in"], 16 * DB)
            dve.wait_ge(s["lfp_copied"], 1)
            V.tensor_tensor_scan(dsamp[:, :], ones[0:NS, 0:1].to_broadcast([NS, LK]), lfall[:, :], 0.0,
                                 ALU.mult, ALU.subtract).then_inc(s["scan_done"], 1)

            for first, last in ((0, 1), (1, HP)):
                with dve.Fori(first, last) as p:
                    link.enter(p - first, 3 + 2 * NTILE)
                    dve.wait_ge(s["qhi_done"], p + 1)
                    if first:
                        dve.wait_ge(s["s_done"], p * NTILE)
                    link(V.scalar_tensor_tensor(out=c3(qlo[:, :]), in0=cols(psA), scalar=HD ** -0.5,
                                                in1=c3(qhi[:, :].bitcast(F32)), op0=ALU.mult, op1=ALU.subtract))
                    V.tensor_scalar(q_s[:, bass.ds(p, 1), :], psA[:, 2:3, SC:SC + NS], HD ** -0.5, None, ALU.mult).then_inc(s["ql_done"], 1)
                    dve.wait_ge(s["kv_done"], p + 1)
                    link(V.tensor_copy(khi[:, :], kv[:, :]))
                    link(V.tensor_tensor(klo[:, :], kv[:, :], khi[:, :].bitcast(F32), ALU.subtract))
                    V.tensor_copy(k_s[:, bass.ds(p, 1), :], kv[:, None, NP:TU]).then_inc(s["kl_done"], 1)
                    dve.wait_ge(s["decay_in"], p * 32 + 32)

                    def scores_max(n):
                        r, i = n // QT, n % QT
                        w = (i + 1) * P
                        dve.wait_ge(s["s_done"], p * NTILE + (n + 1))
                        if n >= 2:
                            dve.wait_ge(s["tr_done"], p * NG + (LAST_GROUP[n - 2] + 1))
                        elif first:
                            dve.wait_ge(s["tr_done"], p * NG)
                        apart(dve)
                        link(V.tensor_tensor_reduce(prob[n % 2][:, 0:w], flat(GP[n % 2])[:, 0:w], decay[:, r, 0:w],
                                                    1.0, NEG, ALU.add, ALU.max, rowmax[:, n % 2:n % 2 + 1]))
                        V.tensor_scalar(negmax[:, n % 2:n % 2 + 1], rowmax[:, n % 2:n % 2 + 1], -1.0, None,
                                        ALU.mult).then_inc(s["mx_done"], 1)

                    def normalise(n):
                        w = (n % QT + 1) * P
                        dve.wait_ge(s["p_done"], p * NTILE + (n + 1))
                        link(V.reciprocal(rowinv[:, n % 2:n % 2 + 1], rowsum[:, n % 2:n % 2 + 1]))
                        V.tensor_scalar(prob[n % 2][:, 0:w], prob[n % 2][:, 0:w], rowinv[:, n % 2:n % 2 + 1], None,
                                        ALU.mult).then_inc(s["pn_done"], 1)

                    def pt_low(n):
                        for g, (t, blocks) in enumerate(GROUPS):
                            if t == n:
                                w = len(blocks) * P
                                dve.wait_ge(s["pth_done"], p * NG + (g + 1))
                                hi = pthi[g % 3][:, 0:len(blocks), :].bitcast(F32).rearrange("p a b -> p (a b)")
                                V.tensor_tensor(ptlo[g % 3][:, 0:len(blocks), :].rearrange("p a b -> p (a b)"),
                                                mi[g % 2][:, 0:w], hi, ALU.subtract).then_inc(s["ptl_done"], 1)

                    def a_low(n):
                        r, i = n // QT, n % QT
                        rows = slice(HD * r, HD * r + HD)
                        dve.wait_ge(s["ah_done"], p * NTILE + (n + 1))
                        V.tensor_tensor(alo[rows, bass.ds(p, 1), i * P:(i + 1) * P], GP[n % 2][rows, 2:3, 0:P],
                                        ahi[rows, bass.ds(p, 1), i * P:(i + 1) * P].bitcast(F32),
                                        ALU.subtract).then_inc(s["al_done"], 1)

                    scores_max(0)
                    for n in range(NTILE):
                        if n + 1 < NTILE:
                            scores_max(n + 1)
                        normalise(n)
                        if n >= 1:
                            pt_low(n - 1)
                        if n >= 2:
                            a_low(n - 2)
                    pt_low(NTILE - 1)
                    a_low(NTILE - 2)
                    a_low(NTILE - 1)
                link.leave(last - first)

            V.tensor_copy(alo[:, :, TU:T], zeros[:, :].rearrange("p (a b) -> p a b", a=NT)).then_inc(s["pad_done"], 1)
            dve.wait_ge(s["qbd_zero"], 1)
            dve.wait_ge(s["kst"], 32 * HP)
            dve.wait_ge(s["vst"], 32 * HP)
            with dve.Fori(0, DB) as b:
                link.enter(b, 3)
                for r in range(2):
                    rows = slice(HD * r, HD * r + HD)
                    V.tensor_copy(qbd[rows, :].rearrange("p (a c) -> p a c", c=80)[:, :, r * DS:(r + 1) * DS],
                                  q_s[rows, :, bass.ds(b * DS, DS)]).then_inc(s["qbd_done"], 1)
                V.tensor_copy(kt_s[:, :, PAST:LK], k_s[:, :, bass.ds(b * DS, DS)]).then_inc(s["qbd_done"], 1)
                for g in range(1, 2 * HP, 2):
                    dve.wait_ge(s["kt_tr"], b * 2 * HP + (g + 1))
                    V.tensor_copy(kt_s[:, g // 2, 512:1024], mi[1][:, :]).then_inc(s["kt_dve"], 1)
                dve.wait_ge(s["dec_in"], b * (16 * H) + 16 * H)
                link(V.tensor_tensor(decs[:, PAST:LK], decs[:, PAST:LK], maskn[:, :], ALU.add))
                dve.wait_ge(s["ss_done"], b + 1)
                apart(dve)
                link(V.tensor_tensor_reduce(decs[:, :], flat(psA)[0:NS, 0:LK], decs[:, :], 1.0, NEG, ALU.add, ALU.max,
                                            rowmax[0:NS, 0:1]))
                V.tensor_scalar(negmax[0:NS, 0:1], rowmax[0:NS, 0:1], -1.0, None, ALU.mult).then_inc(s["sm_done"], 1)
                dve.wait_ge(s["se_done"], b + 1)
                link(V.reciprocal(rowinv[0:NS, 0:1], rowsum[0:NS, 0:1]))
                V.tensor_scalar(decs[:, :], decs[:, :], rowinv[0:NS, 0:1], None, ALU.mult).then_inc(s["sp_done"], 1)
                dve.wait_ge(s["pt_tr"], b * 2 + 2)
                V.tensor_copy(ptrs[0:DS, NPG, :], psB[0:DS, 1, 0:NS]).then_inc(s["pt_dve"], 1)
                dve.wait_ge(s["ov_done"], b + 1)
                V.tensor_tensor(om[:, :].rearrange("p (h d) -> p h d", h=H), psB[0:NS, 2, :].rearrange("p (h d) -> p h d", h=H),
                                blockmask[:, :, None].to_broadcast([NS, H, HD]), ALU.mult).then_inc(s["om_done"], 1)
                dve.wait_ge(s["sah_done"], b + 1)
                V.tensor_tensor(alo[:, :, bass.ds(b * DS + NP, DS)],
                                psB[:, 1, 128:128 + HP * DS].rearrange("p (a b) -> p a b", a=HP),
                                ahi[:, :, bass.ds(b * DS + NP, DS)].bitcast(F32), ALU.subtract).then_inc(s["sal_done"], 1)
            link.leave(DB)

            def branch(j):
                if j == 1:
                    dve.wait_ge(s["ul_out"], 32 * NT)
                if j == 2:
                    dve.wait_ge(s["pt2_out"], 32 * NT)
                with dve.Fori(0, 4) as i:
                    link.enter(i, 2 if j else 0)
                    for k, x in enumerate("AB"):
                        dve.wait_ge(s[f"b{x}"], i + (4 * j + 1))
                        to = merged[:, bass.ds(2 * i + k, 1), :].rearrange("p o (c n) -> p (o c) n", c=3)
                        g3 = c3(sg[k][:, :])
                        if j == 0:
                            V.tensor_tensor(to, cols(GP[k]), g3, ALU.mult).then_inc(s[f"m{x}"], 1)
                        else:
                            link(V.tensor_tensor(c3(part[k][:, :]), cols(GP[k]), g3, ALU.mult))
                            whole = merged[:, bass.ds(2 * i + k, 1), :]
                            V.tensor_tensor(whole, whole, part[k][:, None, :], ALU.add).then_inc(s[f"m{x}"], 1)
                link.leave(4)

            branch(0)
            dve.wait_ge(s["mA"], 4)
            dve.wait_ge(s["mB"], 4)
            link(V.memset(u[:, 0:2], 0.0))
            link(V.memset(yc[:, TU:T], 0.0))
            with dve.Fori(0, NT) as i:
                link.enter(i, 9)

                def tap(k):
                    return vecs[:, bass.ds(i + (V_CW + 4 * k), 1)]

                dve.wait_ge(s["ch_done"], i + 1)
                dve.wait_ge(s["cc_copied"], i + 1)
                V.tensor_tensor(c3(u[:, 2:2 + T]), cols(psB), c3(cc[:, :]), ALU.mult).then_inc(s["u_done"], 1)
                dve.wait_ge(s["u_done"], i + 1)
                link(V.tensor_copy(us[:, :, 2:2 + DS], u[:, 2 + NP:2 + TU].rearrange("p (b t) -> p b t", b=DB)))
                link(V.tensor_copy(us[:, :, 0:2], cst[:, bass.ds(i, 1), :].rearrange("p o (b t) -> p (o b) t", b=DB)))
                link(V.tensor_copy(ulast[:, 2:18].rearrange("p (b t) -> p b t", b=DB), us[:, :, DS:DS + 2]))
                V.tensor_copy(ulast[:, 0:2], u[:, NP:NP + 2]).then_inc(s["ul_done"], 1)
                ysmp = yc[:, NP:TU].rearrange("p (b t) -> p b t", b=DB)
                link(V.tensor_scalar(yc[:, 0:NP], u[:, 0:NP], tap(0), None, ALU.mult))
                link(V.tensor_scalar(ysmp, us[:, :, 0:DS], tap(0), None, ALU.mult))
                for k in (1, 2):
                    link(V.scalar_tensor_tensor(out=yc[:, 0:NP], in0=u[:, k:k + NP], scalar=tap(k), in1=yc[:, 0:NP],
                                                op0=ALU.mult, op1=ALU.add))
                    link(V.scalar_tensor_tensor(out=ysmp, in0=us[:, :, k:k + DS], scalar=tap(k), in1=ysmp,
                                                op0=ALU.mult, op1=ALU.add))
                dve.wait_ge(s["cb_done"], i + 1)
                V.tensor_tensor(c3(yc[:, :]), cols(psA), c3(yc[:, :]), ALU.mult).then_inc(s["y_done"], 1)
                dve.wait_ge(s["chi_done"], i + 1)
                V.tensor_tensor(alo[:, bass.ds(i, 1), :], yc[:, None, :], ahi[:, bass.ds(i, 1), :].bitcast(F32),
                                ALU.subtract).then_inc(s["clo_done"], 1)
                dve.wait_ge(s["clo_done"], i + 1)
                dve.wait_ge(s["ul_tr"], i + 1)
            link.leave(NT)
            branch(1)
            dve.wait_ge(s["mA"], 8)
            dve.wait_ge(s["mB"], 8)
            link(V.memset(ps0[:, :, 0:1], 0.0))
            link(V.memset(pb[:, 0:LEAD], 0.0))
            link(V.memset(yp[:, TU:T], 0.0))
            dve.wait_ge(s["consts"], 2 + LEAD)
            for g, win in enumerate(POOL_WIN):
                link(V.tensor_copy(ps0[:, :, 1:1 + PST], pst[:, g, :].rearrange("p (b t) -> p b t", b=DB)))
                dve.wait_ge(s["pcopied"], g + 1)
                new = pb[:, LEAD + NP:LEAD + TU].rearrange("p (b t) -> p b t", b=DB)
                link(V.tensor_copy(ps0[:, :, LEAD:], new))
                x, xs = pb, ps0
                for k, (y, ys) in enumerate(((w1, ps1), (w2, ps2), (w1, ps1), (w2, ps2))[:g + 1]):
                    d = 2 ** k
                    lo = 2 * d - 1
                    link(V.tensor_tensor(y[:, lo:LEAD + NP], x[:, lo:LEAD + NP], x[:, lo - d:LEAD + NP - d], ALU.add))
                    link(V.tensor_tensor(ys[:, :, lo:], xs[:, :, lo:], xs[:, :, lo - d:LEAD + DS - d], ALU.add))
                    x, xs = y, ys
                if g:
                    dve.wait_ge(s["phi_done"], g)
                link(V.scalar_tensor_tensor(out=yp[:, 0:NP], in0=x[:, LEAD:LEAD + NP], scalar=1.0 / win,
                                            in1=pb[:, LEAD:LEAD + NP], op0=ALU.mult, op1=ALU.subtract))
                link(V.tensor_tensor(x[:, LEAD:LEAD + win - 1], x[:, LEAD:LEAD + win - 1], recip[:, 0:win - 1], ALU.mult))
                link(V.tensor_tensor(yp[:, 0:win - 1], x[:, LEAD:LEAD + win - 1], pb[:, LEAD:LEAD + win - 1], ALU.subtract))
                V.scalar_tensor_tensor(out=yp[:, NP:TU].rearrange("p (b t) -> p b t", b=DB), in0=xs[:, :, LEAD:],
                                       scalar=1.0 / win, in1=ps0[:, :, LEAD:], op0=ALU.mult,
                                       op1=ALU.subtract).then_inc(s["pf_done"], 1)
                dve.wait_ge(s["phi_done"], g + 1)
                V.tensor_tensor(alo[:, g, :], yp[:, :], ahi[:, g, :].bitcast(F32), ALU.subtract).then_inc(s["plo_done"], 1)
                dve.wait_ge(s["plo_done"], g + 1)
            for g in range(NT):
                dve.wait_ge(s["mhi_done"], g + 1)
                V.scalar_tensor_tensor(out=c3(alo[:, g, :]), in0=cols(GP[g % 2]), scalar=vecs[:, V_PS + g:V_PS + g + 1],
                                       in1=c3(ahi[:, g, :].bitcast(F32)), op0=ALU.mult, op1=ALU.subtract).then_inc(s["mlo_done"], 1)
            branch(2)
            dve.wait_ge(s["mA"], 12)
            dve.wait_ge(s["mB"], 12)
            for k in range(KD):
                dve.wait_ge(s["hhi_done"], KD + k + 1)
                V.tensor_tensor(hlo[:, k, :], merged[:, k, :], hhi[:, k, :].bitcast(F32), ALU.subtract).then_inc(s["hlo_done"], 1)
            link(V.memset(mean1[:, :], 1.0 / D))
            dve.wait_ge(s["hlo_done"], 2 * KD)
            for k in range(KD):
                t, x = tmp[k % 2], xr[k % 2]
                dve.wait_ge(s["gemm_done"], 9 + k + 1)
                link(V.tensor_scalar(c3(t[:, :]), cols(GP[k % 2]), mod[:, G1 + k, 0:1], None, ALU.mult))
                link(V.tensor_tensor(t[:, NP:TU].rearrange("p (b t) -> p b t", b=DB),
                                     GP[k % 2][:, 2, SC:SC + NS].rearrange("p (b t) -> p b t", b=DB),
                                     mod[:, G1 + k, 1:NCOND, None].to_broadcast([P, DB, DS]), ALU.mult))
                dve.wait_ge(s[f"xr{k % 2}_in"], 16 * (k // 2 + 1))
                V.scalar_tensor_tensor(out=merged[:, k, :], in0=x[:, :], scalar=ALPHA, in1=t[:, :], op0=ALU.mult,
                                       op1=ALU.add).then_inc(s["wo_ev"], 1)
            dve.wait_ge(s["mean_done"], 1)
            for k in range(KD):
                V.tensor_tensor(c3(merged[:, k, :]), c3(merged[:, k, :]), cols(psA), ALU.subtract).then_inc(s["d_done"], 1)
            dve.wait_ge(s["var_done"], KD)
            V.tensor_scalar(c3(rstd[:, :]), cols(psB), EPS, None, ALU.add).then_inc(s["ve_done"], 1)
            dve.wait_ge(s["sd_done"], 1)
            link(V.reciprocal(rstd[:, :], rstd[:, :]))
            dve.wait_ge(s["d_done"], KD)
            for k in range(KD + 1):
                if k < KD:
                    V.tensor_tensor(merged[:, k, :], merged[:, k, :], rstd[:, :], ALU.mult).then_inc(s["xn_done"], 1)
                if k == 0:
                    continue
                j = k - 1
                t = tmp[j % 2]
                dve.wait_ge(s["x1_done"], j + 1)
                if j == 0:
                    link(V.memset(tmp[0][:, TU:T], 0.0))
                    link(V.memset(tmp[1][:, TU:T], 0.0))
                modulate(j, merged[:, j, :], t[:, :], SH2, SC2).then_inc(s["h2_done"], 1)
                dve.wait_ge(s["hhi_done"], 2 * KD + j + 1)
                V.tensor_tensor(hlo[:, j, :], t[:, :], hhi[:, j, :].bitcast(F32), ALU.subtract).then_inc(s["hlo_done"], 1)
                dve.wait_ge(s["hlo_done"], 2 * KD + j + 1)
                V.tensor_scalar(merged[:, j, :], merged[:, j, :], ALPHA, None, ALU.mult).then_inc(s["xa_done"], 1)
            dve.wait_ge(s["xa_done"], KD)

            def product(i, k):
                n = 2 * i + (k + 1)
                dve.wait_ge(s["fu_done"], n)
                dve.wait_ge(s["sil_done"], n)
                if not isinstance(i, int) or i:
                    dve.wait_ge(s["flo_done"], n - 2)
                V.tensor_tensor(c3(ft[k][:, :]), cols(psB), c3(sil[k][:, :]), ALU.mult).then_inc(s["ft_done"], 1)

            def f_low(i, k):
                dve.wait_ge(s["fhi_done"], 2 * i + (k + 1))
                V.tensor_tensor(alo[:, k, :], ft[k][:, :], ahi[:, k, :].bitcast(F32), ALU.subtract).then_inc(s["flo_done"], 1)

            def down(i):
                for t in range(KD):
                    ps = GP[t % 2]
                    dve.wait_ge(s["dn_done"], i * KD + (t + 1))
                    acc = merged[:, t, :]
                    g2 = mod[:, G2 + t, 0:1]
                    V.scalar_tensor_tensor(out=acc[:, 0:2 * CH].rearrange("p (c n) -> p c n", c=2), in0=ps[:, 0:2, 0:CH], scalar=g2,
                                           in1=acc[:, 0:2 * CH].rearrange("p (c n) -> p c n", c=2),
                                           op0=ALU.mult, op1=ALU.add).then_inc(s["dn_part"], 1)
                    V.scalar_tensor_tensor(out=acc[:, 2 * CH:NP], in0=ps[:, 2, 0:SC], scalar=g2, in1=acc[:, 2 * CH:NP],
                                           op0=ALU.mult, op1=ALU.add).then_inc(s["dn_part"], 1)
                    V.tensor_tensor(t64[:, t % 2, :].rearrange("p (b t) -> p b t", b=DB),
                                    ps[:, 2, SC:SC + NS].rearrange("p (b t) -> p b t", b=DB),
                                    mod[:, G2 + t, 1:NCOND, None].to_broadcast([P, DB, DS]), ALU.mult).then_inc(s["dn_ev"], 1)
                    dve.wait_ge(s["dn_ev"], i * KD + (t + 1))
                    V.tensor_tensor(acc[:, NP:TU], acc[:, NP:TU], t64[:, t % 2, :], ALU.add).then_inc(s["dn_part"], 1)

            product(0, 0)
            f_low(0, 0)
            product(0, 1)
            f_low(0, 1)
            with dve.Fori(1, FFIT) as i:
                product(i, 0)
                down(i - 1)
                f_low(i, 0)
                product(i, 1)
                f_low(i, 1)
                dve.wait_ge(s["dn_part"], i * (3 * KD))
            down(FFIT - 1)
            dve.wait_ge(s["dn_part"], 3 * KD * FFIT)
            def finish(t):
                n = P if t < QT else NS
                m = mv[0:n, t % 2, :]
                dve.wait_ge(s["ysd_done"], t + 1)
                link(V.reciprocal(m[:, 3:4], m[:, 2:3]))
                if t >= 3:
                    dve.wait_ge(s[f"y{t % 3}_out"], 16 * (t // 3))
                V.tensor_scalar(yo[t % 3][0:n, :], flat(GP[t % 2])[0:n, 0:D], m[:, 0:1], m[:, 3:4], ALU.subtract,
                                ALU.mult).then_inc(s["yn_done"], 1)

            for t in range(QT + 1):
                n = P if t < QT else NS
                dve.wait_ge(s["yt_done"], t + 1)
                for j in range(2):
                    link(V.bn_stats(bst[0:n, t % 2, j, :], GP[t % 2][0:n, j, :]))
                link(V.bn_aggr(mv[0:n, t % 2, 0:2], bst[0:n, t % 2, :, :].rearrange("p a b -> p (a b)")))
                V.tensor_scalar(mv[0:n, t % 2, 2:3], mv[0:n, t % 2, 1:2], EPS, None, ALU.add).then_inc(s["yv_done"], 1)
                if t:
                    finish(t - 1)
            finish(QT)

        @block.tensor
        def _(pe):
            mm, tr = nc.tensor.matmul, nc.tensor.transpose

            def gemm(u, slot, ps, blocks, hi=None, lo=None, done=None, used=None, free=()):
                hi, lo = hi or hhi, lo or hlo
                for sem_, n in free:
                    pe.wait_ge(sem_, n)
                for j, (b, k) in enumerate(blocks):
                    first, last = j == 0, j == len(blocks) - 1
                    for c in range(3):
                        mm(ps[:, c, 0:CH], whi[slot][:, b, :], hi[:, k, c * CH:(c + 1) * CH], start=first, stop=False)
                    for c in range(3):
                        mm(ps[:, c, 0:CH], whi[slot][:, b, :], lo[:, k, c * CH:(c + 1) * CH], start=False, stop=False)
                    for c in range(3):
                        m = mm(ps[:, c, 0:CH], wlo[slot][:, b, :], hi[:, k, c * CH:(c + 1) * CH], start=False, stop=last)
                m.then_inc(done, 1)
                return m

            all_k = [(k, k) for k in range(KD)]

            def unit(u):
                pe.wait_ge(s["w_split"], u + 1)

            def used():
                pe.drain().then_inc(s["w_used"], 1)

            pe.wait_ge(s["eye"], 2)
            pe.wait_ge(s["c_silu"], 1)
            for k in range(KD):
                m = tr(mi[0][:, k * NCOND:(k + 1) * NCOND], c9s[:, k * P:(k + 1) * P], ident[0:NCOND, 0:NCOND])
            m.then_inc(s["setup_tr"], 1)
            pe.wait_ge(s["vec_in"], 80)
            tr(mi[1][:, 0:NVEC], vtab[:, :], ident[0:NVEC, 0:NVEC]).then_inc(s["setup_tr"], 1)
            pe.wait_ge(s["st_in"], 32)
            for k in range(NT):
                m = tr(psA[:, 0, k * DB * PST:(k + 1) * DB * PST], stok[:, k * P:(k + 1) * P], ident[0:DB * PST, 0:DB * PST])
            m.then_inc(s["setup_tr"], 1)
            for k in range(NT):
                m = tr(psA[:, 1, k * 2 * DB:(k + 1) * 2 * DB], ctok[:, k * P:(k + 1) * P], ident[0:2 * DB, 0:2 * DB])
            m.then_inc(s["setup_tr"], 1)
            pe.wait_ge(s["x_in"], 48)
            for g in range(18):
                if g >= 3:
                    pe.wait_ge(s["x_act" if (g - 3) % 2 else "x_dve"], (g - 3) // 2 + 1)
                for j in range(4):
                    if g < 16:
                        m = tr(psB[:, g % 3, j * P:(j + 1) * P], xtok[:, 4 * (g % 2) + j, (g // 2) * P:(g // 2 + 1) * P], ident[:, :])
                    else:
                        k = 4 * (g - 16) + j
                        m = tr(psB[:, g % 3, j * NS:(j + 1) * NS], xtok[0:NS, QT, k * P:(k + 1) * P], ident[0:NS, 0:NS])
                m.then_inc(s["x_tr"], 1)
            pe.wait_ge(s["setup_copied"], 3)

            def ada_mm(j):
                pe.wait_ge(ada_in[j % 3], 16 * (j // 3 + 1))
                if j >= 2:
                    pe.wait_ge(s["modrow_done"], j - 1)
                for k in range(KD):
                    m = mm(psA[0:NCOND, j % 2, :], ct[:, k, :], ada[j % 3][:, k, :], start=k == 0, stop=k == KD - 1)
                m.then_inc(s["ada_used"], 1)

            def ada_tr(j):
                pe.wait_ge(s["modrow_done"], j + 1)
                if j >= 2:
                    pe.wait_ge(s["mod_done"], j - 1)
                for k in range(4):
                    m = tr(mi[j % 2][:, k * NCOND:(k + 1) * NCOND], modrow[:, j % 2, k * P:(k + 1) * P], ident[0:NCOND, 0:NCOND])
                m.then_inc(s["mod_tr"], 1)

            def ada_run(j0, j1):
                for j in range(j0, j1 + 1):
                    if j < j1:
                        ada_mm(j)
                    if j > j0:
                        ada_tr(j - 1)

            ada_run(0, 4)
            pe.wait_ge(s["lfp_in"], 16 * DB * NPG)
            pe.wait_ge(s["x_dve"], 9)
            pe.wait_ge(s["x_act"], 9)
            for j in range(2):
                for g in range(4 * j, 4 * j + 4):
                    m = tr(psB[0:NS, j, (g % 4) * P:(g % 4 + 1) * P], lfpast[:, g, :, :].rearrange("p b h -> p (b h)"), ident[:, :])
                m.then_inc(s["lfp_tr"], 1)
            ada_run(4, ADAC)
            pe.wait_ge(s["hlo_done"], KD)
            unit(U_F)
            gemm(U_F, 0, psA, all_k, done=s["gemm_done"], free=((s["modrow_done"], ADAC),))
            used()
            pe.wait_ge(s["mod_done"], ADAC)
            pe.wait_ge(s["lf_done"], 1)
            for g in range(QT):
                m = tr(mi[0][:, g * H:(g + 1) * H], nl8[:, g * P:(g + 1) * P], ident[0:H, 0:H])
            m.then_inc(s["lf_tr"], 1)
            tr(mi[1][0:NS, 0:H], nl8[:, NP:TU], ident[0:H, 0:H]).then_inc(s["lf_tr"], 1)
            pe.wait_ge(s["z_done"], 1)
            pe.wait_ge(s["lfp_copied"], 1)

            for first, last in ((0, 1), (1, HP)):
                with pe.Fori(first, last) as p:
                    if first:
                        pe.wait_ge(s["al_done"], p * NTILE)
                    unit(p * 3 + U_QKV)
                    gemm(0, 1, psA, all_k, done=s["q_done"])
                    used()
                    unit(p * 3 + (U_QKV + 1))
                    gemm(0, 2, psB, all_k, done=s["k_done"])
                    used()
                    unit(p * 3 + (U_QKV + 2))
                    gemm(0, 0, psA, all_k, done=s["v_done"], free=((s["ql_done"], p + 1),))
                    used()

                    def token_major(ps, which):
                        for n in range(QT):
                            m = tr(ps[:, n // 4, (n % 4) * P:(n % 4 + 1) * P], kv[:, n * P:(n + 1) * P], ident[:, :])
                        m.then_inc(s["tok_tr"], 1)
                        tr(ps[0:NS, 2, 0:P], kv[:, NP:TU], ident[:, :]).then_inc(s["tok_tr"], 1)

                    pe.wait_ge(s["kv_done"], p + 1)
                    token_major(psB, 0)
                    pe.wait_ge(s["vf_done"], p + 1)
                    token_major(psA, 1)

                    def scores(n):
                        r, i = n // QT, n % QT
                        rows = slice(HD * r, HD * r + HD)
                        q = slice(i * P, (i + 1) * P)
                        if n < 2:
                            pe.wait_ge(s["tok_copied"], p * 2 + (2 - n))
                            pe.wait_ge(s["kl_done"], p + 1)
                        else:
                            pe.wait_ge(s["mx_done"], p * NTILE + (n - 1))
                        for c in range(0, (i + 1) * P, 512):
                            k = slice(c, min(c + 512, (i + 1) * P))
                            o = GP[n % 2][:, c // 512, 0:k.stop - c]
                            diag = k.stop == (i + 1) * P
                            mm(o, qhi[rows, q], khi[rows, k], start=True, stop=False)
                            mm(o, qhi[rows, q], klo[rows, k], start=False, stop=False)
                            m = mm(o, qlo[rows, q], khi[rows, k], start=False, stop=not diag)
                        m = mm(GP[n % 2][:, i * P // 512, i * P % 512:i * P % 512 + P], identr[:, :], maskr[:, :],
                               start=False, stop=True)
                        m.then_inc(s["s_done"], 1)

                    def transposes(n):
                        pe.wait_ge(s["pn_done"], p * NTILE + (n + 1))
                        for g, (t, blocks) in enumerate(GROUPS):
                            if t != n:
                                continue
                            if g >= 2:
                                pe.wait_ge(s["ptl_done"], p * NG + (g - 1))
                            for j, kb in enumerate(blocks):
                                m = tr(mi[g % 2][:, j * P:(j + 1) * P], prob[n % 2][:, kb * P:(kb + 1) * P], ident[:, :])
                            m.then_inc(s["tr_done"], 1)

                    def values(n):
                        o = GP[n % 2][:, 2, 0:P]
                        if n >= 2:
                            pe.wait_ge(s["al_done"], p * NTILE + (n - 1))
                        if n == 0:
                            pe.wait_ge(s["vl_done"], p + 1)
                        for g, (t, blocks) in enumerate(GROUPS):
                            if t != n:
                                continue
                            pe.wait_ge(s["ptl_done"], p * NG + (g + 1))
                            for j, kb in enumerate(blocks):
                                mm(o, vhi[:, kb, :], pthi[g % 3][:, j, :], start=kb == 0, stop=False)
                                mm(o, vhi[:, kb, :], ptlo[g % 3][:, j, :], start=False, stop=False)
                                m = mm(o, vlo[:, kb, :], pthi[g % 3][:, j, :], start=False, stop=kb == n % QT)
                        m.then_inc(s["o_done"], 1)

                    scores(0)
                    scores(1)
                    for n in range(NTILE):
                        transposes(n)
                        if n >= 1:
                            values(n - 1)
                        if n + 2 < NTILE:
                            scores(n + 2)
                    values(NTILE - 1)

            pe.wait_ge(s["al_done"], NTILE * HP)
            with pe.Fori(0, DB) as b:
                pe.wait_ge(s["kpg_in"], b * (16 * NPG) + 16 * NPG)
                for g in range(2 * HP):
                    if g >= 2:
                        pe.wait_ge(s["kt_dve" if g % 2 else "kt_act"], b * HP + g // 2)
                    for j in range(4):
                        m = tr(mi[g % 2][:, j * P:(j + 1) * P], kpage[:, 4 * (g % 2) + j, (g // 2) * P:(g // 2 + 1) * P], ident[:, :])
                    m.then_inc(s["kt_tr"], 1)
                pe.wait_ge(s["qbd_done"], b * 3 + 3)
                pe.wait_ge(s["kt_act"], b * HP + HP)
                pe.wait_ge(s["kt_dve"], b * HP + HP)
                for c, w in ((0, 512), (512, 512), (1024, DS)):
                    for k in range(HP):
                        m = mm(psA[0:NS, c // 512, 0:w], qbd[:, k * NS:(k + 1) * NS], kt_s[:, k, c:c + w],
                               start=k == 0, stop=k == HP - 1)
                m.then_inc(s["ss_done"], 1)
                pe.wait_ge(s["sp_done"], b + 1)
                apart(pe)
                for g in range(NPG):
                    m = tr(psB[:, 0, g * NS:(g + 1) * NS], decs[:, g * P:(g + 1) * P], ident[0:NS, 0:NS])
                m.then_inc(s["pt_tr"], 1)
                tr(psB[0:DS, 1, 0:NS], decs[:, PAST:LK], ident[0:NS, 0:NS]).then_inc(s["pt_tr"], 1)
                pe.wait_ge(s["vpg_in"], b * (16 * NPG) + 16 * NPG)
                pe.wait_ge(s["vnew_in"], b * 16 + 16)
                pe.wait_ge(s["pt_act"], b + 1)
                pe.wait_ge(s["pt_dve"], b + 1)
                for g in range(NPG):
                    mm(psB[0:NS, 2, :], ptrs[:, g, :], vpage[:, g, :], start=g == 0, stop=False)
                mm(psB[0:NS, 2, :], ptrs[0:DS, NPG, :], vpage[0:DS, NPG, :], start=False, stop=True).then_inc(s["ov_done"], 1)
                pe.wait_ge(s["om_done"], b + 1)
                for k in range(HP):
                    m = mm(psB[:, 1, 128 + k * DS:128 + (k + 1) * DS], om[:, k * P:(k + 1) * P], fold[:, :], start=True, stop=True)
                m.then_inc(s["fold_done"], 1)

            def branch(j, u0, free_a, free_b, ready):
                with pe.Fori(0, 4) as i:
                    for k, x in enumerate("AB"):
                        unit(i * 3 + (u0 + k))
                        pe.wait_ge(*(free_a, free_b)[k])
                        gemm(0, (u0 + k) % RING, GP[k], all_k, done=s[f"g{x}"])
                        used()
                    for sem_, n in ready:
                        pe.wait_ge(sem_, n)
                    unit(i * 3 + (u0 + 2))
                    for k, x in enumerate("AB"):
                        gemm(0, (u0 + 2) % RING, GP[k], [(2 * t + k, t) for t in range(NT)], ahi, alo, done=s[f"b{x}"],
                             free=((s[f"sg{x}"], i + (4 * j + 1)),))
                    used()
                    pe.wait_ge(s["mA"], i + (4 * j + 1))
                    pe.wait_ge(s["mB"], i + (4 * j + 1))

            branch(0, U_BRA, (s["ss_done"], DB), (s["sal_done"], DB), ((s["sal_done"], DB), (s["pad_done"], 2)))
            with pe.Fori(0, NT) as i:
                unit(i * 3 + U_CONV)
                gemm(0, U_CONV % RING, psA, all_k, done=s["cc_done"])
                used()
                unit(i * 3 + (U_CONV + 1))
                gemm(0, (U_CONV + 1) % RING, psB, all_k, done=s["ch_done"])
                used()
                unit(i * 3 + (U_CONV + 2))
                gemm(0, (U_CONV + 2) % RING, psA, all_k, done=s["cb_done"], free=((s["cc_copied"], i + 1),))
                used()
                pe.wait_ge(s["ul_done"], i + 1)
                tr(mi[0][0:18, 0:P], ulast[:, :], ident[:, :]).then_inc(s["ul_tr"], 1)
                pe.wait_ge(s["y_done"], i + 1)
            branch(1, U_BRC, (s["y_done"], NT), (s["u_done"], NT), ((s["clo_done"], NT),))
            for g in range(NT):
                u0 = U_POOL + g
                unit(u0)
                if g >= 2:
                    pe.wait_ge(s["pcopied"], g - 1)
                gemm(u0, u0 % RING, GP[g % 2], all_k, done=s["gemm_done"])
                used()
                pe.wait_ge(s["pcopied"], g + 1)
                if g:
                    pe.wait_ge(s["pt2_copied"], g)
                tr(mi[0][0:PST, 0:P], pb[:, LEAD + NP - PST:LEAD + NP], ident[:, :])
                tr(mi[0][0:NS, P:2 * P], pb[:, LEAD + NP:LEAD + TU], ident[:, :]).then_inc(s["pt2_tr"], 1)
            unit(U_POOL + NT)
            for g in range(NT):
                if g >= 2:
                    pe.wait_ge(s["mlo_done"], g - 1)
                pe.wait_ge(s["plo_done"], g + 1)
                gemm(0, (U_POOL + NT) % RING, GP[g % 2], [(g, g)], ahi, alo, done=s["gemm_done"])
            used()
            branch(2, U_BRP, (s["mlo_done"], NT), (s["mlo_done"], NT), ((s["mlo_done"], NT),))
            pe.wait_ge(s["hlo_done"], 2 * KD)
            for k in range(KD):
                unit(U_WO + k)
                if k >= 2:
                    pe.wait_ge(s["wo_ev"], k - 1)
                gemm(0, (U_WO + k) % RING, GP[k % 2], all_k, done=s["gemm_done"])
                used()
            for k in range(KD):
                pe.wait_ge(s["wo_ev"], 7 if k < 7 else 8)
                for c in range(3):
                    m = mm(psA[:, c, 0:CH], mean1[:, :], merged[:, k, c * CH:(c + 1) * CH], start=k == 0, stop=k == KD - 1)
            m.then_inc(s["mean_done"], 1)
            for k in range(KD):
                pe.wait_ge(s["sq_done"], k + 1)
                for c in range(3):
                    m = mm(psB[:, c, 0:CH], mean1[:, :], tmp[k % 2][:, c * CH:(c + 1) * CH], start=k == 0, stop=k == KD - 1)
                m.then_inc(s["var_done"], 1)

            def hidden(i, k, u0, slot):
                n = 2 * i + (k + 1)
                unit(u0)
                gemm(0, slot % RING, psA, all_k, done=s["fg_done"])
                used()
                unit(u0 + 1)
                gemm(0, (slot + 1) % RING, psB, all_k, done=s["fu_done"])
                used()

            def downs(i, u0, slot):
                for h in range(2):
                    unit(u0 + h)
                    for t in range(4 * h, 4 * h + 4):
                        if t < 2:
                            pe.wait_ge(s["sil_done" if t == 0 else "ft_done"], 2 * i + 3 if not (isinstance(i, int) and i == FFIT - 1) else 2 * FFIT)
                        else:
                            pe.wait_ge(s["dn_ev"], i * KD + (t - 1))
                        if t == 0:
                            pe.wait_ge(s["flo_done"], 2 * i + 2)
                        gemm(0, (slot + h) % RING, GP[t % 2], [(k * 4 + t % 4, k) for k in range(2)], ahi, alo, done=s["dn_done"])
                    used()

            pe.wait_ge(s["hlo_done"], 3 * KD)
            hidden(0, 0, U_FF0, U_FF0)
            pe.wait_ge(s["sil_done"], 1)
            pe.wait_ge(s["ft_done"], 1)
            hidden(0, 1, U_FF0 + 2, U_FF0 + 2)
            with pe.Fori(1, FFIT) as i:
                u0 = i * 6 + (U_FF - 6)
                pe.wait_ge(s["sil_done"], 2 * i)
                pe.wait_ge(s["ft_done"], 2 * i)
                hidden(i, 0, u0, U_FF)
                downs(i - 1, u0 + 2, U_FF + 2)
                pe.wait_ge(s["dn_ev"], i * KD)
                hidden(i, 1, u0 + 4, U_FF + 4)
            downs(FFIT - 1, U_FFE, U_FFE)
            pe.wait_ge(s["dn_part"], 3 * KD * FFIT)
            for t in range(QT + 1):
                n = P if t < QT else NS
                if t >= 2:
                    pe.wait_ge(s["yn_done"], t - 1)
                for k in range(KD):
                    m = tr(GP[t % 2][0:n, k // 4, (k % 4) * P:(k % 4 + 1) * P], merged[:, k, t * P:t * P + n], ident[:, :])
                m.then_inc(s["yt_done"], 1)


_INS = ["x_prompt", "x_sample", "cache_k", "cache_v", "cache_logf", "state_conv", "state_pool", "page_table", "c_prompt",
        "c_sample", "ada_w", "ada_b", "w_in", "b_forget", "conv_w", "pool_w", "pool_scale", "w_br_attn", "w_br_conv",
        "w_br_pool", "w_o", "ln1_g", "ln1_b", "w_gate_up", "w_down", "ln2_g", "ln2_b"]
_OUTS = {
    "y_prompt": (1, NP, D), "y_sample": (DB, DS, D),
    "k_prompt": (1, 1, NP, H, HD), "v_prompt": (1, 1, NP, H, HD), "logf_prompt": (1, 1, NP, H),
    "conv_prompt": (1, 1, 2, HALF), "pool_prompt": (1, 1, PST, HALF),
    "k_sample": (1, DB, DS, H, HD), "v_sample": (1, DB, DS, H, HD), "logf_sample": (1, DB, DS, H),
    "conv_sample": (1, DB, 2, HALF), "pool_sample": (1, DB, PST, HALF),
}


def kernel(**inputs):
    import concourse.bacc as bacc
    from concourse.bass_utils import run_bass_kernel_spmd

    nc = bacc.Bacc("TRN2", target_bir_lowering=False, num_devices=1, dynamic_dma_scratch_size=8192)
    arrays, a = {}, {}
    for name in _INS:
        x = np.ascontiguousarray(inputs[name])
        arrays[f"in_{name}"] = x
        a[name] = nc.dram_tensor(f"in_{name}", x.shape, mybir.dt.from_np(x.dtype), kind="ExternalInput").ap()
    out = {n: nc.dram_tensor(f"out_{n}", sh, F32, kind="ExternalOutput").ap() for n, sh in _OUTS.items()}
    build(nc, a, out)
    r = run_bass_kernel_spmd(nc, [arrays], core_ids=[0])
    return tuple(r.results[0][f"out_{n}"] for n in _OUTS)
```

```python
from contextlib import ExitStack

import numpy as np

import concourse.bass as bass
from concourse import mybir

F32 = mybir.dt.float32
F32R = mybir.dt.float32r
I32 = mybir.dt.int32
ALU = mybir.AluOpType
ACT = mybir.ActivationFunctionType

P = 128
D = 1024
KD = D // P
NP = 1024
QT = NP // P
DB, DS = 8, 8
NS = DB * DS
T = 1092
TU = NP + NS
CH = T // 3
SC = NP - 2 * CH
H, HD = 8, 64
HP = H // 2
PAST, PAGE = 1024, 128
NPG = PAST // PAGE
LK = PAST + DS
HALF = 512
NT = HALF // P
POOL_WIN = (2, 4, 8, 16)
PST = 15
LEAD = 16
FF = 2816
FFIT = FF // (2 * P)
OFF_Q, OFF_K, OFF_V, OFF_F = 0, HALF, 2 * HALF, 3 * HALF
OFF_CB = OFF_F + H
OFF_CC, OFF_CH, OFF_P, OFF_G = (OFF_CB + i * HALF for i in (1, 2, 3, 4))
ALPHA = 2 ** 0.25
EPS = 1e-5
NEG = -1.0e30
NCOND = 1 + DB
SH1, SC1, G1, SH2, SC2, G2 = (KD * i for i in range(6))
ADAC = 6 * D // 512
V_ADA, V_L1G, V_L1B, V_CW, V_PS, NVEC = 0, 48, 56, 64, 76, 80
U_F, U_QKV, U_BRA, U_CONV, U_BRC, U_POOL, U_BRP, U_WO, U_FF0, U_FF, U_FFE, U_END = (
    0, 1, 13, 25, 37, 49, 54, 66, 74, 78, 138, 140)
RING = 3
NTILE = 2 * QT
GROUPS = [(n, list(range(j, min(j + 4, n // 2 + 1))))
          for n in range(NTILE) for j in range(0, n // 2 + 1, 4)]
NG = len(GROUPS)
LAST_GROUP = [max(g for g, (n, _) in enumerate(GROUPS) if n == t) for t in range(NTILE)]
PAIRS = [(i, j) for i in range(QT) for j in range(0, i + 1, 4)]


class Links:

    def __init__(self, eng, sem):
        self.eng, self.sem, self.n, self.off = eng, sem, 0, 0

    def __call__(self, ins):
        ins.then_inc(self.sem, 1)
        self.n += 1
        self.eng.wait_ge(self.sem, self.off + self.n)

    def enter(self, turn, per):
        self.base, self.per, self.off, self.n = self.n, per, turn * per + self.n, 0

    def leave(self, turns):
        assert self.n == self.per, f"{self.n} links in the loop's body, not {self.per}"
        self.off, self.n = 0, self.base + turns * self.per


def build(nc, a, out):
    with ExitStack() as ctx:
        def sem(name):
            return ctx.enter_context(nc.semaphore(name))

        size = (nc.sbuf_bytes_remaining - 64) // 128 * 128
        ctx.enter_context(nc.sbuf_tensor("arena", [P, size // 4], F32))
        base = (nc.sbuf_base - size + 31) // 32 * 32

        class Region:
            def __init__(self, off, size):
                self.off, self.end = off, off + size

            def __call__(self, name, shape, dt=F32):
                o = self.off
                self.off += (4 * int(np.prod(shape[1:])) + 31) // 32 * 32
                assert self.off <= self.end, (name, self.off - self.end)
                return nc.alloc_sbuf_tensor_at(name, shape, dt, offset=o)

        HSZ, MSZ = 4 * 2 * KD * T, 4 * KD * T
        r_h, r_a = base, base + HSZ
        r_m = r_a + MSZ
        r_w = r_m + MSZ
        keep = Region(r_w, base + size - r_w)

        raw = [keep(f"raw{i}", [P, 8, P]) for i in range(RING)]
        whi = [keep(f"whi{i}", [P, 8, P], F32R) for i in range(RING)]
        wlo = [keep(f"wlo{i}", [P, 8, P], F32R) for i in range(RING)]
        ident = keep("ident", [P, P])
        identr = keep("identr", [P, P], F32R)
        maskr = keep("maskr", [P, P], F32R)
        mod = keep("mod", [P, 6 * KD, NCOND])
        vecs = keep("vecs", [P, NVEC])
        q_s = keep("q_s", [P, HP, NS])
        k_s = keep("k_s", [P, HP, NS])
        pst = keep("pst", [P, NT, DB * PST])
        cst = keep("cst", [P, NT, DB * 2])
        recip = keep("recip", [P, LEAD])
        zeros = keep("zeros", [P, 16])
        ones = keep("ones", [P, 1])
        stat = keep("stat", [P, 16])
        rowmax, negmax, rowsum, rowinv = (stat[:, 2 * i:2 * i + 2] for i in range(4))
        bfor = keep("bfor", [H, 1])
        ptab = keep("ptab", [1, DB * NPG], I32)
        maskn = keep("maskn", [NS, DS])
        fold = keep("fold", [NS, DS])
        blockmask = keep("blockmask", [NS, H])
        r_s, r_end = keep.off, base + size

        hhi = Region(r_h, HSZ)("hhi", [P, KD, T], F32R)
        hlo = Region(r_h + HSZ // 2, HSZ // 2)("hlo", [P, KD, T], F32R)
        merged = Region(r_m, MSZ)("merged", [P, KD, T])
        ahi = Region(r_a, MSZ // 2)("ahi", [P, NT, T], F32R)
        alo = Region(r_a + MSZ // 2, MSZ // 2)("alo", [P, NT, T], F32R)

        R = Region(r_h, HSZ)
        xtok = R("xtok", [P, QT + 1, D])
        c9 = R("c9", [NCOND, D])
        c9s = R("c9s", [NCOND, D])
        vtab = R("vtab", [NVEC, P])
        stok = R("stok", [DB * PST, HALF])
        ctok = R("ctok", [DB * 2, HALF])
        lfpast = R("lfpast", [P, NPG, DB, H])
        fill = R("fill", [P, P])
        foldh, maskh = R("foldh", [NS, H, DS]), R("maskh", [NS, H, DS])
        R = Region(r_a, MSZ)
        ada = [R("ada0", [P, KD, 512]), R("ada1", [P, KD, 512])]
        S = Region(r_s, r_end - r_s)
        ada.append(S("ada2", [P, KD, 512]))
        modrow = S("modrow", [NCOND, 2, 512])
        ct = S("ct", [P, KD, NCOND])
        lfall = S("lfall", [NS, LK])
        xt = Region(r_m, MSZ)("xt", [P, KD, T])
        R = Region(r_m, MSZ)
        z8, nl8, e8 = R("z8", [H, T]), R("nl8", [H, T]), R("e8", [H, T])
        dsamp = R("dsamp", [NS, LK])
        lfo = R("lfo", [P, QT, H])
        lfs = R("lfs", [NS, H])
        R = Region(r_m, MSZ)
        qhi, qlo = R("qhi", [P, T], F32R), R("qlo", [P, T], F32R)
        khi, klo = R("khi", [P, T], F32R), R("klo", [P, T], F32R)
        kv = R("kv", [P, T])
        vhi, vlo = R("vhi", [P, QT, P], F32R), R("vlo", [P, QT, P], F32R)
        S = Region(r_s, r_end - r_s)
        decay = S("decay", [P, 2, NP])
        tok = R("tok", [P, QT + 1, P])
        pthi = [S(f"pthi{i}", [P, 4, 2, P], F32R) for i in range(2)]
        ptlo = [S(f"ptlo{i}", [P, 4, 2, P], F32R) for i in range(2)]
        prob = [S("prob0", [P, NP]), S("prob1", [P, NP])]
        R = Region(r_m, MSZ)
        kpage = R("kpage", [P, NPG, HALF])
        kt_s = R("kt_s", [P, HP, LK])
        S = Region(r_s, r_end - r_s)
        vpage = S("vpage", [P, NPG + 1, HALF])
        decs = S("decs", [NS, LK])
        ptrs = S("ptrs", [P, NPG + 1, NS])
        qbd = S("qbd", [P, 320])
        om = S("om", [NS, HALF])
        S = Region(r_s, r_end - r_s)
        sg = [S("sg0", [P, T]), S("sg1", [P, T])]
        part = [S("part0", [P, T]), S("part1", [P, T])]
        S = Region(r_s, r_end - r_s)
        cc = S("cc", [P, T])
        u = S("u", [P, 2 + T])
        us = S("us", [P, DB, 2 + DS])
        yc = S("yc", [P, T])
        ulast = S("ulast", [P, 18])
        utok = S("utok", [18, P])
        S = Region(r_s, r_end - r_s)
        pb = S("pb", [P, LEAD + T])
        w1, w2 = S("w1", [P, LEAD + NP]), S("w2", [P, LEAD + NP])
        ps0, ps1, ps2 = (S(f"ps{i}", [P, DB, LEAD + DS]) for i in range(3))
        yp = S("yp", [P, T])
        ptok = S("ptok", [NS, 2, P])
        S = Region(r_s, r_end - r_s)
        xr = [S("xr0", [P, T]), S("xr1", [P, T])]
        tmp = [S("tmp0", [P, T]), S("tmp1", [P, T])]
        rstd = S("rstd", [P, T])
        mean1 = S("mean1", [P, P])
        S = Region(r_s, r_end - r_s)
        sil = [S("sil0", [P, T]), S("sil1", [P, T])]
        ft = [S("ft0", [P, T]), S("ft1", [P, T])]
        t64 = S("t64", [P, 2, NS])
        R = Region(r_h, HSZ)
        gb = R("gb", [P, 2, D])
        yo = [R(f"yo{i}", [P, D]) for i in range(3)]
        bst = R("bst", [P, 2, 2, 6])
        mv = R("mv", [P, 2, 4])

        def pst_(name, shape):
            return ctx.enter_context(nc.psum_tensor(name, shape, F32))

        psA, psB = pst_("psA", [P, 3, 512]), pst_("psB", [P, 3, 512])
        mi = [pst_("ps6", [P, 512]), pst_("ps7", [P, 512])]
        GP = [psA, psB]

        def cols(ps, n=P):
            return ps[0:n, :, 0:CH]

        def c3(x):
            return x.rearrange("p (c n) -> p c n", c=3)

        def flat(ps):
            return ps[:, :, :].rearrange("p a b -> p (a b)")

        def scratch(name, shape):
            return nc.dram_tensor(name, shape, F32).ap()

        x_keep = scratch("x_keep", [P, KD, T])
        nd_p = scratch("nd_p", [H, NP])
        nd_s = scratch("nd_s", [NS, LK])

        w_in, w_gu, w_dn, w_o = a["w_in"][0], a["w_gate_up"][0], a["w_down"][0], a["w_o"][0]

        names = """c_in vec_in x_in st_in lfp_in bf_in pt_in ada0_in ada1_in ada2_in copied
            consts eye idle c_silu       lfp_tr lfp_copied
            x_tr x_dve x_act x_stored xt_done xt_mod ada_used modrow_done mod_tr mod_done hhi_done hlo_done
            raw0 raw1 raw2 w_split w_begun dve_link act_link pool_link
            gemm_done z_done setup_tr setup_copied e_done lf_done lf_tr  lfs_out lfnew_in scan_done nd_out lfo_out
            q_done k_done v_done qhi_done ql_done kv_done kl_done vf_done tok_tr tok_copied
            kst vst vl_done decay_in
            s_done mx_done p_done pn_done tr_done pth_done ptl_done o_done ah_done al_done
            kpg_in vpg_in dec_in vnew_in kt_tr kt_act kt_dve  qbd_done ss_done sm_done se_done sp_done
            pt_tr pt_act pt_dve ov_done om_done fold_done sah_done sal_done pad_done sconst qbd_zero
            cb_done cc_done ch_done cc_copied u_done y_done chi_done clo_done ul_done ul_tr ul_copied ul_out
             pcopied pf_done phi_done plo_done pt2_tr pt2_copied pt2_out  mhi_done mlo_done
               wo_ev xr0_in xr1_in mean_done d_done sq_done var_done ve_done sd_done 
            xn_done x1_done h2_done   xa_done 
            fg_done fu_done sil_done ft_done fhi_done flo_done dn_done dn_ev dn_part
            gb_in yt_done yv_done ysd_done yn_done yg_done y0_out y1_out y2_out""".split()
        s = {n: sem(n) for n in names}
        for n in ("gA", "gB", "bA", "bB", "sgA", "sgB", "mA", "mB"):
            s[n] = sem(n)
        raw_in = [s["raw0"], s["raw1"], s["raw2"]]
        ada_in = [s["ada0_in"], s["ada1_in"], s["ada2_in"]]

        def x_group(g):
            if g < 2 * KD:
                return xt[:, g // 2, 512 * (g % 2):512 * (g % 2) + 512]
            return xt[:, 4 * (g - 2 * KD):4 * (g - 2 * KD) + 4, NP:TU]

        def x_bank(g):
            ps = psB[:, g % 3, 0:512 if g < 2 * KD else 4 * NS]
            return ps if g < 2 * KD else ps.rearrange("p (a b) -> p a b", b=NS)

        att_s = psB[:, 1, P:P + HP * DS].rearrange("p (a b) -> p a b", a=HP)

        def modrow_copy(act, j):
            act.wait_ge(s["ada_used"], j + 1)
            if j >= 2:
                act.wait_ge(s["mod_tr"], j - 1)
            nc.scalar.copy(modrow[:, j % 2, :], psA[0:NCOND, j % 2, :]).then_inc(s["modrow_done"], 1)

        def h2_high(act, k):
            act.wait_ge(s["h2_done"], k + 1)
            nc.scalar.copy(hhi[:, k, :], tmp[k % 2][:, :]).then_inc(s["hhi_done"], 1)

        def apart(eng):
            eng.sem_inc(s["idle"], 1)

        def page_loads(eng, b, buf, name, loaded):
            for g in range(NPG):
                page = eng.value_load(ptab[0:1, bass.ds(b * NPG + g, 1)], min_val=0, max_val=a[name].shape[1] - 1)
                eng.dma_start(buf[:, g, :], a[name][0, bass.ds(page, 1)].rearrange("o p h d -> p (o h d)")).then_inc(loaded, 16)

        block = ctx.enter_context(nc.Block())

        @block.sync
        def _(sp):
            def wunit(u, slot, src, shape=None):
                if not isinstance(u, int) or u >= RING:
                    sp.wait_ge(s["w_split"], u - RING + 1)
                    if not isinstance(u, int):
                        apart(sp)
                dst = raw[slot][:, :, :]
                if shape:
                    dst = dst.rearrange("p (k j) n -> p k (j n)", k=shape)
                sp.dma_start(dst, src).then_inc(raw_in[slot], 16)

            def tiles(w, c, n=P):
                return w.rearrange("(k p) n -> p k n", p=P)[:, :, bass.ds(c, n)]

            sp.dma_start(c9[0:1, :], a["c_prompt"]).then_inc(s["c_in"], 16)
            sp.dma_start(c9[1:NCOND, :], a["c_sample"]).then_inc(s["c_in"], 16)
            sp.dma_start(ptab[:, :], a["page_table"].rearrange("b (o n) -> o (b n)", o=1)).then_inc(s["pt_in"], 16)
            sp.dma_start(stok[:, :], a["state_pool"].rearrange("o b t c -> (o b t) c")).then_inc(s["st_in"], 16)
            sp.dma_start(ctok[:, :], a["state_conv"].rearrange("o b t c -> (o b t) c")).then_inc(s["st_in"], 16)
            sp.dma_start(bfor[:, :], a["b_forget"].rearrange("o h -> h o")).then_inc(s["bf_in"], 16)
            xv = a["x_prompt"][0].rearrange("(n p) d -> p n d", p=P)
            for j in range(2):
                sp.dma_start(xtok[:, 4 * j:4 * j + 4, :], xv[:, 4 * j:4 * j + 4, :]).then_inc(s["x_in"], 16)
            sp.dma_start(xtok[0:NS, QT, :], a["x_sample"].rearrange("b t d -> (b t) d")).then_inc(s["x_in"], 16)
            for row, src in ((V_ADA, a["ada_b"].rearrange("o (t p) -> (o t) p", p=P)),
                             (V_L1G, a["ln1_g"].rearrange("o (t p) -> (o t) p", p=P)),
                             (V_L1B, a["ln1_b"].rearrange("o (t p) -> (o t) p", p=P)),
                             (V_CW, a["conv_w"].rearrange("o k (t p) -> (o k t) p", p=P)),
                             (V_PS, a["pool_scale"].rearrange("o (t p) -> (o t) p", p=P))):
                sp.dma_start(vtab[row:row + src.shape[0], :], src).then_inc(s["vec_in"], 16)
            adav = a["ada_w"][0].rearrange("(k p) n -> p k n", p=P)

            def ada_chunk(j):
                if j >= 3:
                    sp.wait_ge(s["ada_used"], j - 2)
                sp.dma_start(ada[j % 3][:, :, :], adav[:, :, 512 * j:512 * j + 512]).then_inc(ada_in[j % 3], 16)

            for j in range(4):
                ada_chunk(j)
            sp.dma_start(out["pool_sample"][0, :, 0:PST - DS, :], a["state_pool"][0, :, DS:PST, :]).then_inc(s["copied"], 16)
            sp.wait_ge(s["pt_in"], 16)
            with sp.Fori(0, DB) as b:
                for g in range(NPG):
                    page = sp.value_load(ptab[0:1, bass.ds(b * NPG + g, 1)], min_val=0, max_val=a["cache_logf"].shape[1] - 1)
                    sp.dma_start(lfpast[:, g, bass.ds(b, 1), :],
                                 a["cache_logf"][0, bass.ds(page, 1), :, :].rearrange("o p h -> p o h")).then_inc(s["lfp_in"], 16)
            for j in range(4, 7):
                ada_chunk(j)
            sp.wait_ge(s["xt_done"], 1)
            sp.wait_ge(s["x_dve"], 9)
            sp.wait_ge(s["x_act"], 9)
            sp.dma_start(x_keep, xt[:, :, :]).then_inc(s["x_stored"], 16)
            for j in range(7, ADAC):
                ada_chunk(j)
            wunit(0, 0, tiles(w_in, OFF_F))
            for j in range(2):
                wunit(1 + j, 1 + j, tiles(w_in, (OFF_Q, OFF_K)[j]))
            wunit(3, 0, tiles(w_in, OFF_V))
            with sp.Fori(1, HP) as p:
                for j, off in enumerate((OFF_Q, OFF_K, OFF_V)):
                    wunit(p * 3 + (U_QKV + j), (U_QKV + j) % RING, tiles(w_in, p * P + off))
            for j in range(2):
                wunit(U_BRA + j, (U_BRA + j) % RING, tiles(w_in, OFF_G + j * P))
            wunit(U_BRA + 2, (U_BRA + 2) % RING, tiles(a["w_br_attn"][0], 0, 2 * P), 4)
            sp.wait_ge(s["al_done"], NTILE * HP)
            sp.wait_ge(s["vl_done"], HP)
            sp.wait_ge(s["vst"], 32 * HP)
            sp.wait_ge(s["kst"], 32 * HP)
            sp.wait_ge(s["o_done"], QT * HP)

            def sample_loads(b):
                page_loads(sp, b, kpage, "cache_k", s["kpg_in"])
                if not isinstance(b, int):
                    sp.wait_ge(s["pt_tr"], 2 * b)
                    apart(sp)
                sp.dma_start(decs[:, :], nd_s[bass.ds(b * H, H), None, :].to_broadcast([H, DS, LK])).then_inc(s["dec_in"], 16)

            sample_loads(0)
            with sp.Fori(1, DB) as b:
                sp.wait_ge(s["kt_tr"], b * 2 * HP)
                apart(sp)
                sample_loads(b)

            def branch_loads(u0, gate, w, first=0):
                with sp.Fori(first, 4) as i:
                    for j in range(2):
                        wunit(i * 3 + (u0 + j), (u0 + j) % RING, tiles(w_in, i * 256 + (OFF_G + gate * D + j * P)))
                    wunit(i * 3 + (u0 + 2), (u0 + 2) % RING, tiles(w, i * 256, 256), 4)

            branch_loads(U_BRA, 0, a["w_br_attn"][0], 1)
            with sp.Fori(0, NT) as i:
                for j, off in enumerate((OFF_CC, OFF_CH, OFF_CB)):
                    wunit(i * 3 + (U_CONV + j), (U_CONV + j) % RING, tiles(w_in, i * P + off))
            branch_loads(U_BRC, 1, a["w_br_conv"][0])
            for j in range(4):
                wunit(U_POOL + j, (U_POOL + j) % RING, tiles(w_in, OFF_P + j * P))
            sp.wait_ge(s["w_split"], U_POOL + 4 - RING + 1)
            sp.dma_start(raw[(U_POOL + 4) % RING][:, 0:NT, :],
                         a["pool_w"][0].rearrange("g c d -> c g d")).then_inc(raw_in[(U_POOL + 4) % RING], 16)
            branch_loads(U_BRP, 2, a["w_br_pool"][0])
            for j in range(KD):
                wunit(U_WO + j, (U_WO + j) % RING, tiles(w_o, j * P))

            def ff_cols(u0, slot, i, f):
                for j in range(2):
                    wunit(u0 + j, (slot + j) % RING, tiles(w_gu, i * 256 + (j * FF + f * P)))

            def dn_rows(u0, slot, i):
                rows = w_dn.rearrange("(i k p) n -> i p k n", k=2, p=P)
                for j in range(2):
                    src = rows[bass.ds(i, 1), :, :, j * 512:j * 512 + 512].rearrange("o p k n -> p (o k) n")
                    wunit(u0 + j, (slot + j) % RING, src, 2)

            ff_cols(U_FF0, U_FF0, 0, 0)
            ff_cols(U_FF0 + 2, U_FF0 + 2, 0, 1)
            with sp.Fori(1, FFIT) as i:
                u0 = i * 6 + (U_FF - 6)
                ff_cols(u0, U_FF, i, 0)
                dn_rows(u0 + 2, U_FF + 2, i - 1)
                ff_cols(u0 + 4, U_FF + 4, i, 1)
            dn_rows(U_FFE, U_FFE, FFIT - 1)
            sp.wait_ge(s["fg_done"], 2 * FFIT)
            sp.wait_ge(s["fu_done"], 2 * FFIT)
            sp.dma_start(gb[:, 0, :], a["ln2_g"].to_broadcast([P, D])).then_inc(s["gb_in"], 16)
            sp.dma_start(gb[:, 1, :], a["ln2_b"].to_broadcast([P, D])).then_inc(s["gb_in"], 16)
            outs = (s["y0_out"], s["y1_out"], s["y2_out"])
            for t in range(QT + 1):
                sp.wait_ge(s["yg_done"], 2 * (t + 1))
                if t < QT:
                    sp.dma_start(out["y_prompt"][0, t * P:(t + 1) * P, :], yo[t % 3][:, :]).then_inc(outs[t % 3], 16)
                else:
                    sp.dma_start(out["y_sample"].rearrange("b t d -> (b t) d"), yo[t % 3][0:NS, :]).then_inc(outs[t % 3], 16)
            for o in outs:
                sp.wait_ge(o, 48)
            sp.wait_ge(s["copied"], 16)
            sp.wait_ge(s["lfo_out"], 16)
            sp.wait_ge(s["lfs_out"], 16)
            sp.wait_ge(s["kst"], 32 * HP)
            sp.wait_ge(s["vst"], 32 * HP)
            sp.wait_ge(s["ul_out"], 32 * NT)
            sp.wait_ge(s["pt2_out"], 32 * NT)

        @block.gpsimd
        def _(pool):
            link = Links(pool, s["pool_link"])
            link(nc.gpsimd.memset(ident[:, :], 0.0))
            link(nc.gpsimd.affine_select(out=ident[:, :], in_=ident[:, :], compare_op=ALU.not_equal, fill=1.0,
                                         base=0, pattern=[[-1, P]], channel_multiplier=1))
            nc.gpsimd.tensor_copy(identr[:, :], ident[:, :]).then_inc(s["eye"], 1)
            link(nc.gpsimd.memset(fill[:, :], 0.0))
            link(nc.gpsimd.affine_select(out=fill[:, :], in_=fill[:, :], compare_op=ALU.is_ge, fill=NEG,
                                         base=0, pattern=[[-1, P]], channel_multiplier=1))
            nc.gpsimd.tensor_copy(maskr[:, :], fill[:, :]).then_inc(s["eye"], 1)
            nc.gpsimd.memset(zeros[:, :], 0.0).then_inc(s["consts"], 1)
            nc.gpsimd.memset(ones[:, :], 1.0).then_inc(s["consts"], 1)
            def band(x, fill_, lo):
                return nc.gpsimd.affine_select(
                    out=x, in_=x, compare_op=ALU.is_ge, fill=fill_, base=0 if lo else DS - 1,
                    pattern=[[-DS if lo else DS, H]] + ([[0, DS]] if len(x.shape) == 3 else []),
                    channel_multiplier=1 if lo else -1)

            link(nc.gpsimd.memset(blockmask[:, :], 1.0))
            link(band(blockmask[:, :], 0.0, True))
            link(band(blockmask[:, :], 0.0, False))
            link(nc.gpsimd.memset(foldh[:, :, :], 0.0))
            link(nc.gpsimd.affine_select(out=foldh[:, :, :], in_=foldh[:, :, :], compare_op=ALU.not_equal, fill=1.0,
                                         base=0, pattern=[[-DS, H], [-1, DS]], channel_multiplier=1))
            link(nc.gpsimd.memset(maskh[:, :, :], NEG))
            link(band(maskh[:, :, :], 0.0, True))
            link(band(maskh[:, :, :], 0.0, False))
            nc.gpsimd.affine_select(out=maskh[:, :, :], in_=maskh[:, :, :], compare_op=ALU.is_gt, fill=0.0,
                                    base=0, pattern=[[DS, H], [1, DS]], channel_multiplier=-1).then_inc(s["sconst"], 1)
            for t in range(LEAD):
                nc.gpsimd.memset(recip[:, t:t + 1], 1.0 / (t + 1)).then_inc(s["consts"], 1)

            def parts(slot, n=8):
                apart(pool)
                link(nc.gpsimd.tensor_copy(whi[slot][:, 0:n, :], raw[slot][:, 0:n, :]))
                nc.gpsimd.tensor_tensor(wlo[slot][:, 0:n, :], raw[slot][:, 0:n, :],
                                        whi[slot][:, 0:n, :].bitcast(F32), ALU.subtract).then_inc(s["w_split"], 1)

            def one(u, n=8):
                pool.wait_ge(raw_in[u % RING], 16 * (u // RING + 1))
                if u >= RING:
                    pool.wait_ge(s["w_begun"], u - RING + 2)
                parts(u % RING, n)

            def three(first, turns, extra=None, per=3):
                with pool.Fori(0, turns) as i:
                    link.enter(i, per)
                    for u in range(first, first + 3):
                        pool.wait_ge(raw_in[u % RING], i * 16 + 16 * (u // RING + 1))
                        pool.wait_ge(s["w_begun"], i * 3 + (u - RING + 2))
                        parts(u % RING)
                    if extra:
                        extra(i)
                link.leave(turns)

            def values(p):
                pool.wait_ge(s["tok_copied"], p * 2 + 2)
                if not isinstance(p, int):
                    pool.wait_ge(s["o_done"], p * QT)
                apart(pool)
                link(nc.gpsimd.tensor_copy(vhi[:, :, :], tok[:, 0:QT, :]))
                nc.gpsimd.tensor_tensor(vlo[:, :, :], tok[:, 0:QT, :], vhi[:, :, :].bitcast(F32),
                                        ALU.subtract).then_inc(s["vl_done"], 1)

            for u_ in range(4):
                one(u_)
            values(0)
            with pool.Fori(1, HP) as p:
                link.enter(p - 1, 4)
                for j in range(3):
                    u_ = U_QKV + j
                    pool.wait_ge(raw_in[u_ % RING], p * 16 + 16 * (u_ // RING + 1))
                    pool.wait_ge(s["w_begun"], p * 3 + (u_ - RING + 2))
                    parts(u_ % RING)
                values(p)
            link.leave(HP - 1)
            pool.wait_ge(s["al_done"], NTILE * HP)
            pool.wait_ge(s["kst"], 32 * HP)
            pool.wait_ge(s["vst"], 32 * HP)
            nc.gpsimd.memset(qbd[:, :], 0.0).then_inc(s["qbd_zero"], 1)
            one(U_BRA)
            one(U_BRA + 1)
            pool.wait_ge(s["pt_in"], 16)
            def sample_values(b):
                page_loads(pool, b, vpage, "cache_v", s["vpg_in"])
                pool.dma_start(vpage[0:DS, NPG, :],
                               out["v_sample"][0, bass.ds(b, 1)].rearrange("o t h d -> t (o h d)")).then_inc(s["vnew_in"], 16)

            sample_values(0)
            with pool.Fori(1, DB) as b:
                pool.wait_ge(s["ov_done"], b)
                apart(pool)
                sample_values(b)
            one(U_BRA + 2)
            three(U_BRA + 3, 33 // 3)
            for u_ in range(U_POOL, U_POOL + 4):
                one(u_)
            one(U_POOL + 4, NT)
            three(U_BRP, 4)
            for u_ in range(U_WO, U_FF):
                one(u_)
            three(U_FF, 2 * (FFIT - 1))
            for u_ in range(U_FFE, U_END):
                one(u_)
            pool.wait_ge(s["gb_in"], 32)
            for t in range(QT + 1):
                n = P if t < QT else NS
                pool.wait_ge(s["yn_done"], t + 1)
                y = yo[t % 3][0:n, :]
                nc.gpsimd.tensor_tensor(y, y, gb[0:n, 0, :], ALU.mult).then_inc(s["yg_done"], 1)
                pool.wait_ge(s["yg_done"], 2 * t + 1)
                nc.gpsimd.tensor_tensor(y, y, gb[0:n, 1, :], ALU.add).then_inc(s["yg_done"], 1)

        @block.scalar
        def _(act):
            link = Links(act, s["act_link"])
            act.wait_ge(s["c_in"], 32)
            nc.scalar.activation(c9s[:, :], c9[:, :], ACT.Silu).then_inc(s["c_silu"], 1)
            for g in range(1, 18, 2):
                act.wait_ge(s["x_tr"], g + 1)
                nc.scalar.copy(x_group(g), x_bank(g)).then_inc(s["x_act"], 1)
            for j in range(4):
                modrow_copy(act, j)
            act.wait_ge(s["lfp_tr"], 2)
            nc.scalar.copy(lfall[:, 0:PAST], flat(psB)[0:NS, 0:PAST]).then_inc(s["lfp_copied"], 1)
            for k in range(KD):
                act.wait_ge(s["xt_mod"], k + 1)
                nc.scalar.copy(hhi[:, k, :], xt[:, k, :]).then_inc(s["hhi_done"], 1)
            for j in range(4, ADAC):
                modrow_copy(act, j)
            act.wait_ge(s["z_done"], 1)
            link(nc.scalar.activation(e8[:, :], e8[:, :], ACT.Exp))
            nc.scalar.activation(e8[:, :], e8[:, :], ACT.Ln, bias=1.0).then_inc(s["e_done"], 1)
            act.wait_ge(s["lf_tr"], 2)
            link(nc.scalar.copy(lfo[:, :, :], mi[0][:, 0:QT * H].rearrange("p (a b) -> p a b", b=H)))
            link(nc.scalar.copy(lfs[:, :], mi[1][0:NS, 0:H]))
            act.dma_start(out["logf_prompt"][0, 0].rearrange("(n p) h -> p n h", p=P), lfo[:, :, :]).then_inc(s["lfo_out"], 16)
            act.dma_start(out["logf_sample"][0].rearrange("b t h -> (b t) h"), lfs[:, :]).then_inc(s["lfs_out"], 16)
            act.wait_ge(s["lfs_out"], 16)
            for b in range(DB):
                act.dma_start(lfall[b * H:(b + 1) * H, PAST:LK], out["logf_sample"][0, b].rearrange("t h -> h t"),
                              allow_slow_non_contiguous=True).then_inc(s["lfnew_in"], 16)
            act.wait_ge(s["scan_done"], 2)
            act.dma_start(nd_p, z8[:, 0:NP]).then_inc(s["nd_out"], 16)
            act.dma_start(nd_s, dsamp[:, :]).then_inc(s["nd_out"], 16)
            act.wait_ge(s["nd_out"], 32)
            act.wait_ge(s["lfo_out"], 16)

            def token_major(p, ps, which, dram_p, dram_s, stored):
                act.wait_ge(s["tok_tr"], p * 4 + (2 * which + 1))
                link(nc.scalar.copy(tok[:, 0:QT, :].rearrange("p (a b) c -> p a (b c)", a=2), ps[:, 0:2, :]))
                act.wait_ge(s["tok_tr"], p * 4 + (2 * which + 2))
                nc.scalar.copy(tok[0:NS, QT, :], ps[0:NS, 2, 0:P]).then_inc(s["tok_copied"], 1)
                act.wait_ge(s["tok_copied"], p * 2 + (which + 1))
                dp = out[dram_p][0, 0].rearrange("(n p) h d -> p n (h d)", p=P)
                act.dma_start(dp[:, :, bass.ds(p * P, P)], tok[:, 0:QT, :]).then_inc(s[stored], 16)
                ds_ = out[dram_s][0].rearrange("b t h d -> (b t) (h d)")
                act.dma_start(ds_[:, bass.ds(p * P, P)], tok[0:NS, QT, :]).then_inc(s[stored], 16)

            for first, last in ((0, 1), (1, HP)):
                with act.Fori(first, last) as p:
                    link.enter(p - first, 2)
                    act.wait_ge(s["mx_done"], p * NTILE) if first else None
                    for r in range(2):
                        act.dma_start(decay[:, r, :], nd_p[bass.ds(2 * p + r, 1), :].to_broadcast([P, NP])).then_inc(s["decay_in"], 16)
                    act.wait_ge(s["q_done"], p + 1)
                    if first:
                        act.wait_ge(s["s_done"], p * NTILE)
                    nc.scalar.activation(c3(qhi[:, :]), cols(psA), ACT.Copy, scale=HD ** -0.5).then_inc(s["qhi_done"], 1)
                    act.wait_ge(s["k_done"], p + 1)
                    if first:
                        act.wait_ge(s["tok_tr"], p * 4)
                    nc.scalar.copy(c3(kv[:, :]), cols(psB)).then_inc(s["kv_done"], 1)
                    if first:
                        act.wait_ge(s["vst"], p * 32)
                        act.wait_ge(s["vl_done"], p)
                    token_major(p, psB, 0, "k_prompt", "k_sample", "kst")
                    act.wait_ge(s["v_done"], p + 1)
                    act.wait_ge(s["kl_done"], p + 1)
                    nc.scalar.copy(c3(kv[:, :]), cols(psA)).then_inc(s["vf_done"], 1)
                    act.wait_ge(s["kst"], p * 32 + 32)
                    token_major(p, psA, 1, "v_prompt", "v_sample", "vst")

                    def exp(n):
                        w = (n // 2 + 1) * P
                        act.wait_ge(s["mx_done"], p * NTILE + (n + 1))
                        nc.scalar.activation(prob[n % 2][:, 0:w], prob[n % 2][:, 0:w], ACT.Exp, bias=negmax[:, n % 2:n % 2 + 1],
                                             accum_out=rowsum[:, n % 2:n % 2 + 1]).then_inc(s["p_done"], 1)

                    def pt_hi(n):
                        for g, (t, blocks) in enumerate(GROUPS):
                            if t != n:
                                continue
                            m = PAIRS.index((n // 2, blocks[0]))
                            act.wait_ge(s["tr_done"], p * NG + (g + 1))
                            if m >= 2:
                                act.wait_ge(s["o_done"], p * QT + (PAIRS[m - 2][0] + 1))
                            elif first:
                                act.wait_ge(s["o_done"], p * QT)
                            nb = len(blocks)
                            nc.scalar.copy(pthi[m % 2][:, 0:nb, n % 2, :],
                                           mi[g % 2][:, 0:nb * P].rearrange("p (a b) -> p a b", a=nb)).then_inc(s["pth_done"], 1)

                    def a_hi(i):
                        act.wait_ge(s["o_done"], p * QT + (i + 1))
                        for r in range(2):
                            rows = slice(HD * r, HD * r + HD)
                            nc.scalar.copy(ahi[rows, bass.ds(p, 1), i * P:(i + 1) * P],
                                           GP[i % 2][rows, 2:3, r * P:(r + 1) * P]).then_inc(s["ah_done"], 1)

                    exp(0)
                    exp(1)
                    for i in range(QT):
                        for n in (2 * i, 2 * i + 1):
                            pt_hi(n)
                            if n + 2 < NTILE:
                                exp(n + 2)
                        a_hi(i)
                link.leave(last - first)

            nc.scalar.copy(ahi[:, :, TU:T], zeros[:, :].rearrange("p (a b) -> p a b", a=NT)).then_inc(s["pad_done"], 1)

            def keys_t(b, g):
                act.wait_ge(s["kt_tr"], b * 2 * HP + (g + 1))
                nc.scalar.copy(kt_s[:, g // 2, 0:512], mi[0][:, :]).then_inc(s["kt_act"], 1)

            def sample(b, more):
                if more:
                    keys_t(b + 1, 0)
                act.wait_ge(s["sm_done"], b + 1)
                nc.scalar.activation(decs[:, :], decs[:, :], ACT.Exp, bias=negmax[0:NS, 0:1],
                                     accum_out=rowsum[0:NS, 0:1]).then_inc(s["se_done"], 1)
                if more:
                    for g in range(2, 2 * HP, 2):
                        keys_t(b + 1, g)
                act.wait_ge(s["pt_tr"], b * 2 + 1)
                nc.scalar.copy(ptrs[:, 0:NPG, :].rearrange("p a b -> p (a b)"), psB[:, 0, :]).then_inc(s["pt_act"], 1)
                act.wait_ge(s["fold_done"], b + 1)
                nc.scalar.copy(ahi[:, :, bass.ds(b * DS + NP, DS)], att_s).then_inc(s["sah_done"], 1)

            for g in range(0, 2 * HP, 2):
                keys_t(0, g)
            with act.Fori(0, DB - 1) as b:
                sample(b, True)
            sample(DB - 1, False)

            def gates(j):
                with act.Fori(0, 4) as i:
                    for x, ps in (("A", psA), ("B", psB)):
                        act.wait_ge(s[f"g{x}"], i + (4 * j + 1))
                        k = "AB".index(x)
                        nc.scalar.activation(c3(sg[k][:, :]), cols(ps), ACT.Sigmoid).then_inc(s[f"sg{x}"], 1)

            gates(0)
            act.wait_ge(s["mA"], 4)
            act.wait_ge(s["mB"], 4)
            with act.Fori(0, NT) as i:
                act.wait_ge(s["cc_done"], i + 1)
                nc.scalar.copy(c3(cc[:, :]), cols(psA)).then_inc(s["cc_copied"], 1)
                act.wait_ge(s["ul_tr"], i + 1)
                nc.scalar.copy(utok[:, :], mi[0][0:18, 0:P]).then_inc(s["ul_copied"], 1)
                act.wait_ge(s["ul_copied"], i + 1)
                act.dma_start(out["conv_prompt"][0, 0][:, bass.ds(i * P, P)], utok[0:2, :]).then_inc(s["ul_out"], 16)
                act.dma_start(out["conv_sample"][0].rearrange("b t c -> (b t) c")[:, bass.ds(i * P, P)], utok[2:18, :]).then_inc(s["ul_out"], 16)
                act.wait_ge(s["y_done"], i + 1)
                nc.scalar.copy(ahi[:, bass.ds(i, 1), :], yc[:, None, :]).then_inc(s["chi_done"], 1)
                act.wait_ge(s["ul_out"], i * 32 + 32)
            act.wait_ge(s["clo_done"], NT)
            gates(1)
            act.wait_ge(s["mA"], 8)
            act.wait_ge(s["mB"], 8)
            for g in range(NT):
                act.wait_ge(s["gemm_done"], 1 + g + 1)
                if g:
                    act.wait_ge(s["pf_done"], g)
                    act.wait_ge(s["pt2_tr"], g)
                nc.scalar.copy(c3(pb[:, LEAD:LEAD + T]), cols(GP[g % 2])).then_inc(s["pcopied"], 1)
                act.wait_ge(s["pt2_tr"], g + 1)
                if g:
                    act.wait_ge(s["pt2_out"], 32 * g)
                link(nc.scalar.copy(ptok[0:PST, 0, :], mi[0][0:PST, 0:P]))
                nc.scalar.copy(ptok[:, 1, :], mi[0][0:NS, P:2 * P]).then_inc(s["pt2_copied"], 1)
                act.wait_ge(s["pt2_copied"], g + 1)
                act.dma_start(out["pool_prompt"][0, 0][:, g * P:(g + 1) * P], ptok[0:PST, 0, :]).then_inc(s["pt2_out"], 16)
                act.dma_start(out["pool_sample"][0, :, PST - DS:PST, g * P:(g + 1) * P], ptok[:, 1, :]).then_inc(s["pt2_out"], 16)
                act.wait_ge(s["pf_done"], g + 1)
                nc.scalar.copy(ahi[:, g, :], yp[:, :]).then_inc(s["phi_done"], 1)
            for g in range(NT):
                act.wait_ge(s["gemm_done"], 5 + g + 1)
                nc.scalar.activation(c3(ahi[:, g, :]), cols(GP[g % 2]), ACT.Copy,
                                     scale=vecs[:, V_PS + g:V_PS + g + 1]).then_inc(s["mhi_done"], 1)
            act.wait_ge(s["plo_done"], NT)
            gates(2)
            act.wait_ge(s["gA"], 12)
            act.wait_ge(s["gB"], 12)
            for k in range(KD):
                act.wait_ge(s["mB" if k % 2 else "mA"], 8 + k // 2 + 1)
                nc.scalar.copy(hhi[:, k, :], merged[:, k, :]).then_inc(s["hhi_done"], 1)
            act.wait_ge(s["mB"], 12)
            act.wait_ge(s["mA"], 12)
            for k in range(KD):
                if k >= 2:
                    act.wait_ge(s["wo_ev"], k - 1)
                act.dma_start(xr[k % 2][:, :], x_keep[:, k, :]).then_inc(s[f"xr{k % 2}_in"], 16)
            for k in range(KD):
                act.wait_ge(s["d_done"], k + 1)
                if k >= 2:
                    act.wait_ge(s["var_done"], k - 1)
                nc.scalar.activation(tmp[k % 2][:, :], merged[:, k, :], ACT.Square).then_inc(s["sq_done"], 1)
            act.wait_ge(s["ve_done"], 1)
            nc.scalar.activation(rstd[:, :], rstd[:, :], ACT.Sqrt).then_inc(s["sd_done"], 1)
            for k in range(KD):
                act.wait_ge(s["xn_done"], k + 1)
                nc.scalar.activation(merged[:, k, :], merged[:, k, :], ACT.Identity, bias=vecs[:, V_L1B + k:V_L1B + k + 1],
                                     scale=vecs[:, V_L1G + k:V_L1G + k + 1]).then_inc(s["x1_done"], 1)
                if k >= 1:
                    h2_high(act, k - 1)
            h2_high(act, KD - 1)

            def silu(i, k):
                n = 2 * i + (k + 1)
                act.wait_ge(s["fg_done"], n)
                if not isinstance(i, int) or i:
                    act.wait_ge(s["ft_done"], n - 2)
                nc.scalar.activation(c3(sil[k][:, :]), cols(psA), ACT.Silu).then_inc(s["sil_done"], 1)

            def f_high(i, k):
                n = 2 * i + (k + 1)
                act.wait_ge(s["ft_done"], n)
                if not isinstance(i, int) or i:
                    act.wait_ge(s["dn_done"], KD * i)
                nc.scalar.copy(ahi[:, k, :], ft[k][:, :]).then_inc(s["fhi_done"], 1)

            silu(0, 0)
            f_high(0, 0)
            silu(0, 1)
            f_high(0, 1)
            with act.Fori(1, FFIT) as i:
                silu(i, 0)
                f_high(i, 0)
                silu(i, 1)
                f_high(i, 1)
            for t in range(QT + 1):
                n = P if t < QT else NS
                act.wait_ge(s["yv_done"], t + 1)
                nc.scalar.activation(mv[0:n, t % 2, 2:3], mv[0:n, t % 2, 2:3], ACT.Sqrt).then_inc(s["ysd_done"], 1)

        @block.vector
        def _(dve):
            link = Links(dve, s["dve_link"])
            V = nc.vector

            def per_batch(m):
                return m[:, :, 1:NCOND, None].to_broadcast([P, m.shape[1], DB, DS])

            def modulate(k, x, y, shift, scale):
                link(V.tensor_tensor(y[:, NP:TU].rearrange("p (b t) -> p b t", b=DB),
                                     x[:, NP:TU].rearrange("p (b t) -> p b t", b=DB),
                                     mod[:, scale + k, 1:NCOND, None].to_broadcast([P, DB, DS]), ALU.mult))
                link(V.tensor_tensor(y[:, NP:TU].rearrange("p (b t) -> p b t", b=DB),
                                     y[:, NP:TU].rearrange("p (b t) -> p b t", b=DB),
                                     mod[:, shift + k, 1:NCOND, None].to_broadcast([P, DB, DS]), ALU.add))
                return V.tensor_scalar(y[:, 0:NP], x[:, 0:NP], mod[:, scale + k, 0:1], mod[:, shift + k, 0:1],
                                       ALU.mult, ALU.add)

            V.memset(xt[:, :, TU:T], 0.0).then_inc(s["xt_done"], 1)
            dve.wait_ge(s["setup_tr"], 1)
            V.tensor_copy(ct[:, :, :].rearrange("p a b -> p (a b)"), mi[0][:, 0:KD * NCOND]).then_inc(s["setup_copied"], 1)
            dve.wait_ge(s["setup_tr"], 2)
            link(V.tensor_copy(vecs[:, :], mi[1][:, 0:NVEC]))
            dve.wait_ge(s["setup_tr"], 3)
            V.tensor_copy(pst[:, :, :].rearrange("p a b -> p (a b)"), psA[:, 0, 0:NT * DB * PST]).then_inc(s["setup_copied"], 1)
            dve.wait_ge(s["setup_tr"], 4)
            V.tensor_copy(cst[:, :, :].rearrange("p a b -> p (a b)"), psA[:, 1, 0:NT * DB * 2]).then_inc(s["setup_copied"], 1)
            dve.wait_ge(s["sconst"], 1)
            link(V.tensor_reduce(fold[:, :], foldh[:, :, :].rearrange("p h t -> p t h"), mybir.AxisListType.X, ALU.add))
            link(V.tensor_reduce(maskn[:, :], maskh[:, :, :].rearrange("p h t -> p t h"), mybir.AxisListType.X, ALU.add))
            for g in range(0, 18, 2):
                dve.wait_ge(s["x_tr"], g + 1)
                V.tensor_copy(x_group(g), x_bank(g)).then_inc(s["x_dve"], 1)

            def mod_chunk(j):
                dve.wait_ge(s["mod_tr"], j + 1)
                V.tensor_tensor(mod[:, 4 * j:4 * j + 4, :], mi[j % 2][:, 0:4 * NCOND].rearrange("p (a b) -> p a b", a=4),
                                vecs[:, V_ADA + 4 * j:V_ADA + 4 * j + 4, None].to_broadcast([P, 4, NCOND]),
                                ALU.add).then_inc(s["mod_done"], 1)

            for j in range(4):
                mod_chunk(j)
            dve.wait_ge(s["mod_done"], 4)
            link(V.tensor_scalar(mod[:, SC1:SC1 + KD, :], mod[:, SC1:SC1 + KD, :], 1.0, None, ALU.add))
            dve.wait_ge(s["x_stored"], 16)
            dve.wait_ge(s["x_act"], 9)
            dve.wait_ge(s["x_dve"], 9)
            dve.wait_ge(s["eye"], 2)
            dve.wait_ge(s["lfp_copied"], 1)
            for k in range(KD):
                modulate(k, xt[:, k, :], xt[:, k, :], SH1, SC1).then_inc(s["xt_mod"], 1)
                if k:
                    dve.wait_ge(s["hhi_done"], k)
                    V.tensor_tensor(hlo[:, k - 1, :], xt[:, k - 1, :], hhi[:, k - 1, :].bitcast(F32), ALU.subtract).then_inc(s["hlo_done"], 1)
            dve.wait_ge(s["hhi_done"], KD)
            V.tensor_tensor(hlo[:, KD - 1, :], xt[:, KD - 1, :], hhi[:, KD - 1, :].bitcast(F32), ALU.subtract).then_inc(s["hlo_done"], 1)
            for j in range(4, ADAC):
                mod_chunk(j)
            dve.wait_ge(s["mod_done"], ADAC)
            link(V.tensor_scalar(mod[:, SC2:SC2 + KD, :], mod[:, SC2:SC2 + KD, :], 1.0, None, ALU.add))
            dve.wait_ge(s["gemm_done"], 1)
            dve.wait_ge(s["bf_in"], 16)
            dve.wait_ge(s["hlo_done"], KD)
            link(V.tensor_scalar(c3(z8[:, :]), cols(psA, H), bfor[:, 0:1], None, ALU.add))
            V.scalar_tensor_tensor(out=e8[:, :], in0=z8[:, :], scalar=-1.0, in1=z8[:, :], op0=ALU.mult, op1=ALU.min).then_inc(s["z_done"], 1)
            link(V.tensor_scalar(nl8[:, :], z8[:, :], 0.0, None, ALU.min))
            dve.wait_ge(s["e_done"], 1)
            V.tensor_tensor(nl8[:, :], nl8[:, :], e8[:, :], ALU.subtract).then_inc(s["lf_done"], 1)
            dve.wait_ge(s["lf_done"], 1)
            dve.wait_ge(s["consts"], 2)
            V.tensor_tensor_scan(z8[:, 0:NP], ones[0:H, 0:1].to_broadcast([H, NP]), nl8[:, 0:NP], 0.0,
                                 ALU.mult, ALU.subtract).then_inc(s["scan_done"], 1)
            dve.wait_ge(s["lfnew_in"], 16 * DB)
            dve.wait_ge(s["lfp_copied"], 1)
            V.tensor_tensor_scan(dsamp[:, :], ones[0:NS, 0:1].to_broadcast([NS, LK]), lfall[:, :], 0.0,
                                 ALU.mult, ALU.subtract).then_inc(s["scan_done"], 1)

            for first, last in ((0, 1), (1, HP)):
                with dve.Fori(first, last) as p:
                    link.enter(p - first, 3 + 2 * NTILE)
                    dve.wait_ge(s["qhi_done"], p + 1)
                    if first:
                        dve.wait_ge(s["s_done"], p * NTILE)
                    link(V.scalar_tensor_tensor(out=c3(qlo[:, :]), in0=cols(psA), scalar=HD ** -0.5,
                                                in1=c3(qhi[:, :].bitcast(F32)), op0=ALU.mult, op1=ALU.subtract))
                    V.tensor_scalar(q_s[:, bass.ds(p, 1), :], psA[:, 2:3, SC:SC + NS], HD ** -0.5, None, ALU.mult).then_inc(s["ql_done"], 1)
                    dve.wait_ge(s["kv_done"], p + 1)
                    link(V.tensor_copy(khi[:, :], kv[:, :]))
                    link(V.tensor_tensor(klo[:, :], kv[:, :], khi[:, :].bitcast(F32), ALU.subtract))
                    V.tensor_copy(k_s[:, bass.ds(p, 1), :], kv[:, None, NP:TU]).then_inc(s["kl_done"], 1)
                    dve.wait_ge(s["decay_in"], p * 32 + 32)

                    def scores_max(n):
                        r, i = n % 2, n // 2
                        w = (i + 1) * P
                        dve.wait_ge(s["s_done"], p * NTILE + (n + 1))
                        if n >= 2:
                            dve.wait_ge(s["tr_done"], p * NG + (LAST_GROUP[n - 2] + 1))
                        elif first:
                            dve.wait_ge(s["tr_done"], p * NG)
                        apart(dve)
                        link(V.tensor_tensor_reduce(prob[n % 2][:, 0:w], flat(GP[n % 2])[:, 0:w], decay[:, r, 0:w],
                                                    1.0, NEG, ALU.add, ALU.max, rowmax[:, n % 2:n % 2 + 1]))
                        V.tensor_scalar(negmax[:, n % 2:n % 2 + 1], rowmax[:, n % 2:n % 2 + 1], -1.0, None,
                                        ALU.mult).then_inc(s["mx_done"], 1)

                    def normalise(n):
                        w = (n // 2 + 1) * P
                        dve.wait_ge(s["p_done"], p * NTILE + (n + 1))
                        link(V.reciprocal(rowinv[:, n % 2:n % 2 + 1], rowsum[:, n % 2:n % 2 + 1]))
                        V.tensor_scalar(prob[n % 2][:, 0:w], prob[n % 2][:, 0:w], rowinv[:, n % 2:n % 2 + 1], None,
                                        ALU.mult).then_inc(s["pn_done"], 1)

                    def pt_low(n):
                        for g, (t, blocks) in enumerate(GROUPS):
                            if t == n:
                                m, nb = PAIRS.index((n // 2, blocks[0])), len(blocks)
                                dve.wait_ge(s["pth_done"], p * NG + (g + 1))
                                V.tensor_tensor(ptlo[m % 2][:, 0:nb, n % 2, :],
                                                mi[g % 2][:, 0:nb * P].rearrange("p (a b) -> p a b", a=nb),
                                                pthi[m % 2][:, 0:nb, n % 2, :].bitcast(F32), ALU.subtract).then_inc(s["ptl_done"], 1)

                    def a_low(i):
                        for r in range(2):
                            rows = slice(HD * r, HD * r + HD)
                            dve.wait_ge(s["ah_done"], p * NTILE + (2 * i + r + 1))
                            V.tensor_tensor(alo[rows, bass.ds(p, 1), i * P:(i + 1) * P], GP[i % 2][rows, 2:3, r * P:(r + 1) * P],
                                            ahi[rows, bass.ds(p, 1), i * P:(i + 1) * P].bitcast(F32),
                                            ALU.subtract).then_inc(s["al_done"], 1)

                    for n in range(2):
                        scores_max(n)
                    for n in range(2):
                        normalise(n)
                    for i in range(QT):
                        pt_low(2 * i)
                        if i + 1 < QT:
                            scores_max(2 * i + 2)
                        pt_low(2 * i + 1)
                        if i + 1 < QT:
                            normalise(2 * i + 2)
                            scores_max(2 * i + 3)
                            normalise(2 * i + 3)
                        a_low(i)
                link.leave(last - first)

            V.tensor_copy(alo[:, :, TU:T], zeros[:, :].rearrange("p (a b) -> p a b", a=NT)).then_inc(s["pad_done"], 1)
            dve.wait_ge(s["qbd_zero"], 1)
            dve.wait_ge(s["kst"], 32 * HP)
            dve.wait_ge(s["vst"], 32 * HP)

            def queries(b):
                for r in range(2):
                    rows = slice(HD * r, HD * r + HD)
                    V.tensor_copy(qbd[rows, :].rearrange("p (a c) -> p a c", c=80)[:, :, r * DS:(r + 1) * DS],
                                  q_s[rows, :, bass.ds(b * DS, DS)]).then_inc(s["qbd_done"], 1)
                V.tensor_copy(kt_s[:, :, PAST:LK], k_s[:, :, bass.ds(b * DS, DS)]).then_inc(s["qbd_done"], 1)

            def keys_t(b, g):
                dve.wait_ge(s["kt_tr"], b * 2 * HP + (g + 1))
                V.tensor_copy(kt_s[:, g // 2, 512:1024], mi[1][:, :]).then_inc(s["kt_dve"], 1)

            def sample(b, more):
                dve.wait_ge(s["dec_in"], b * 16 + 16)
                link(V.tensor_tensor(decs[:, PAST:LK], decs[:, PAST:LK], maskn[:, :], ALU.add))
                dve.wait_ge(s["ss_done"], b + 1)
                apart(dve)
                link(V.tensor_tensor_reduce(decs[:, :], flat(psA)[0:NS, 0:LK], decs[:, :], 1.0, NEG, ALU.add, ALU.max,
                                            rowmax[0:NS, 0:1]))
                V.tensor_scalar(negmax[0:NS, 0:1], rowmax[0:NS, 0:1], -1.0, None, ALU.mult).then_inc(s["sm_done"], 1)
                if more:
                    queries(b + 1)
                    keys_t(b + 1, 1)
                    keys_t(b + 1, 3)
                dve.wait_ge(s["se_done"], b + 1)
                link(V.reciprocal(rowinv[0:NS, 0:1], rowsum[0:NS, 0:1]))
                V.tensor_scalar(decs[:, :], decs[:, :], rowinv[0:NS, 0:1], None, ALU.mult).then_inc(s["sp_done"], 1)
                if more:
                    keys_t(b + 1, 5)
                    keys_t(b + 1, 7)
                dve.wait_ge(s["pt_tr"], b * 2 + 2)
                V.tensor_copy(ptrs[0:DS, NPG, :], psB[0:DS, 1, 0:NS]).then_inc(s["pt_dve"], 1)
                dve.wait_ge(s["ov_done"], b + 1)
                V.tensor_tensor(om[:, :].rearrange("p (h d) -> p h d", h=H), psB[0:NS, 2, :].rearrange("p (h d) -> p h d", h=H),
                                blockmask[:, :, None].to_broadcast([NS, H, HD]), ALU.mult).then_inc(s["om_done"], 1)
                dve.wait_ge(s["sah_done"], b + 1)
                V.tensor_tensor(alo[:, :, bass.ds(b * DS + NP, DS)], att_s,
                                ahi[:, :, bass.ds(b * DS + NP, DS)].bitcast(F32), ALU.subtract).then_inc(s["sal_done"], 1)

            queries(0)
            for g in range(1, 2 * HP, 2):
                keys_t(0, g)
            with dve.Fori(0, DB - 1) as b:
                link.enter(b, 3)
                sample(b, True)
            link.leave(DB - 1)
            sample(DB - 1, False)

            def branch(j):
                if j == 1:
                    dve.wait_ge(s["ul_out"], 32 * NT)
                if j == 2:
                    dve.wait_ge(s["pt2_out"], 32 * NT)
                with dve.Fori(0, 4) as i:
                    link.enter(i, 2 if j else 0)
                    for k, x in enumerate("AB"):
                        dve.wait_ge(s[f"b{x}"], i + (4 * j + 1))
                        to = merged[:, bass.ds(2 * i + k, 1), :].rearrange("p o (c n) -> p (o c) n", c=3)
                        g3 = c3(sg[k][:, :])
                        if j == 0:
                            V.tensor_tensor(to, cols(GP[k]), g3, ALU.mult).then_inc(s[f"m{x}"], 1)
                        else:
                            link(V.tensor_tensor(c3(part[k][:, :]), cols(GP[k]), g3, ALU.mult))
                            whole = merged[:, bass.ds(2 * i + k, 1), :]
                            V.tensor_tensor(whole, whole, part[k][:, None, :], ALU.add).then_inc(s[f"m{x}"], 1)
                link.leave(4)

            branch(0)
            dve.wait_ge(s["mA"], 4)
            dve.wait_ge(s["mB"], 4)
            link(V.memset(u[:, 0:2], 0.0))
            link(V.memset(yc[:, TU:T], 0.0))
            with dve.Fori(0, NT) as i:
                link.enter(i, 9)

                def tap(k):
                    return vecs[:, bass.ds(i + (V_CW + 4 * k), 1)]

                dve.wait_ge(s["ch_done"], i + 1)
                dve.wait_ge(s["cc_copied"], i + 1)
                V.tensor_tensor(c3(u[:, 2:2 + T]), cols(psB), c3(cc[:, :]), ALU.mult).then_inc(s["u_done"], 1)
                dve.wait_ge(s["u_done"], i + 1)
                link(V.tensor_copy(us[:, :, 2:2 + DS], u[:, 2 + NP:2 + TU].rearrange("p (b t) -> p b t", b=DB)))
                link(V.tensor_copy(us[:, :, 0:2], cst[:, bass.ds(i, 1), :].rearrange("p o (b t) -> p (o b) t", b=DB)))
                link(V.tensor_copy(ulast[:, 2:18].rearrange("p (b t) -> p b t", b=DB), us[:, :, DS:DS + 2]))
                V.tensor_copy(ulast[:, 0:2], u[:, NP:NP + 2]).then_inc(s["ul_done"], 1)
                ysmp = yc[:, NP:TU].rearrange("p (b t) -> p b t", b=DB)
                link(V.tensor_scalar(yc[:, 0:NP], u[:, 0:NP], tap(0), None, ALU.mult))
                link(V.tensor_scalar(ysmp, us[:, :, 0:DS], tap(0), None, ALU.mult))
                for k in (1, 2):
                    link(V.scalar_tensor_tensor(out=yc[:, 0:NP], in0=u[:, k:k + NP], scalar=tap(k), in1=yc[:, 0:NP],
                                                op0=ALU.mult, op1=ALU.add))
                    link(V.scalar_tensor_tensor(out=ysmp, in0=us[:, :, k:k + DS], scalar=tap(k), in1=ysmp,
                                                op0=ALU.mult, op1=ALU.add))
                dve.wait_ge(s["cb_done"], i + 1)
                V.tensor_tensor(c3(yc[:, :]), cols(psA), c3(yc[:, :]), ALU.mult).then_inc(s["y_done"], 1)
                dve.wait_ge(s["chi_done"], i + 1)
                V.tensor_tensor(alo[:, bass.ds(i, 1), :], yc[:, None, :], ahi[:, bass.ds(i, 1), :].bitcast(F32),
                                ALU.subtract).then_inc(s["clo_done"], 1)
                dve.wait_ge(s["clo_done"], i + 1)
                dve.wait_ge(s["ul_tr"], i + 1)
            link.leave(NT)
            branch(1)
            dve.wait_ge(s["mA"], 8)
            dve.wait_ge(s["mB"], 8)
            link(V.memset(ps0[:, :, 0:1], 0.0))
            link(V.memset(pb[:, 0:LEAD], 0.0))
            link(V.memset(yp[:, TU:T], 0.0))
            dve.wait_ge(s["consts"], 2 + LEAD)
            for g, win in enumerate(POOL_WIN):
                link(V.tensor_copy(ps0[:, :, 1:1 + PST], pst[:, g, :].rearrange("p (b t) -> p b t", b=DB)))
                dve.wait_ge(s["pcopied"], g + 1)
                new = pb[:, LEAD + NP:LEAD + TU].rearrange("p (b t) -> p b t", b=DB)
                link(V.tensor_copy(ps0[:, :, LEAD:], new))
                x, xs = pb, ps0
                for k, (y, ys) in enumerate(((w1, ps1), (w2, ps2), (w1, ps1), (w2, ps2))[:g + 1]):
                    d = 2 ** k
                    lo = 2 * d - 1
                    link(V.tensor_tensor(y[:, lo:LEAD + NP], x[:, lo:LEAD + NP], x[:, lo - d:LEAD + NP - d], ALU.add))
                    link(V.tensor_tensor(ys[:, :, lo:], xs[:, :, lo:], xs[:, :, lo - d:LEAD + DS - d], ALU.add))
                    x, xs = y, ys
                if g:
                    dve.wait_ge(s["phi_done"], g)
                link(V.scalar_tensor_tensor(out=yp[:, 0:NP], in0=x[:, LEAD:LEAD + NP], scalar=1.0 / win,
                                            in1=pb[:, LEAD:LEAD + NP], op0=ALU.mult, op1=ALU.subtract))
                link(V.tensor_tensor(x[:, LEAD:LEAD + win - 1], x[:, LEAD:LEAD + win - 1], recip[:, 0:win - 1], ALU.mult))
                link(V.tensor_tensor(yp[:, 0:win - 1], x[:, LEAD:LEAD + win - 1], pb[:, LEAD:LEAD + win - 1], ALU.subtract))
                V.scalar_tensor_tensor(out=yp[:, NP:TU].rearrange("p (b t) -> p b t", b=DB), in0=xs[:, :, LEAD:],
                                       scalar=1.0 / win, in1=ps0[:, :, LEAD:], op0=ALU.mult,
                                       op1=ALU.subtract).then_inc(s["pf_done"], 1)
                dve.wait_ge(s["phi_done"], g + 1)
                V.tensor_tensor(alo[:, g, :], yp[:, :], ahi[:, g, :].bitcast(F32), ALU.subtract).then_inc(s["plo_done"], 1)
                dve.wait_ge(s["plo_done"], g + 1)
            for g in range(NT):
                dve.wait_ge(s["mhi_done"], g + 1)
                V.scalar_tensor_tensor(out=c3(alo[:, g, :]), in0=cols(GP[g % 2]), scalar=vecs[:, V_PS + g:V_PS + g + 1],
                                       in1=c3(ahi[:, g, :].bitcast(F32)), op0=ALU.mult, op1=ALU.subtract).then_inc(s["mlo_done"], 1)
            branch(2)
            dve.wait_ge(s["mA"], 12)
            dve.wait_ge(s["mB"], 12)
            for k in range(KD):
                dve.wait_ge(s["hhi_done"], KD + k + 1)
                V.tensor_tensor(hlo[:, k, :], merged[:, k, :], hhi[:, k, :].bitcast(F32), ALU.subtract).then_inc(s["hlo_done"], 1)
            link(V.memset(mean1[:, :], 1.0 / D))
            dve.wait_ge(s["hlo_done"], 2 * KD)
            for k in range(KD):
                t, x = tmp[k % 2], xr[k % 2]
                dve.wait_ge(s["gemm_done"], 9 + k + 1)
                link(V.tensor_scalar(c3(t[:, :]), cols(GP[k % 2]), mod[:, G1 + k, 0:1], None, ALU.mult))
                link(V.tensor_tensor(t[:, NP:TU].rearrange("p (b t) -> p b t", b=DB),
                                     GP[k % 2][:, 2, SC:SC + NS].rearrange("p (b t) -> p b t", b=DB),
                                     mod[:, G1 + k, 1:NCOND, None].to_broadcast([P, DB, DS]), ALU.mult))
                dve.wait_ge(s[f"xr{k % 2}_in"], 16 * (k // 2 + 1))
                V.scalar_tensor_tensor(out=merged[:, k, :], in0=x[:, :], scalar=ALPHA, in1=t[:, :], op0=ALU.mult,
                                       op1=ALU.add).then_inc(s["wo_ev"], 1)
            dve.wait_ge(s["mean_done"], 1)
            for k in range(KD):
                V.tensor_tensor(c3(merged[:, k, :]), c3(merged[:, k, :]), cols(psA), ALU.subtract).then_inc(s["d_done"], 1)
            dve.wait_ge(s["var_done"], KD)
            V.tensor_scalar(c3(rstd[:, :]), cols(psB), EPS, None, ALU.add).then_inc(s["ve_done"], 1)
            dve.wait_ge(s["sd_done"], 1)
            link(V.reciprocal(rstd[:, :], rstd[:, :]))
            dve.wait_ge(s["d_done"], KD)
            for k in range(KD + 1):
                if k < KD:
                    V.tensor_tensor(merged[:, k, :], merged[:, k, :], rstd[:, :], ALU.mult).then_inc(s["xn_done"], 1)
                if k == 0:
                    continue
                j = k - 1
                t = tmp[j % 2]
                dve.wait_ge(s["x1_done"], j + 1)
                if j == 0:
                    link(V.memset(tmp[0][:, TU:T], 0.0))
                    link(V.memset(tmp[1][:, TU:T], 0.0))
                modulate(j, merged[:, j, :], t[:, :], SH2, SC2).then_inc(s["h2_done"], 1)
                dve.wait_ge(s["hhi_done"], 2 * KD + j + 1)
                V.tensor_tensor(hlo[:, j, :], t[:, :], hhi[:, j, :].bitcast(F32), ALU.subtract).then_inc(s["hlo_done"], 1)
                dve.wait_ge(s["hlo_done"], 2 * KD + j + 1)
                V.tensor_scalar(merged[:, j, :], merged[:, j, :], ALPHA, None, ALU.mult).then_inc(s["xa_done"], 1)
            dve.wait_ge(s["xa_done"], KD)

            def product(i, k):
                n = 2 * i + (k + 1)
                dve.wait_ge(s["fu_done"], n)
                dve.wait_ge(s["sil_done"], n)
                if not isinstance(i, int) or i:
                    dve.wait_ge(s["flo_done"], n - 2)
                V.tensor_tensor(c3(ft[k][:, :]), cols(psB), c3(sil[k][:, :]), ALU.mult).then_inc(s["ft_done"], 1)

            def f_low(i, k):
                dve.wait_ge(s["fhi_done"], 2 * i + (k + 1))
                V.tensor_tensor(alo[:, k, :], ft[k][:, :], ahi[:, k, :].bitcast(F32), ALU.subtract).then_inc(s["flo_done"], 1)

            def down(i):
                for t in range(KD):
                    ps = GP[t % 2]
                    dve.wait_ge(s["dn_done"], i * KD + (t + 1))
                    acc = merged[:, t, :]
                    g2 = mod[:, G2 + t, 0:1]
                    V.scalar_tensor_tensor(out=acc[:, 0:2 * CH].rearrange("p (c n) -> p c n", c=2), in0=ps[:, 0:2, 0:CH], scalar=g2,
                                           in1=acc[:, 0:2 * CH].rearrange("p (c n) -> p c n", c=2),
                                           op0=ALU.mult, op1=ALU.add).then_inc(s["dn_part"], 1)
                    V.scalar_tensor_tensor(out=acc[:, 2 * CH:NP], in0=ps[:, 2, 0:SC], scalar=g2, in1=acc[:, 2 * CH:NP],
                                           op0=ALU.mult, op1=ALU.add).then_inc(s["dn_part"], 1)
                    V.tensor_tensor(t64[:, t % 2, :].rearrange("p (b t) -> p b t", b=DB),
                                    ps[:, 2, SC:SC + NS].rearrange("p (b t) -> p b t", b=DB),
                                    mod[:, G2 + t, 1:NCOND, None].to_broadcast([P, DB, DS]), ALU.mult).then_inc(s["dn_ev"], 1)
                    dve.wait_ge(s["dn_ev"], i * KD + (t + 1))
                    V.tensor_tensor(acc[:, NP:TU], acc[:, NP:TU], t64[:, t % 2, :], ALU.add).then_inc(s["dn_part"], 1)

            product(0, 0)
            f_low(0, 0)
            product(0, 1)
            f_low(0, 1)
            with dve.Fori(1, FFIT) as i:
                product(i, 0)
                down(i - 1)
                f_low(i, 0)
                product(i, 1)
                f_low(i, 1)
                dve.wait_ge(s["dn_part"], i * (3 * KD))
            down(FFIT - 1)
            dve.wait_ge(s["dn_part"], 3 * KD * FFIT)
            def finish(t):
                n = P if t < QT else NS
                m = mv[0:n, t % 2, :]
                dve.wait_ge(s["ysd_done"], t + 1)
                link(V.reciprocal(m[:, 3:4], m[:, 2:3]))
                if t >= 3:
                    dve.wait_ge(s[f"y{t % 3}_out"], 16 * (t // 3))
                V.tensor_scalar(yo[t % 3][0:n, :], flat(GP[t % 2])[0:n, 0:D], m[:, 0:1], m[:, 3:4], ALU.subtract,
                                ALU.mult).then_inc(s["yn_done"], 1)

            for t in range(QT + 1):
                n = P if t < QT else NS
                dve.wait_ge(s["yt_done"], t + 1)
                for j in range(2):
                    link(V.bn_stats(bst[0:n, t % 2, j, :], GP[t % 2][0:n, j, :]))
                link(V.bn_aggr(mv[0:n, t % 2, 0:2], bst[0:n, t % 2, :, :].rearrange("p a b -> p (a b)")))
                V.tensor_scalar(mv[0:n, t % 2, 2:3], mv[0:n, t % 2, 1:2], EPS, None, ALU.add).then_inc(s["yv_done"], 1)
                if t:
                    finish(t - 1)
            finish(QT)

        @block.tensor
        def _(pe):
            mm, tr = nc.tensor.matmul, nc.tensor.transpose

            def gemm(slot, ps, blocks, hi=None, lo=None, done=None, begin=True, free=()):
                hi, lo = hi or hhi, lo or hlo
                for sem_, n in free:
                    pe.wait_ge(sem_, n)
                for j, (b, k) in enumerate(blocks):
                    first, last = j == 0, j == len(blocks) - 1
                    for c in range(3):
                        m = mm(ps[:, c, 0:CH], whi[slot][:, b, :], hi[:, k, c * CH:(c + 1) * CH], start=first, stop=False)
                        if begin and first and c == 0:
                            m.then_inc(s["w_begun"], 1)
                    for c in range(3):
                        mm(ps[:, c, 0:CH], whi[slot][:, b, :], lo[:, k, c * CH:(c + 1) * CH], start=False, stop=False)
                    for c in range(3):
                        m = mm(ps[:, c, 0:CH], wlo[slot][:, b, :], hi[:, k, c * CH:(c + 1) * CH], start=False, stop=last)
                m.then_inc(done, 1)
                return m

            all_k = [(k, k) for k in range(KD)]

            def unit(u):
                pe.wait_ge(s["w_split"], u + 1)

            pe.wait_ge(s["eye"], 2)
            pe.wait_ge(s["c_silu"], 1)
            for k in range(KD):
                m = tr(mi[0][:, k * NCOND:(k + 1) * NCOND], c9s[:, k * P:(k + 1) * P], ident[0:NCOND, 0:NCOND])
            m.then_inc(s["setup_tr"], 1)
            pe.wait_ge(s["vec_in"], 80)
            tr(mi[1][:, 0:NVEC], vtab[:, :], ident[0:NVEC, 0:NVEC]).then_inc(s["setup_tr"], 1)
            pe.wait_ge(s["st_in"], 32)
            for k in range(NT):
                m = tr(psA[:, 0, k * DB * PST:(k + 1) * DB * PST], stok[:, k * P:(k + 1) * P], ident[0:DB * PST, 0:DB * PST])
            m.then_inc(s["setup_tr"], 1)
            for k in range(NT):
                m = tr(psA[:, 1, k * 2 * DB:(k + 1) * 2 * DB], ctok[:, k * P:(k + 1) * P], ident[0:2 * DB, 0:2 * DB])
            m.then_inc(s["setup_tr"], 1)
            pe.wait_ge(s["x_in"], 48)
            for g in range(18):
                if g >= 3:
                    pe.wait_ge(s["x_act" if (g - 3) % 2 else "x_dve"], (g - 3) // 2 + 1)
                for j in range(4):
                    if g < 16:
                        m = tr(psB[:, g % 3, j * P:(j + 1) * P], xtok[:, 4 * (g % 2) + j, (g // 2) * P:(g // 2 + 1) * P], ident[:, :])
                    else:
                        k = 4 * (g - 16) + j
                        m = tr(psB[:, g % 3, j * NS:(j + 1) * NS], xtok[0:NS, QT, k * P:(k + 1) * P], ident[0:NS, 0:NS])
                m.then_inc(s["x_tr"], 1)
            pe.wait_ge(s["setup_copied"], 3)

            def ada_mm(j):
                pe.wait_ge(ada_in[j % 3], 16 * (j // 3 + 1))
                if j >= 2:
                    pe.wait_ge(s["modrow_done"], j - 1)
                for k in range(KD):
                    m = mm(psA[0:NCOND, j % 2, :], ct[:, k, :], ada[j % 3][:, k, :], start=k == 0, stop=k == KD - 1)
                m.then_inc(s["ada_used"], 1)

            def ada_tr(j):
                pe.wait_ge(s["modrow_done"], j + 1)
                if j >= 2:
                    pe.wait_ge(s["mod_done"], j - 1)
                for k in range(4):
                    m = tr(mi[j % 2][:, k * NCOND:(k + 1) * NCOND], modrow[:, j % 2, k * P:(k + 1) * P], ident[0:NCOND, 0:NCOND])
                m.then_inc(s["mod_tr"], 1)

            def ada_run(j0, j1):
                for j in range(j0, j1 + 1):
                    if j < j1:
                        ada_mm(j)
                    if j > j0:
                        ada_tr(j - 1)

            ada_run(0, 4)
            pe.wait_ge(s["lfp_in"], 16 * DB * NPG)
            pe.wait_ge(s["x_dve"], 9)
            pe.wait_ge(s["x_act"], 9)
            for j in range(2):
                for g in range(4 * j, 4 * j + 4):
                    m = tr(psB[0:NS, j, (g % 4) * P:(g % 4 + 1) * P], lfpast[:, g, :, :].rearrange("p b h -> p (b h)"), ident[:, :])
                m.then_inc(s["lfp_tr"], 1)
            ada_run(4, ADAC)
            pe.wait_ge(s["hlo_done"], KD)
            unit(U_F)
            gemm(0, psA, all_k, done=s["gemm_done"], free=((s["modrow_done"], ADAC),))
            pe.wait_ge(s["mod_done"], ADAC)
            pe.wait_ge(s["lf_done"], 1)
            for g in range(QT):
                m = tr(mi[0][:, g * H:(g + 1) * H], nl8[:, g * P:(g + 1) * P], ident[0:H, 0:H])
            m.then_inc(s["lf_tr"], 1)
            tr(mi[1][0:NS, 0:H], nl8[:, NP:TU], ident[0:H, 0:H]).then_inc(s["lf_tr"], 1)
            pe.wait_ge(s["z_done"], 1)
            pe.wait_ge(s["lfp_copied"], 1)

            for first, last in ((0, 1), (1, HP)):
                with pe.Fori(first, last) as p:
                    if first:
                        pe.wait_ge(s["al_done"], p * NTILE)
                    unit(p * 3 + U_QKV)
                    gemm(1, psA, all_k, done=s["q_done"])
                    unit(p * 3 + (U_QKV + 1))
                    gemm(2, psB, all_k, done=s["k_done"])
                    unit(p * 3 + (U_QKV + 2))
                    gemm(0, psA, all_k, done=s["v_done"], free=((s["ql_done"], p + 1),))

                    def token_major(ps, which):
                        for n in range(QT):
                            m = tr(ps[:, n // 4, (n % 4) * P:(n % 4 + 1) * P], kv[:, n * P:(n + 1) * P], ident[:, :])
                        m.then_inc(s["tok_tr"], 1)
                        tr(ps[0:NS, 2, 0:P], kv[:, NP:TU], ident[:, :]).then_inc(s["tok_tr"], 1)

                    pe.wait_ge(s["kv_done"], p + 1)
                    token_major(psB, 0)
                    pe.wait_ge(s["vf_done"], p + 1)
                    token_major(psA, 1)

                    def scores(n):
                        r, i = n % 2, n // 2
                        rows = slice(HD * r, HD * r + HD)
                        q = slice(i * P, (i + 1) * P)
                        if n < 2:
                            pe.wait_ge(s["tok_copied"], p * 2 + (2 - n))
                            pe.wait_ge(s["kl_done"], p + 1)
                        else:
                            pe.wait_ge(s["mx_done"], p * NTILE + (n - 1))
                        for c in range(0, (i + 1) * P, 512):
                            k = slice(c, min(c + 512, (i + 1) * P))
                            o = GP[n % 2][:, c // 512, 0:k.stop - c]
                            diag = k.stop == (i + 1) * P
                            mm(o, qhi[rows, q], khi[rows, k], start=True, stop=False)
                            mm(o, qhi[rows, q], klo[rows, k], start=False, stop=False)
                            m = mm(o, qlo[rows, q], khi[rows, k], start=False, stop=not diag)
                        m = mm(GP[n % 2][:, i * P // 512, i * P % 512:i * P % 512 + P], identr[:, :], maskr[:, :],
                               start=False, stop=True)
                        m.then_inc(s["s_done"], 1)

                    def transposes(n):
                        pe.wait_ge(s["pn_done"], p * NTILE + (n + 1))
                        for g, (t, blocks) in enumerate(GROUPS):
                            if t != n:
                                continue
                            if g >= 2:
                                pe.wait_ge(s["ptl_done"], p * NG + (g - 1))
                            for j, kb in enumerate(blocks):
                                m = tr(mi[g % 2][:, j * P:(j + 1) * P], prob[n % 2][:, kb * P:(kb + 1) * P], ident[:, :])
                            m.then_inc(s["tr_done"], 1)

                    def values(i):
                        o = GP[i % 2][:, 2, 0:2 * P]
                        if i >= 2:
                            pe.wait_ge(s["al_done"], p * NTILE + 2 * (i - 1))
                        if i == 0:
                            pe.wait_ge(s["vl_done"], p + 1)
                        for m, (t, j0) in enumerate(PAIRS):
                            if t != i:
                                continue
                            blocks = range(j0, min(j0 + 4, i + 1))
                            pe.wait_ge(s["ptl_done"], p * NG + (GROUPS.index((2 * i + 1, list(blocks))) + 1))
                            for j, kb in enumerate(blocks):
                                ph, pl = (x[m % 2][:, j, :, :].rearrange("p r q -> p (r q)") for x in (pthi, ptlo))
                                mm(o, vhi[:, kb, :], ph, start=kb == 0, stop=False)
                                mm(o, vhi[:, kb, :], pl, start=False, stop=False)
                                mo = mm(o, vlo[:, kb, :], ph, start=False, stop=kb == i)
                        mo.then_inc(s["o_done"], 1)

                    scores(0)
                    scores(1)
                    for i in range(QT):
                        for n in (2 * i, 2 * i + 1):
                            transposes(n)
                            if n + 2 < NTILE:
                                scores(n + 2)
                        values(i)

            pe.wait_ge(s["al_done"], NTILE * HP)

            def keys_t(b):
                pe.wait_ge(s["kpg_in"], b * (16 * NPG) + 16 * NPG)
                for g in range(2 * HP):
                    if g >= 2:
                        pe.wait_ge(s["kt_dve" if g % 2 else "kt_act"], b * HP + g // 2)
                    for j in range(4):
                        m = tr(mi[g % 2][:, j * P:(j + 1) * P], kpage[:, 4 * (g % 2) + j, (g // 2) * P:(g // 2 + 1) * P], ident[:, :])
                    m.then_inc(s["kt_tr"], 1)

            def sample(b, more):
                pe.wait_ge(s["qbd_done"], b * 3 + 3)
                pe.wait_ge(s["kt_act"], b * HP + HP)
                pe.wait_ge(s["kt_dve"], b * HP + HP)
                for c, w in ((0, 512), (512, 512), (1024, DS)):
                    for k in range(HP):
                        m = mm(psA[0:NS, c // 512, 0:w], qbd[:, k * NS:(k + 1) * NS], kt_s[:, k, c:c + w],
                               start=k == 0, stop=k == HP - 1)
                m.then_inc(s["ss_done"], 1)
                if more:
                    keys_t(b + 1)
                pe.wait_ge(s["sp_done"], b + 1)
                apart(pe)
                for g in range(NPG):
                    m = tr(psB[:, 0, g * NS:(g + 1) * NS], decs[:, g * P:(g + 1) * P], ident[0:NS, 0:NS])
                m.then_inc(s["pt_tr"], 1)
                tr(psB[0:DS, 1, 0:NS], decs[:, PAST:LK], ident[0:NS, 0:NS]).then_inc(s["pt_tr"], 1)
                pe.wait_ge(s["vpg_in"], b * (16 * NPG) + 16 * NPG)
                pe.wait_ge(s["vnew_in"], b * 16 + 16)
                pe.wait_ge(s["pt_act"], b + 1)
                pe.wait_ge(s["pt_dve"], b + 1)
                for g in range(NPG):
                    mm(psB[0:NS, 2, :], ptrs[:, g, :], vpage[:, g, :], start=g == 0, stop=False)
                mm(psB[0:NS, 2, :], ptrs[0:DS, NPG, :], vpage[0:DS, NPG, :], start=False, stop=True).then_inc(s["ov_done"], 1)
                pe.wait_ge(s["om_done"], b + 1)
                for k in range(HP):
                    m = mm(att_s[:, k, :], om[:, k * P:(k + 1) * P], fold[:, :], start=True, stop=True)
                m.then_inc(s["fold_done"], 1)

            keys_t(0)
            with pe.Fori(0, DB - 1) as b:
                sample(b, True)
            sample(DB - 1, False)

            def branch(j, u0, free_a, free_b, ready):
                for first, last in ((0, 1), (1, 4)):
                    with pe.Fori(first, last) as i:
                        for k, x in enumerate("AB"):
                            unit(i * 3 + (u0 + k))
                            free = (s[f"m{x}"], i + 4 * j) if first else (free_a, free_b)[k]
                            gemm((u0 + k) % RING, GP[k], all_k, done=s[f"g{x}"], free=(free,))
                        if not first:
                            for sem_, n in ready:
                                pe.wait_ge(sem_, n)
                        unit(i * 3 + (u0 + 2))
                        for k, x in enumerate("AB"):
                            gemm((u0 + 2) % RING, GP[k], [(2 * t + k, t) for t in range(NT)], ahi, alo, done=s[f"b{x}"],
                                 begin=k == 0, free=((s[f"sg{x}"], i + (4 * j + 1)),))

            branch(0, U_BRA, (s["ss_done"], DB), (s["sal_done"], DB), ((s["sal_done"], DB), (s["pad_done"], 2)))
            pe.wait_ge(s["mA"], 4)
            pe.wait_ge(s["mB"], 4)
            with pe.Fori(0, NT) as i:
                unit(i * 3 + U_CONV)
                gemm(U_CONV % RING, psA, all_k, done=s["cc_done"])
                unit(i * 3 + (U_CONV + 1))
                gemm((U_CONV + 1) % RING, psB, all_k, done=s["ch_done"])
                unit(i * 3 + (U_CONV + 2))
                gemm((U_CONV + 2) % RING, psA, all_k, done=s["cb_done"], free=((s["cc_copied"], i + 1),))
                pe.wait_ge(s["ul_done"], i + 1)
                tr(mi[0][0:18, 0:P], ulast[:, :], ident[:, :]).then_inc(s["ul_tr"], 1)
                pe.wait_ge(s["y_done"], i + 1)
            branch(1, U_BRC, (s["y_done"], NT), (s["u_done"], NT), ((s["clo_done"], NT),))
            for g in range(NT):
                u0 = U_POOL + g
                unit(u0)
                pe.wait_ge(s["mB" if g else "mA"], 8)
                if g >= 2:
                    pe.wait_ge(s["pcopied"], g - 1)
                gemm(u0 % RING, GP[g % 2], all_k, done=s["gemm_done"])
                pe.wait_ge(s["pcopied"], g + 1)
                if g:
                    pe.wait_ge(s["pt2_copied"], g)
                tr(mi[0][0:PST, 0:P], pb[:, LEAD + NP - PST:LEAD + NP], ident[:, :])
                tr(mi[0][0:NS, P:2 * P], pb[:, LEAD + NP:LEAD + TU], ident[:, :]).then_inc(s["pt2_tr"], 1)
            unit(U_POOL + NT)
            for g in range(NT):
                if g >= 2:
                    pe.wait_ge(s["mlo_done"], g - 1)
                pe.wait_ge(s["plo_done"], g + 1)
                gemm((U_POOL + NT) % RING, GP[g % 2], [(g, g)], ahi, alo, done=s["gemm_done"],
                     begin=g == 0)
            branch(2, U_BRP, (s["mlo_done"], NT), (s["mlo_done"], NT), ((s["mlo_done"], NT),))
            pe.wait_ge(s["hlo_done"], 2 * KD)
            for k in range(KD):
                unit(U_WO + k)
                pe.wait_ge(s["mB" if k else "mA"], 12)
                if k >= 2:
                    pe.wait_ge(s["wo_ev"], k - 1)
                gemm((U_WO + k) % RING, GP[k % 2], all_k, done=s["gemm_done"])
            for k in range(KD):
                pe.wait_ge(s["wo_ev"], 7 if k < 7 else 8)
                for c in range(3):
                    m = mm(psA[:, c, 0:CH], mean1[:, :], merged[:, k, c * CH:(c + 1) * CH], start=k == 0, stop=k == KD - 1)
            m.then_inc(s["mean_done"], 1)
            for k in range(KD):
                pe.wait_ge(s["sq_done"], k + 1)
                for c in range(3):
                    m = mm(psB[:, c, 0:CH], mean1[:, :], tmp[k % 2][:, c * CH:(c + 1) * CH], start=k == 0, stop=k == KD - 1)
                m.then_inc(s["var_done"], 1)

            def hidden(u0, slot, free_a=(), free_b=()):
                unit(u0)
                gemm(slot % RING, psA, all_k, done=s["fg_done"], free=free_a)
                unit(u0 + 1)
                gemm((slot + 1) % RING, psB, all_k, done=s["fu_done"], free=free_b)

            def downs(i, u0, slot):
                for h in range(2):
                    unit(u0 + h)
                    for t in range(4 * h, 4 * h + 4):
                        if t < 2:
                            pe.wait_ge(s["sil_done" if t == 0 else "ft_done"], 2 * i + 3 if not (isinstance(i, int) and i == FFIT - 1) else 2 * FFIT)
                        else:
                            pe.wait_ge(s["dn_ev"], i * KD + (t - 1))
                        if t == 0:
                            pe.wait_ge(s["flo_done"], 2 * i + 2)
                        gemm((slot + h) % RING, GP[t % 2], [(k * 4 + t % 4, k) for k in range(2)], ahi, alo, done=s["dn_done"],
                             begin=t == 4 * h)

            pe.wait_ge(s["hlo_done"], 3 * KD)
            hidden(U_FF0, U_FF0)
            hidden(U_FF0 + 2, U_FF0 + 2, [(s["sil_done"], 1)], [(s["ft_done"], 1)])
            with pe.Fori(1, FFIT) as i:
                u0 = i * 6 + (U_FF - 6)
                hidden(u0, U_FF, [(s["sil_done"], 2 * i)], [(s["ft_done"], 2 * i)])
                downs(i - 1, u0 + 2, U_FF + 2)
                hidden(u0 + 4, U_FF + 4, [(s["dn_ev"], i * KD - 1)], [(s["dn_ev"], i * KD)])
            downs(FFIT - 1, U_FFE, U_FFE)
            pe.wait_ge(s["dn_part"], 3 * KD * FFIT)
            for t in range(QT + 1):
                n = P if t < QT else NS
                if t >= 2:
                    pe.wait_ge(s["yn_done"], t - 1)
                for k in range(KD):
                    m = tr(GP[t % 2][0:n, k // 4, (k % 4) * P:(k % 4 + 1) * P], merged[:, k, t * P:t * P + n], ident[:, :])
                m.then_inc(s["yt_done"], 1)


_INS = ["x_prompt", "x_sample", "cache_k", "cache_v", "cache_logf", "state_conv", "state_pool", "page_table", "c_prompt",
        "c_sample", "ada_w", "ada_b", "w_in", "b_forget", "conv_w", "pool_w", "pool_scale", "w_br_attn", "w_br_conv",
        "w_br_pool", "w_o", "ln1_g", "ln1_b", "w_gate_up", "w_down", "ln2_g", "ln2_b"]
_OUTS = {
    "y_prompt": (1, NP, D), "y_sample": (DB, DS, D),
    "k_prompt": (1, 1, NP, H, HD), "v_prompt": (1, 1, NP, H, HD), "logf_prompt": (1, 1, NP, H),
    "conv_prompt": (1, 1, 2, HALF), "pool_prompt": (1, 1, PST, HALF),
    "k_sample": (1, DB, DS, H, HD), "v_sample": (1, DB, DS, H, HD), "logf_sample": (1, DB, DS, H),
    "conv_sample": (1, DB, 2, HALF), "pool_sample": (1, DB, PST, HALF),
}


def kernel(**inputs):
    import concourse.bacc as bacc
    from concourse.bass_utils import run_bass_kernel_spmd

    nc = bacc.Bacc("TRN2", target_bir_lowering=False, num_devices=1, dynamic_dma_scratch_size=8192)
    arrays, a = {}, {}
    for name in _INS:
        x = np.ascontiguousarray(inputs[name])
        arrays[f"in_{name}"] = x
        a[name] = nc.dram_tensor(f"in_{name}", x.shape, mybir.dt.from_np(x.dtype), kind="ExternalInput").ap()
    out = {n: nc.dram_tensor(f"out_{n}", sh, F32, kind="ExternalOutput").ap() for n, sh in _OUTS.items()}
    build(nc, a, out)
    r = run_bass_kernel_spmd(nc, [arrays], core_ids=[0])
    return tuple(r.results[0][f"out_{n}"] for n in _OUTS)
```

```python
from contextlib import ExitStack

import numpy as np

import concourse.bass as bass
from concourse import mybir

F32 = mybir.dt.float32
F32R = mybir.dt.float32r
I32 = mybir.dt.int32
ALU = mybir.AluOpType
ACT = mybir.ActivationFunctionType

P = 128
D = 1024
KD = D // P
NP = 1024
QT = NP // P
DB, DS = 8, 8
NS = DB * DS
T = 1092
TU = NP + NS
CH = T // 3
SC = NP - 2 * CH
H, HD = 8, 64
HP = H // 2
PAST, PAGE = 1024, 128
NPG = PAST // PAGE
LK = PAST + DS
KH = PAST // 2
LR = KH + DS
HALF = 512
NT = HALF // P
POOL_WIN = (2, 4, 8, 16)
POOL_ORDER = (3, 2, 1, 0)
PST = 15
LEAD = 16
FF = 2816
FFIT = FF // (2 * P)
OFF_Q, OFF_K, OFF_V, OFF_F = 0, HALF, 2 * HALF, 3 * HALF
OFF_CB = OFF_F + H
OFF_CC, OFF_CH, OFF_P, OFF_G = (OFF_CB + i * HALF for i in (1, 2, 3, 4))
ALPHA = 2 ** 0.25
EPS = 1e-5
NEG = -1.0e30
NCOND = 1 + DB
SH1, SC1, G1, SH2, SC2, G2 = (KD * i for i in range(6))
ADAC = 6 * D // 512
V_ADA, V_L1G, V_L1B, V_CW, V_PS, NVEC = 0, 48, 56, 64, 76, 80
U_F, U_QKV, U_BRA, U_CONV, U_BRC, U_POOL, U_BRP, U_WO, U_FF0, U_FF, U_FFE, U_END = (
    0, 1, 13, 25, 37, 49, 54, 66, 74, 78, 138, 140)
RING = 3
NTILE = 2 * QT
GROUPS = [(n, list(range(j, min(j + 4, n // 2 + 1))))
          for n in range(NTILE) for j in range(0, n // 2 + 1, 4)]
NG = len(GROUPS)
LAST_GROUP = [max(g for g, (n, _) in enumerate(GROUPS) if n == t) for t in range(NTILE)]
PAIRS = [(i, j) for i in range(QT) for j in range(0, i + 1, 4)]


class Links:

    def __init__(self, eng, sem):
        self.eng, self.sem, self.n, self.off = eng, sem, 0, 0

    def __call__(self, ins):
        ins.then_inc(self.sem, 1)
        self.n += 1
        self.eng.wait_ge(self.sem, self.off + self.n)

    def enter(self, turn, per):
        self.base, self.per, self.off, self.n = self.n, per, turn * per + self.n, 0

    def leave(self, turns):
        assert self.n == self.per, f"{self.n} links in the loop's body, not {self.per}"
        self.off, self.n = 0, self.base + turns * self.per


def build(nc, a, out):
    with ExitStack() as ctx:
        def sem(name):
            return ctx.enter_context(nc.semaphore(name))

        size = (nc.sbuf_bytes_remaining - 64) // 128 * 128
        ctx.enter_context(nc.sbuf_tensor("arena", [P, size // 4], F32))
        base = (nc.sbuf_base - size + 31) // 32 * 32

        class Region:
            def __init__(self, off, size):
                self.off, self.end = off, off + size

            def __call__(self, name, shape, dt=F32):
                o = self.off
                self.off += (4 * int(np.prod(shape[1:])) + 31) // 32 * 32
                assert self.off <= self.end, (name, self.off - self.end)
                return nc.alloc_sbuf_tensor_at(name, shape, dt, offset=o)

        HSZ, MSZ = 4 * 2 * KD * T, 4 * KD * T
        r_h, r_a = base, base + HSZ
        r_m = r_a + MSZ
        r_w = r_m + MSZ
        keep = Region(r_w, base + size - r_w)

        raw = [keep(f"raw{i}", [P, 8, P]) for i in range(RING)]
        whi = [keep(f"whi{i}", [P, 8, P], F32R) for i in range(RING)]
        wlo = [keep(f"wlo{i}", [P, 8, P], F32R) for i in range(RING)]
        ident = keep("ident", [P, P])
        identr = keep("identr", [P, P], F32R)
        maskr = keep("maskr", [P, P], F32R)
        mod = keep("mod", [P, 6 * KD, NCOND])
        vecs = keep("vecs", [P, NVEC])
        q_s = keep("q_s", [P, HP, NS])
        k_s = keep("k_s", [P, HP, NS])
        pst = keep("pst", [P, NT, DB * PST])
        cst = keep("cst", [P, NT, DB * 2])
        recip = keep("recip", [P, LEAD])
        zeros = keep("zeros", [P, 16])
        ones = keep("ones", [P, 1])
        eps = keep("eps", [P, 1])
        scaled = keep("scaled", [P, KD, NCOND])
        aln = keep("aln", [P, 2 * KD])
        stat = keep("stat", [P, 16])
        other = keep("other", [P, 1])
        rowmax, negmax, rowsum, rowinv = (stat[:, 2 * i:2 * i + 2] for i in range(4))
        bfor = keep("bfor", [H, 1])
        ptab = keep("ptab", [1, DB * NPG], I32)
        maskn = keep("maskn", [P, DS])
        fold = keep("fold", [P, DS])
        blockmask = keep("blockmask", [P, H])
        r_s, r_end = keep.off, base + size

        hhi = Region(r_h, HSZ)("hhi", [P, KD, T], F32R)
        hlo = Region(r_h + HSZ // 2, HSZ // 2)("hlo", [P, KD, T], F32R)
        merged = Region(r_m, MSZ)("merged", [P, KD, T])
        ahi = Region(r_a, MSZ // 2)("ahi", [P, NT, T], F32R)
        alo = Region(r_a + MSZ // 2, MSZ // 2)("alo", [P, NT, T], F32R)

        R = Region(r_h, HSZ)
        xtok = R("xtok", [P, QT + 1, D])
        c9 = R("c9", [NCOND, D])
        c9s = R("c9s", [NCOND, D])
        vtab = R("vtab", [NVEC, P])
        stok = R("stok", [DB * PST, HALF])
        ctok = R("ctok", [DB * 2, HALF])
        fill = R("fill", [P, P])
        foldh, maskh = R("foldh", [P, H, DS]), R("maskh", [P, H, DS])
        R = Region(r_a, MSZ)
        ada = [R("ada0", [P, KD, 512]), R("ada1", [P, KD, 512])]
        modrow = R("modrow", [P, 2, P])
        ct = R("ct", [P, KD, 32])
        tail = 4 * NPG * DB * H
        S = Region(r_end - tail, tail)
        lfpast = S("lfpast", [P, NPG, DB, H])
        xt = Region(r_m, MSZ)("xt", [P, KD, T])
        R = Region(r_s + 4 * 2 * NP, r_end - tail - r_s - 4 * 2 * NP)
        S = Region(R.off, R.end - R.off)
        ht = [S("ht0", [P, T]), S("ht1", [P, T])]
        z8, nl8, e8 = R("z8", [H, T]), R("nl8", [H, T]), R("e8", [H, T])
        lfall = R("lfall", [NS, LK])
        dsamp = R("dsamp", [NS, LK])
        lfo = R("lfo", [P, QT, H])
        lfs = R("lfs", [NS, H])
        R = Region(r_m, MSZ)
        qhi, qlo = R("qhi", [P, T], F32R), R("qlo", [P, T], F32R)
        khi, klo = R("khi", [P, T], F32R), R("klo", [P, T], F32R)
        kv = R("kv", [P, T])
        vhi, vlo = R("vhi", [P, QT, P], F32R), R("vlo", [P, QT, P], F32R)
        S = Region(r_s, r_end - tail - r_s)
        decay = S("decay", [P, 2, NP])
        tok = R("tok", [P, QT + 1, P])
        pt = [[S(f"pt{part}{i}", [P, 4, 2, P], F32R) for part in ("hi", "lo")] for i in range(2)]
        pthi, ptlo = zip(*pt)
        tokv = Region(S.off - 4 * 2 * 8 * P, 4 * 2 * 8 * P)("tokv", [P, QT + 1, P])
        prob = [S("prob0", [P, NP]), S("prob1", [P, NP])]
        R = Region(r_m, MSZ)
        kpage = R("kpage", [P, NPG, HALF])
        kt_s = R("kt_s", [P, HP, LK])
        S = Region(r_s, r_end - r_s)
        vpage = S("vpage", [P, NPG + 1, HALF])
        decs = S("decs", [P, LR])
        ptrs = S("ptrs", [P, NPG // 2 + 1, P])
        qbd = S("qbd", [P, 320])
        om = S("om", [P, HALF])
        S = Region(r_s, r_end - r_s)
        sg = [S("sg0", [P, T]), S("sg1", [P, T])]
        part = [S("part0", [P, T]), S("part1", [P, T])]
        S = Region(r_s, r_end - r_s)
        cc = S("cc", [P, T])
        u = S("u", [P, 2 + T])
        us = S("us", [P, DB, 2 + DS])
        yc = S("yc", [P, T])
        ulast = S("ulast", [P, 18])
        utok = S("utok", [18, P])
        S = Region(r_s, r_end - r_s)
        pb = S("pb", [P, LEAD + T])
        w1, w2 = S("w1", [P, LEAD + NP]), S("w2", [P, LEAD + NP])
        ps0, ps1, ps2 = (S(f"ps{i}", [P, DB, LEAD + DS]) for i in range(3))
        yp = S("yp", [P, T])
        ptok = S("ptok", [NS, 2, P])
        S = Region(r_s, r_end - r_s)
        xr = [S("xr0", [P, T]), S("xr1", [P, T])]
        tmp = [S("tmp0", [P, T]), S("tmp1", [P, T])]
        rstd = S("rstd", [P, T])
        mean1 = S("mean1", [P, P])
        ysum = S("ysum", [P, T])
        S = Region(r_s, r_end - r_s)
        sil = [S("sil0", [P, T]), S("sil1", [P, T])]
        ft = [S("ft0", [P, T]), S("ft1", [P, T])]
        t64 = S("t64", [P, 2, NS])
        R = Region(r_h, HSZ)
        gb = R("gb", [P, 2, D])
        yo = [R(f"yo{i}", [P, D]) for i in range(3)]
        bst = R("bst", [P, 2, 2, 6])
        mv = R("mv", [P, 2, 5])

        def pst_(name, shape):
            return ctx.enter_context(nc.psum_tensor(name, shape, F32))

        psA, psB = pst_("psA", [P, 3, 512]), pst_("psB", [P, 3, 512])
        mi = [pst_("ps6", [P, 512]), pst_("ps7", [P, 512])]
        GP = [psA, psB]

        def cols(ps, n=P):
            return ps[0:n, :, 0:CH]

        def c3(x):
            return x.rearrange("p (c n) -> p c n", c=3)

        def flat(ps):
            return ps[:, :, :].rearrange("p a b -> p (a b)")

        def scratch(name, shape):
            return nc.dram_tensor(name, shape, F32).ap()

        x_keep = scratch("x_keep", [P, KD, T])
        nd_p = scratch("nd_p", [H, NP])
        nd_s = scratch("nd_s", [NS, LK])

        w_in, w_gu, w_dn, w_o = a["w_in"][0], a["w_gate_up"][0], a["w_down"][0], a["w_o"][0]

        names = """
            c_in vec_in x_in st_in lfp_in lfq_in pt_in ada0_in ada1_in consts eye idle c_silu
            setup_tr setup_copied x_tr x_dve x_act x_stored lfp_tr lfp_copied
            ada_used modrow_done mod_tr mod_done sc1_done hp_done hs_done hhi_done hlo_done
            raw0 raw1 raw2 w_split w_begun dve_link act_link pool_link gemm_done
            z_done e_done lf_done lf_tr lf_copied lfs_out lfnew_in scan_done ndp_out nds_out early_out
            q_done k_done v_done qhi_done ql_done kv_done kl_done vf_done tok_tr tok_copied kst vst vl_done decay_in
            s_done mx_done p_done pn_done tr_done pth_done ptl_done o_done ah_done al_done
            kpg_in vpg_in dec_in vnew_in kt_tr kt_act kt_dve qbd_zero qbd_done ss_done sm_done se_done sp_done
            pt_tr pt_act pt_dve ov_done om_done fold_done sah_done sal_done pad_done
            cb_done cc_done ch_done cc_copied u_done y_done chi_done clo_done ul_done ul_tr ul_copied ul_out
            pcopied pf_done phi_done plo_done pt2_tr pt2_copied pt2_out mhi_done mlo_done
            wo_ev xr0_in xr1_in ysum_done mean_done d_done sq_done var_done sd_done xn_done xa_done
            fg_done fu_done sil_done ft_done fhi_done flo_done dn_done dn_ev dn_part
            gb_in yt_done yv_done ysd_done yr_done yn_done ym_done yg_done y0_out y1_out y2_out""".split()
        s = {n: sem(n) for n in names}
        for n in ("gA", "gB", "bA", "bB", "sgA", "sgB", "mA", "mB"):
            s[n] = sem(n)
        raw_in = [s["raw0"], s["raw1"], s["raw2"]]
        ada_in = [s["ada0_in"], s["ada1_in"]]

        def x_group(g):
            if g < 2 * KD:
                return xt[:, g // 2, 512 * (g % 2):512 * (g % 2) + 512]
            return xt[:, 4 * (g - 2 * KD):4 * (g - 2 * KD) + 4, NP:TU]

        def x_bank(g):
            ps = psB[:, g % 3, 0:512 if g < 2 * KD else 4 * NS]
            return ps if g < 2 * KD else ps.rearrange("p (a b) -> p a b", b=NS)

        def kt_group(g):
            return kt_s[:, g % HP, 512 * (g // HP):512 * (g // HP) + 512]

        att_s = psB[:, 1, P:P + HP * DS].rearrange("p (a b) -> p a b", a=HP)

        def modrow_copy(act, j):
            act.wait_ge(s["ada_used"], j + 1)
            if j >= 2:
                act.wait_ge(s["mod_tr"], j - 1)
            nc.scalar.copy(modrow[:, j % 2, :], mi[j % 2][:, 0:P]).then_inc(s["modrow_done"], 1)

        def mod_chunk(dve, j):
            dve.wait_ge(s["mod_tr"], j + 1)
            nc.vector.tensor_tensor(mod[:, 4 * j:4 * j + 4, :],
                                    mi[j % 2][:, P:2 * P].rearrange("p (a b) -> p a b", a=4)[:, :, 0:NCOND],
                                    vecs[:, V_ADA + 4 * j:V_ADA + 4 * j + 4, None].to_broadcast([P, 4, NCOND]),
                                    ALU.add).then_inc(s["mod_done"], 1)

        def apart(eng):
            eng.sem_inc(s["idle"], 1)

        def page_loads(eng, b, buf, name, loaded, pages=range(NPG)):
            for g in pages:
                page = eng.value_load(ptab[0:1, bass.ds(b * NPG + g, 1)], min_val=0, max_val=a[name].shape[1] - 1)
                eng.dma_start(buf[:, g, :], a[name][0, bass.ds(page, 1)].rearrange("o p h d -> p (o h d)")).then_inc(loaded, 16)

        def forget_loads(eng, b, loaded):
            for g in range(NPG):
                page = eng.value_load(ptab[0:1, bass.ds(b * NPG + g, 1)], min_val=0, max_val=a["cache_logf"].shape[1] - 1)
                eng.dma_start(lfpast[:, g, bass.ds(b, 1), :],
                              a["cache_logf"][0, bass.ds(page, 1), :, :].rearrange("o p h -> p o h")).then_inc(loaded, 16)

        block = ctx.enter_context(nc.Block())

        @block.sync
        def _(sp):
            def wunit(u, slot, src, shape=None):
                if not isinstance(u, int) or u >= RING:
                    sp.wait_ge(s["w_split"], u - RING + 1)
                    if not isinstance(u, int):
                        apart(sp)
                dst = raw[slot][:, :, :]
                if shape:
                    dst = dst.rearrange("p (k j) n -> p k (j n)", k=shape)
                sp.dma_start(dst, src).then_inc(raw_in[slot], 16)

            def tiles(w, c, n=P):
                return w.rearrange("(k p) n -> p k n", p=P)[:, :, bass.ds(c, n)]

            sp.dma_start(c9[0:1, :], a["c_prompt"]).then_inc(s["c_in"], 16)
            sp.dma_start(c9[1:NCOND, :], a["c_sample"]).then_inc(s["c_in"], 16)
            sp.dma_start(ptab[:, :], a["page_table"].rearrange("b (o n) -> o (b n)", o=1)).then_inc(s["pt_in"], 16)
            sp.dma_start(stok[:, :], a["state_pool"].rearrange("o b t c -> (o b t) c")).then_inc(s["st_in"], 16)
            sp.dma_start(ctok[:, :], a["state_conv"].rearrange("o b t c -> (o b t) c")).then_inc(s["st_in"], 16)
            sp.dma_start(bfor[:, :], a["b_forget"].rearrange("o h -> h o")).then_inc(s["st_in"], 16)
            xv = a["x_prompt"][0].rearrange("(n p) d -> p n d", p=P)
            for j in range(2):
                sp.dma_start(xtok[:, 4 * j:4 * j + 4, :], xv[:, 4 * j:4 * j + 4, :]).then_inc(s["x_in"], 16)
            sp.dma_start(xtok[0:NS, QT, :], a["x_sample"].rearrange("b t d -> (b t) d")).then_inc(s["x_in"], 16)
            for row, src in ((V_ADA, a["ada_b"].rearrange("o (t p) -> (o t) p", p=P)),
                             (V_L1G, a["ln1_g"].rearrange("o (t p) -> (o t) p", p=P)),
                             (V_L1B, a["ln1_b"].rearrange("o (t p) -> (o t) p", p=P)),
                             (V_CW, a["conv_w"].rearrange("o k (t p) -> (o k t) p", p=P)),
                             (V_PS, a["pool_scale"].rearrange("o (t p) -> (o t) p", p=P))):
                sp.dma_start(vtab[row:row + src.shape[0], :], src).then_inc(s["vec_in"], 16)
            adav = a["ada_w"][0].rearrange("(k p) n -> p k n", p=P)

            def ada_chunk(j):
                if j >= 2:
                    sp.wait_ge(s["ada_used"], j - 1)
                sp.dma_start(ada[j % 2][:, :, :], adav[:, :, 512 * j:512 * j + 512]).then_inc(ada_in[j % 2], 16)

            ada_chunk(0)
            ada_chunk(1)
            sp.wait_ge(s["pt_in"], 16)
            with sp.Fori(1, 3) as b:
                forget_loads(sp, b, s["lfq_in"])
            ada_chunk(2)
            ada_chunk(3)
            wunit(0, 0, tiles(w_in, OFF_F))
            wunit(1, 1, tiles(w_in, OFF_Q))
            sp.wait_ge(s["x_dve"], 10)
            sp.wait_ge(s["x_act"], 9)
            sp.dma_start(x_keep, xt[:, :, :]).then_inc(s["x_stored"], 16)
            wunit(2, 2, tiles(w_in, OFF_K))
            for j in range(4, 8):
                ada_chunk(j)
            wunit(3, 0, tiles(w_in, OFF_V))
            ada_chunk(8)
            ada_chunk(9)
            sp.wait_ge(s["lfs_out"], 16)
            sp.wait_ge(s["lfp_copied"], 1)
            for b in range(DB):
                sp.dma_start(lfall[b * H:(b + 1) * H, PAST:LK], out["logf_sample"][0, b].rearrange("t h -> h t"),
                             allow_slow_non_contiguous=True).then_inc(s["lfnew_in"], 16)
            ada_chunk(10)
            ada_chunk(11)
            sp.wait_ge(s["scan_done"], 2)
            sp.dma_start(nd_s, dsamp[:, :]).then_inc(s["nds_out"], 16)
            sp.dma_start(out["pool_sample"][0, :, 0:PST - DS, :], a["state_pool"][0, :, DS:PST, :]).then_inc(s["early_out"], 16)
            with sp.Fori(1, HP) as p:
                for j, off in enumerate((OFF_Q, OFF_K, OFF_V)):
                    wunit(p * 3 + (U_QKV + j), (U_QKV + j) % RING, tiles(w_in, p * P + off))
            for j in range(2):
                wunit(U_BRA + j, (U_BRA + j) % RING, tiles(w_in, OFF_G + j * P))
            wunit(U_BRA + 2, (U_BRA + 2) % RING, tiles(a["w_br_attn"][0], 0, 2 * P), 4)
            sp.wait_ge(s["s_done"], NTILE * HP)
            for half in range(2):
                page_loads(sp, 0, kpage, "cache_k", s["kpg_in"], range(4 * half, 4 * half + 4))
            sp.wait_ge(s["al_done"], NTILE * HP)
            sp.wait_ge(s["vl_done"], HP)
            sp.wait_ge(s["vst"], 32 * HP)
            sp.wait_ge(s["kst"], 32 * HP)
            sp.wait_ge(s["o_done"], QT * HP)

            def key_loads(b, half):
                sp.wait_ge(s["kt_tr"], b * 2 * HP - HP * (1 - half))
                apart(sp)
                page_loads(sp, b, kpage, "cache_k", s["kpg_in"], range(4 * half, 4 * half + 4))

            def decay_loads(b):
                if not isinstance(b, int) or b:
                    sp.wait_ge(s["pt_tr"], 2 * b)
                    apart(sp)
                for half in range(2):
                    for c, src, w in ((0, half * KH, KH), (KH, PAST, DS)):
                        sp.dma_start(decs[half * NS:(half + 1) * NS, c:c + w],
                                     nd_s[bass.ds(b * H, H), None, src:src + w].to_broadcast([H, DS, w])).then_inc(s["dec_in"], 16)

            decay_loads(0)
            key_loads(1, 0)
            key_loads(1, 1)
            with sp.Fori(1, DB - 1) as b:
                key_loads(b + 1, 0)
                decay_loads(b)
                key_loads(b + 1, 1)
            decay_loads(DB - 1)

            def branch_loads(u0, gate, w, first=0):
                with sp.Fori(first, 4) as i:
                    for j in range(2):
                        wunit(i * 3 + (u0 + j), (u0 + j) % RING, tiles(w_in, i * 256 + (OFF_G + gate * D + j * P)))
                    wunit(i * 3 + (u0 + 2), (u0 + 2) % RING, tiles(w, i * 256, 256), 4)

            branch_loads(U_BRA, 0, a["w_br_attn"][0], 1)
            with sp.Fori(0, NT) as i:
                for j, off in enumerate((OFF_CC, OFF_CH, OFF_CB)):
                    wunit(i * 3 + (U_CONV + j), (U_CONV + j) % RING, tiles(w_in, i * P + off))
            branch_loads(U_BRC, 1, a["w_br_conv"][0])
            for j, g in enumerate(POOL_ORDER):
                wunit(U_POOL + j, (U_POOL + j) % RING, tiles(w_in, OFF_P + g * P))
            sp.wait_ge(s["w_split"], U_POOL + 4 - RING + 1)
            sp.dma_start(raw[(U_POOL + 4) % RING][:, 0:NT, :],
                         a["pool_w"][0].rearrange("g c d -> c g d")).then_inc(raw_in[(U_POOL + 4) % RING], 16)
            branch_loads(U_BRP, 2, a["w_br_pool"][0])
            for j in range(KD):
                wunit(U_WO + j, (U_WO + j) % RING, tiles(w_o, j * P))

            def ff_cols(u0, slot, i, f):
                for j in range(2):
                    wunit(u0 + j, (slot + j) % RING, tiles(w_gu, i * 256 + (j * FF + f * P)))

            def dn_rows(u0, slot, i):
                rows = w_dn.rearrange("(i k p) n -> i p k n", k=2, p=P)
                for j in range(2):
                    src = rows[bass.ds(i, 1), :, :, j * 512:j * 512 + 512].rearrange("o p k n -> p (o k) n")
                    wunit(u0 + j, (slot + j) % RING, src, 2)

            ff_cols(U_FF0, U_FF0, 0, 0)
            ff_cols(U_FF0 + 2, U_FF0 + 2, 0, 1)
            with sp.Fori(1, FFIT) as i:
                u0 = i * 6 + (U_FF - 6)
                ff_cols(u0, U_FF, i, 0)
                dn_rows(u0 + 2, U_FF + 2, i - 1)
                ff_cols(u0 + 4, U_FF + 4, i, 1)
            dn_rows(U_FFE, U_FFE, FFIT - 1)
            sp.wait_ge(s["fg_done"], 2 * FFIT)
            sp.wait_ge(s["fu_done"], 2 * FFIT)
            sp.dma_start(gb[:, 0, :], a["ln2_g"].to_broadcast([P, D])).then_inc(s["gb_in"], 16)
            sp.dma_start(gb[:, 1, :], a["ln2_b"].to_broadcast([P, D])).then_inc(s["gb_in"], 16)
            outs = (s["y0_out"], s["y1_out"], s["y2_out"])
            for t in range(QT + 1):
                sp.wait_ge(s["yg_done"], t + 1)
                if t < QT:
                    sp.dma_start(out["y_prompt"][0, t * P:(t + 1) * P, :], yo[t % 3][:, :]).then_inc(outs[t % 3], 16)
                else:
                    sp.dma_start(out["y_sample"].rearrange("b t d -> (b t) d"), yo[t % 3][0:NS, :]).then_inc(outs[t % 3], 16)
            for o in outs:
                sp.wait_ge(o, 48)
            sp.wait_ge(s["early_out"], 32)
            sp.wait_ge(s["lfs_out"], 16)
            sp.wait_ge(s["kst"], 32 * HP)
            sp.wait_ge(s["vst"], 32 * HP)
            sp.wait_ge(s["ul_out"], 32 * NT)
            sp.wait_ge(s["pt2_out"], 32 * NT)

        @block.gpsimd
        def _(pool):
            link = Links(pool, s["pool_link"])
            link(nc.gpsimd.memset(ident[:, :], 0.0))
            link(nc.gpsimd.affine_select(out=ident[:, :], in_=ident[:, :], compare_op=ALU.not_equal, fill=1.0,
                                         base=0, pattern=[[-1, P]], channel_multiplier=1))
            nc.gpsimd.tensor_copy(identr[:, :], ident[:, :]).then_inc(s["eye"], 1)
            link(nc.gpsimd.memset(fill[:, :], 0.0))
            link(nc.gpsimd.affine_select(out=fill[:, :], in_=fill[:, :], compare_op=ALU.is_ge, fill=NEG,
                                         base=0, pattern=[[-1, P]], channel_multiplier=1))
            nc.gpsimd.tensor_copy(maskr[:, :], fill[:, :]).then_inc(s["eye"], 1)
            nc.gpsimd.memset(zeros[:, :], 0.0).then_inc(s["consts"], 1)
            nc.gpsimd.memset(ones[:, :], 1.0).then_inc(s["consts"], 1)
            nc.gpsimd.memset(eps[:, :], EPS).then_inc(s["consts"], 1)

            def band(x, fill_, lo):
                return nc.gpsimd.affine_select(
                    out=x, in_=x, compare_op=ALU.is_ge, fill=fill_, base=0 if lo else DS - 1,
                    pattern=[[-DS if lo else DS, H]] + ([[0, DS]] if len(x.shape) == 3 else []),
                    channel_multiplier=1 if lo else -1)

            link(nc.gpsimd.memset(blockmask[:, :], 1.0))
            link(nc.gpsimd.memset(foldh[:, :, :], 0.0))
            link(nc.gpsimd.memset(maskh[:, :, :], NEG))
            for half in range(2):
                rows = slice(NS * half, NS * half + NS)
                link(band(blockmask[rows, :], 0.0, True))
                link(band(blockmask[rows, :], 0.0, False))
                link(nc.gpsimd.affine_select(out=foldh[rows, :, :], in_=foldh[rows, :, :], compare_op=ALU.not_equal, fill=1.0,
                                             base=0, pattern=[[-DS, H], [-1, DS]], channel_multiplier=1))
            rows = slice(NS, 2 * NS)
            link(band(maskh[rows, :, :], 0.0, True))
            link(band(maskh[rows, :, :], 0.0, False))
            nc.gpsimd.affine_select(out=maskh[rows, :, :], in_=maskh[rows, :, :], compare_op=ALU.is_gt, fill=0.0,
                                    base=0, pattern=[[DS, H], [1, DS]], channel_multiplier=-1).then_inc(s["consts"], 1)
            pool.wait_ge(s["consts"], 4)
            for t in range(LEAD):
                nc.gpsimd.memset(recip[:, t:t + 1], 1.0 / (t + 1)).then_inc(s["consts"], 1)

            def parts(slot, n=8):
                apart(pool)
                link(nc.gpsimd.tensor_copy(whi[slot][:, 0:n, :], raw[slot][:, 0:n, :]))
                nc.gpsimd.tensor_tensor(wlo[slot][:, 0:n, :], raw[slot][:, 0:n, :],
                                        whi[slot][:, 0:n, :].bitcast(F32), ALU.subtract).then_inc(s["w_split"], 1)

            def one(u, n=8):
                pool.wait_ge(raw_in[u % RING], 16 * (u // RING + 1))
                if u >= RING:
                    pool.wait_ge(s["w_begun"], u - RING + 2)
                parts(u % RING, n)

            def three(first, turns):
                with pool.Fori(0, turns) as i:
                    link.enter(i, 3)
                    for u in range(first, first + 3):
                        pool.wait_ge(raw_in[u % RING], i * 16 + 16 * (u // RING + 1))
                        pool.wait_ge(s["w_begun"], i * 3 + (u - RING + 2))
                        parts(u % RING)
                link.leave(turns)

            def values(p):
                pool.wait_ge(s["tok_copied"], p * 2 + 2)
                if not isinstance(p, int):
                    pool.wait_ge(s["o_done"], p * QT)
                apart(pool)
                link(nc.gpsimd.tensor_copy(vhi[:, :, :], tokv[:, 0:QT, :]))
                nc.gpsimd.tensor_tensor(vlo[:, :, :], tokv[:, 0:QT, :], vhi[:, :, :].bitcast(F32),
                                        ALU.subtract).then_inc(s["vl_done"], 1)

            pool.wait_ge(s["pt_in"], 16)
            with pool.Fori(3, DB) as b:
                forget_loads(pool, b, s["lfp_in"])
            for u_ in range(4):
                one(u_)
            values(0)
            with pool.Fori(1, HP) as p:
                link.enter(p - 1, 4)
                for j in range(3):
                    u_ = U_QKV + j
                    pool.wait_ge(raw_in[u_ % RING], p * 16 + 16 * (u_ // RING + 1))
                    pool.wait_ge(s["w_begun"], p * 3 + (u_ - RING + 2))
                    parts(u_ % RING)
                values(p)
            link.leave(HP - 1)
            pool.wait_ge(s["al_done"], NTILE * HP)
            pool.wait_ge(s["kst"], 32 * HP)
            pool.wait_ge(s["vst"], 32 * HP)
            nc.gpsimd.memset(qbd[:, :], 0.0).then_inc(s["qbd_zero"], 1)
            one(U_BRA)
            one(U_BRA + 1)
            pool.wait_ge(s["pt_in"], 16)
            def sample_values(b):
                page_loads(pool, b, vpage, "cache_v", s["vpg_in"])
                pool.dma_start(vpage[0:DS, NPG, :],
                               out["v_sample"][0, bass.ds(b, 1)].rearrange("o t h d -> t (o h d)")).then_inc(s["vnew_in"], 16)

            sample_values(0)
            with pool.Fori(1, DB) as b:
                pool.wait_ge(s["ov_done"], b)
                apart(pool)
                sample_values(b)
            one(U_BRA + 2)
            three(U_BRA + 3, (U_POOL - U_BRA - 3) // 3)
            for u_ in range(U_POOL, U_POOL + 4):
                one(u_)
            one(U_POOL + 4, NT)
            three(U_BRP, 4)
            for u_ in range(U_WO, U_FF):
                one(u_)
                k = u_ - U_WO - 3
                if 1 <= k <= 6:
                    pool.wait_ge(s["wo_ev"], k + 1)
                    if k > 1:
                        pool.wait_ge(s["ysum_done"], k - 1)
                    nc.gpsimd.tensor_tensor(ysum[:, :], merged[:, 0, :] if k == 1 else ysum[:, :], merged[:, k, :],
                                            ALU.add).then_inc(s["ysum_done"], 1)
            for k in range(KD):
                pool.wait_ge(s["hp_done"], KD + k + 1)
                pool.wait_ge(s["hs_done"], KD + k + 1)
                nc.gpsimd.tensor_scalar(merged[:, k, :], merged[:, k, :], aln[:, k:k + 1], aln[:, KD + k:KD + k + 1],
                                        ALU.mult, ALU.add).then_inc(s["xa_done"], 1)
            three(U_FF, 2 * (FFIT - 1))
            for u_ in range(U_FFE, U_END):
                one(u_)
            pool.wait_ge(s["gb_in"], 32)
            for t in range(QT + 1):
                n = P if t < QT else NS
                pool.wait_ge(s["ym_done"], t + 1)
                y = yo[t % 3][0:n, :]
                nc.gpsimd.tensor_tensor(y, y, gb[0:n, 1, :], ALU.add).then_inc(s["yg_done"], 1)

        @block.scalar
        def _(act):
            link = Links(act, s["act_link"])
            act.wait_ge(s["c_in"], 32)
            nc.scalar.activation(c9s[:, :], c9[:, :], ACT.Silu).then_inc(s["c_silu"], 1)
            act.wait_ge(s["pt_in"], 16)
            forget_loads(act, 0, s["lfq_in"])
            for g in range(1, 18, 2):
                act.wait_ge(s["x_tr"], g + 1)
                nc.scalar.copy(x_group(g), x_bank(g)).then_inc(s["x_act"], 1)
            for j in range(4):
                modrow_copy(act, j)
            act.wait_ge(s["sc1_done"], 1)
            act.wait_ge(s["x_dve"], 9)
            act.wait_ge(s["x_act"], 9)
            act.wait_ge(s["eye"], 2)
            for k in range(KD):
                if k >= 2:
                    act.wait_ge(s["hlo_done"], k - 1)
                nc.scalar.activation(ht[k % 2][:, 0:NP], xt[:, k, 0:NP], ACT.Identity, bias=mod[:, SH1 + k, 0:1],
                                     scale=mod[:, SC1 + k, 0:1]).then_inc(s["hp_done"], 1)
                act.wait_ge(s["hp_done"], k + 1)
                act.wait_ge(s["hs_done"], k + 1)
                nc.scalar.copy(hhi[:, k, :], ht[k % 2][:, :]).then_inc(s["hhi_done"], 1)
            act.wait_ge(s["lfp_tr"], 2)
            nc.scalar.copy(lfall[:, 0:PAST], flat(psB)[0:NS, 0:PAST]).then_inc(s["lfp_copied"], 1)
            act.wait_ge(s["z_done"], 1)
            link(nc.scalar.activation(e8[:, :], e8[:, :], ACT.Exp))
            nc.scalar.activation(e8[:, :], e8[:, :], ACT.Ln, bias=1.0).then_inc(s["e_done"], 1)
            modrow_copy(act, 4)
            modrow_copy(act, 5)
            act.wait_ge(s["scan_done"], 1)
            act.dma_start(nd_p, z8[:, 0:NP]).then_inc(s["ndp_out"], 16)
            act.wait_ge(s["lf_tr"], 1)
            nc.scalar.copy(lfs[:, :], psB[0:NS, 2, P:P + H]).then_inc(s["lf_copied"], 1)
            act.wait_ge(s["lf_copied"], 1)
            act.dma_start(out["logf_sample"][0].rearrange("b t h -> (b t) h"), lfs[:, :]).then_inc(s["lfs_out"], 16)
            nc.scalar.copy(lfo[:, :, :], psB[:, 2, 0:QT * H].rearrange("p (a b) -> p a b", b=H)).then_inc(s["lf_copied"], 1)
            act.wait_ge(s["lf_copied"], 2)
            act.dma_start(out["logf_prompt"][0, 0].rearrange("(n p) h -> p n h", p=P), lfo[:, :, :]).then_inc(s["early_out"], 16)

            def token_major(p, ps, which, dram_p, dram_s, stored):
                act.wait_ge(s["tok_tr"], p * 4 + (2 * which + 1))
                to = (tok, tokv)[which]
                link(nc.scalar.copy(to[:, 0:QT, :].rearrange("p (a b) c -> p a (b c)", a=2), ps[:, 0:2, :]))
                act.wait_ge(s["tok_tr"], p * 4 + (2 * which + 2))
                nc.scalar.copy(to[0:NS, QT, :], ps[0:NS, 2, 0:P]).then_inc(s["tok_copied"], 1)
                act.wait_ge(s["tok_copied"], p * 2 + (which + 1))
                dp = out[dram_p][0, 0].rearrange("(n p) h d -> p n (h d)", p=P)
                act.dma_start(dp[:, :, bass.ds(p * P, P)], to[:, 0:QT, :]).then_inc(s[stored], 16)
                ds_ = out[dram_s][0].rearrange("b t h d -> (b t) (h d)")
                act.dma_start(ds_[:, bass.ds(p * P, P)], to[0:NS, QT, :]).then_inc(s[stored], 16)

            for first, last in ((0, 1), (1, HP)):
                with act.Fori(first, last) as p:
                    link.enter(p - first, 2)
                    act.wait_ge(s["q_done"], p + 1)
                    if first:
                        act.wait_ge(s["s_done"], p * NTILE)
                    else:
                        act.wait_ge(s["x_stored"], 16)
                    nc.scalar.activation(c3(qhi[:, :]), cols(psA), ACT.Copy, scale=HD ** -0.5).then_inc(s["qhi_done"], 1)
                    if not first:
                        modrow_copy(act, 6)
                        modrow_copy(act, 7)
                    if first:
                        act.wait_ge(s["mx_done"], p * NTILE)
                    else:
                        act.wait_ge(s["ndp_out"], 16)
                    for r in range(2):
                        act.dma_start(decay[:, r, :], nd_p[bass.ds(2 * p + r, 1), :].to_broadcast([P, NP])).then_inc(s["decay_in"], 16)
                    act.wait_ge(s["k_done"], p + 1)
                    if first:
                        act.wait_ge(s["tok_tr"], p * 4)
                    nc.scalar.copy(c3(kv[:, :]), cols(psB)).then_inc(s["kv_done"], 1)
                    if not first:
                        for j in range(8, ADAC):
                            modrow_copy(act, j)
                    if first:
                        act.wait_ge(s["kst"], p * 32)
                    act.wait_ge(s["v_done"], p + 1)
                    act.wait_ge(s["kl_done"], p + 1)
                    act.wait_ge(s["tok_tr"], p * 4 + 2)
                    nc.scalar.copy(c3(kv[:, :]), cols(psA)).then_inc(s["vf_done"], 1)
                    token_major(p, psB, 0, "k_prompt", "k_sample", "kst")
                    if not first:
                        act.wait_ge(s["early_out"], 32)
                        act.wait_ge(s["ndp_out"], 16)
                        act.wait_ge(s["nds_out"], 16)
                    token_major(p, psA, 1, "v_prompt", "v_sample", "vst")

                    def exp(n):
                        w = (n // 2 + 1) * P
                        act.wait_ge(s["mx_done"], p * NTILE + (n + 1))
                        nc.scalar.activation(prob[n % 2][:, 0:w], prob[n % 2][:, 0:w], ACT.Exp, bias=negmax[:, n % 2:n % 2 + 1],
                                             accum_out=rowsum[:, n % 2:n % 2 + 1]).then_inc(s["p_done"], 1)

                    def pt_hi(n):
                        for g, (t, blocks) in enumerate(GROUPS):
                            if t != n:
                                continue
                            m = PAIRS.index((n // 2, blocks[0]))
                            act.wait_ge(s["tr_done"], p * NG + (g + 1))
                            if m >= 2:
                                act.wait_ge(s["o_done"], p * QT + (PAIRS[m - 2][0] + 1))
                            elif first:
                                act.wait_ge(s["o_done"], p * QT)
                            if m == 1 and n % 2 == 0:
                                act.wait_ge(s["vst"], p * 32 + 32)
                                act.wait_ge(s["vl_done"], p + 1)
                            nb = len(blocks)
                            nc.scalar.copy(pthi[m % 2][:, 0:nb, n % 2, :],
                                           mi[g % 2][:, 0:nb * P].rearrange("p (a b) -> p a b", a=nb)).then_inc(s["pth_done"], 1)

                    def a_hi(i):
                        act.wait_ge(s["o_done"], p * QT + (i + 1))
                        for r in range(2):
                            rows = slice(HD * r, HD * r + HD)
                            nc.scalar.copy(ahi[rows, bass.ds(p, 1), i * P:(i + 1) * P],
                                           GP[i % 2][rows, 2:3, r * P:(r + 1) * P]).then_inc(s["ah_done"], 1)

                    exp(0)
                    exp(1)
                    for i in range(QT):
                        pt_hi(2 * i)
                        pt_hi(2 * i + 1)
                        if i + 1 < QT:
                            exp(2 * i + 2)
                            exp(2 * i + 3)
                        a_hi(i)
                link.leave(last - first)

            nc.scalar.copy(ahi[:, :, TU:T], zeros[:, :].rearrange("p (a b) -> p a b", a=NT)).then_inc(s["pad_done"], 1)

            def keys_t(b, g):
                act.wait_ge(s["kt_tr"], b * 2 * HP + (g + 1))
                nc.scalar.copy(kt_group(g), mi[0][:, :]).then_inc(s["kt_act"], 1)

            def sample(b, more):
                if more:
                    keys_t(b + 1, 0)
                act.wait_ge(s["sm_done"], b + 1)
                nc.scalar.activation(decs[:, :], decs[:, :], ACT.Exp, bias=negmax[:, 0:1],
                                     accum_out=rowsum[:, 0:1]).then_inc(s["se_done"], 1)
                if more:
                    keys_t(b + 1, 2)
                    keys_t(b + 1, 4)
                act.wait_ge(s["pt_tr"], b * 2 + 1)
                nc.scalar.copy(ptrs[:, 0:NPG // 2, :].rearrange("p a b -> p (a b)"), psB[:, 0, :]).then_inc(s["pt_act"], 1)
                if more:
                    keys_t(b + 1, 6)
                act.wait_ge(s["fold_done"], b + 1)
                nc.scalar.copy(ahi[:, :, bass.ds(b * DS + NP, DS)], att_s).then_inc(s["sah_done"], 1)

            for g in range(0, 2 * HP, 2):
                keys_t(0, g)
            with act.Fori(0, DB - 1) as b:
                sample(b, True)
            sample(DB - 1, False)

            def gates(j):
                with act.Fori(0, 4) as i:
                    for x, ps in (("A", psA), ("B", psB)):
                        act.wait_ge(s[f"g{x}"], i + (4 * j + 1))
                        k = "AB".index(x)
                        nc.scalar.activation(c3(sg[k][:, :]), cols(ps), ACT.Sigmoid).then_inc(s[f"sg{x}"], 1)

            gates(0)
            act.wait_ge(s["mA"], 4)
            act.wait_ge(s["mB"], 4)
            with act.Fori(0, NT) as i:
                act.wait_ge(s["cc_done"], i + 1)
                nc.scalar.copy(c3(cc[:, :]), cols(psA)).then_inc(s["cc_copied"], 1)
                act.wait_ge(s["ul_tr"], i + 1)
                nc.scalar.copy(utok[:, :], mi[0][0:18, 0:P]).then_inc(s["ul_copied"], 1)
                act.wait_ge(s["ul_copied"], i + 1)
                act.dma_start(out["conv_prompt"][0, 0][:, bass.ds(i * P, P)], utok[0:2, :]).then_inc(s["ul_out"], 16)
                act.dma_start(out["conv_sample"][0].rearrange("b t c -> (b t) c")[:, bass.ds(i * P, P)], utok[2:18, :]).then_inc(s["ul_out"], 16)
                act.wait_ge(s["y_done"], i + 1)
                nc.scalar.copy(ahi[:, bass.ds(i, 1), :], yc[:, None, :]).then_inc(s["chi_done"], 1)
                act.wait_ge(s["ul_out"], i * 32 + 32)
            act.wait_ge(s["clo_done"], NT)
            gates(1)
            act.wait_ge(s["mA"], 8)
            act.wait_ge(s["mB"], 8)
            for j, g in enumerate(POOL_ORDER):
                act.wait_ge(s["gemm_done"], 1 + j + 1)
                if j:
                    act.wait_ge(s["pf_done"], j)
                    act.wait_ge(s["pt2_tr"], j)
                nc.scalar.copy(c3(pb[:, LEAD:LEAD + T]), cols(GP[j % 2])).then_inc(s["pcopied"], 1)
                act.wait_ge(s["pf_done"], j + 1)
                nc.scalar.copy(ahi[:, g, :], yp[:, :]).then_inc(s["phi_done"], 1)
                act.wait_ge(s["pt2_tr"], j + 1)
                if j:
                    act.wait_ge(s["pt2_out"], 32 * j)
                link(nc.scalar.copy(ptok[0:PST, 0, :], mi[0][0:PST, 0:P]))
                nc.scalar.copy(ptok[:, 1, :], mi[0][0:NS, P:2 * P]).then_inc(s["pt2_copied"], 1)
                act.wait_ge(s["pt2_copied"], j + 1)
                act.dma_start(out["pool_prompt"][0, 0][:, g * P:(g + 1) * P], ptok[0:PST, 0, :]).then_inc(s["pt2_out"], 16)
                act.dma_start(out["pool_sample"][0, :, PST - DS:PST, g * P:(g + 1) * P], ptok[:, 1, :]).then_inc(s["pt2_out"], 16)
            for j, g in enumerate(POOL_ORDER):
                act.wait_ge(s["gemm_done"], 5 + j + 1)
                nc.scalar.activation(c3(ahi[:, g, :]), cols(GP[j % 2]), ACT.Copy,
                                     scale=vecs[:, V_PS + g:V_PS + g + 1]).then_inc(s["mhi_done"], 1)
            act.wait_ge(s["plo_done"], NT)
            gates(2)
            act.wait_ge(s["gA"], 12)
            act.wait_ge(s["gB"], 12)
            for k in range(KD):
                act.wait_ge(s["mB" if k % 2 else "mA"], 8 + k // 2 + 1)
                nc.scalar.copy(hhi[:, k, :], merged[:, k, :]).then_inc(s["hhi_done"], 1)
            act.wait_ge(s["mB"], 12)
            act.wait_ge(s["mA"], 12)
            for k in range(KD):
                if k >= 2:
                    act.wait_ge(s["wo_ev"], k - 1)
                act.dma_start(xr[k % 2][:, :], x_keep[:, k, :]).then_inc(s[f"xr{k % 2}_in"], 16)
            for k in range(KD):
                act.wait_ge(s["d_done"], k + 1)
                if k >= 2:
                    act.wait_ge(s["var_done"], k - 1)
                nc.scalar.activation(tmp[k % 2][:, :], merged[:, k, :], ACT.Square).then_inc(s["sq_done"], 1)
            act.wait_ge(s["var_done"], KD)
            act.wait_ge(s["consts"], 3)
            nc.scalar.activation(c3(rstd[:, :]), cols(psB), ACT.Sqrt, bias=eps[:, :]).then_inc(s["sd_done"], 1)
            for k in range(KD):
                act.wait_ge(s["xn_done"], k + 1)
                if k >= 2:
                    act.wait_ge(s["hlo_done"], 2 * KD + k - 1)
                nc.scalar.activation(tmp[k % 2][:, 0:NP], merged[:, k, 0:NP], ACT.Identity, bias=mod[:, SH2 + k, 0:1],
                                     scale=mod[:, SC2 + k, 0:1]).then_inc(s["hp_done"], 1)
                act.wait_ge(s["hp_done"], KD + k + 1)
                act.wait_ge(s["hs_done"], KD + k + 1)
                nc.scalar.copy(hhi[:, k, :], tmp[k % 2][:, :]).then_inc(s["hhi_done"], 1)

            def silu(i, k):
                n = 2 * i + (k + 1)
                act.wait_ge(s["fg_done"], n)
                if not isinstance(i, int) or i:
                    act.wait_ge(s["ft_done"], n - 2)
                nc.scalar.activation(c3(sil[k][:, :]), cols(psA), ACT.Silu).then_inc(s["sil_done"], 1)

            def f_high(i, k):
                n = 2 * i + (k + 1)
                act.wait_ge(s["ft_done"], n)
                if not isinstance(i, int) or i:
                    act.wait_ge(s["dn_done"], KD * i)
                nc.scalar.copy(ahi[:, k, :], ft[k][:, :]).then_inc(s["fhi_done"], 1)

            silu(0, 0)
            f_high(0, 0)
            silu(0, 1)
            f_high(0, 1)
            with act.Fori(1, FFIT) as i:
                silu(i, 0)
                f_high(i, 0)
                silu(i, 1)
                f_high(i, 1)
            def normal(t):
                n = P if t < QT else NS
                act.wait_ge(s["yr_done"], t + 1)
                if t >= 3:
                    act.wait_ge(s[f"y{t % 3}_out"], 16 * (t // 3))
                nc.scalar.activation(yo[t % 3][0:n, :], flat(GP[t % 2])[0:n, 0:D], ACT.Identity, bias=mv[0:n, t % 2, 4:5],
                                     scale=mv[0:n, t % 2, 3:4]).then_inc(s["yn_done"], 1)

            for t in range(QT + 1):
                n = P if t < QT else NS
                act.wait_ge(s["yv_done"], t + 1)
                nc.scalar.activation(mv[0:n, t % 2, 2:3], mv[0:n, t % 2, 1:2], ACT.Sqrt, bias=eps[0:n, :]).then_inc(s["ysd_done"], 1)
                normal(t)

        @block.vector
        def _(dve):
            link = Links(dve, s["dve_link"])
            V = nc.vector

            def modulate(k, x, y, shift, scale):
                new = y[:, NP:TU].rearrange("p (b t) -> p b t", b=DB)
                link(V.tensor_tensor(new, x[:, NP:TU].rearrange("p (b t) -> p b t", b=DB),
                                     mod[:, scale + k, 1:NCOND, None].to_broadcast([P, DB, DS]), ALU.mult))
                return V.tensor_tensor(new, new, mod[:, shift + k, 1:NCOND, None].to_broadcast([P, DB, DS]), ALU.add)

            dve.wait_ge(s["setup_tr"], 1)
            link(V.memset(ct[:, :, :], 0.0))
            V.tensor_copy(ct[:, :, 0:NCOND], mi[0][:, 0:KD * NCOND].rearrange("p (a b) -> p a b", a=KD)).then_inc(s["setup_copied"], 1)
            dve.wait_ge(s["setup_tr"], 2)
            link(V.tensor_copy(vecs[:, :], mi[1][:, 0:NVEC]))
            dve.wait_ge(s["setup_tr"], 3)
            V.tensor_copy(pst[:, :, :].rearrange("p a b -> p (a b)"), psA[:, 0, 0:NT * DB * PST]).then_inc(s["setup_copied"], 1)
            dve.wait_ge(s["setup_tr"], 4)
            V.tensor_copy(cst[:, :, :].rearrange("p a b -> p (a b)"), psA[:, 1, 0:NT * DB * 2]).then_inc(s["setup_copied"], 1)
            dve.wait_ge(s["consts"], 4)
            link(V.tensor_reduce(fold[:, :], foldh[:, :, :].rearrange("p h t -> p t h"), mybir.AxisListType.X, ALU.add))
            link(V.tensor_reduce(maskn[:, :], maskh[:, :, :].rearrange("p h t -> p t h"), mybir.AxisListType.X, ALU.min))
            for g in range(0, 18, 2):
                dve.wait_ge(s["x_tr"], g + 1)
                V.tensor_copy(x_group(g), x_bank(g)).then_inc(s["x_dve"], 1)
            V.memset(xt[:, :, TU:T], 0.0).then_inc(s["x_dve"], 1)

            for j in range(4):
                mod_chunk(dve, j)
            dve.wait_ge(s["mod_done"], 4)
            V.tensor_scalar(mod[:, SC1:SC1 + KD, :], mod[:, SC1:SC1 + KD, :], 1.0, None, ALU.add).then_inc(s["sc1_done"], 1)
            for j in range(2):
                link(V.memset(ht[j][:, TU:T], 0.0))
            dve.wait_ge(s["sc1_done"], 1)
            dve.wait_ge(s["x_act"], 9)
            dve.wait_ge(s["x_dve"], 9)
            dve.wait_ge(s["eye"], 2)

            def h_low(k):
                dve.wait_ge(s["hhi_done"], k + 1)
                V.tensor_tensor(hlo[:, k, :], ht[k % 2][:, :], hhi[:, k, :].bitcast(F32), ALU.subtract).then_inc(s["hlo_done"], 1)

            for k in range(KD):
                if k >= 2:
                    dve.wait_ge(s["hlo_done"], k - 1)
                modulate(k, xt[:, k, :], ht[k % 2][:, :], SH1, SC1).then_inc(s["hs_done"], 1)
                if k:
                    h_low(k - 1)
            h_low(KD - 1)
            dve.wait_ge(s["gemm_done"], 1)
            dve.wait_ge(s["st_in"], 48)
            dve.wait_ge(s["hlo_done"], KD)
            link(V.tensor_scalar(c3(z8[:, :]), cols(psA, H), bfor[:, 0:1], None, ALU.add))
            V.scalar_tensor_tensor(out=e8[:, :], in0=z8[:, :], scalar=-1.0, in1=z8[:, :], op0=ALU.mult, op1=ALU.min).then_inc(s["z_done"], 1)
            link(V.tensor_scalar(nl8[:, :], z8[:, :], 0.0, None, ALU.min))
            dve.wait_ge(s["e_done"], 1)
            V.tensor_tensor(nl8[:, :], nl8[:, :], e8[:, :], ALU.subtract).then_inc(s["lf_done"], 1)
            dve.wait_ge(s["lf_done"], 1)
            dve.wait_ge(s["consts"], 2)
            V.tensor_tensor_scan(z8[:, 0:NP], ones[0:H, 0:1].to_broadcast([H, NP]), nl8[:, 0:NP], 0.0,
                                 ALU.mult, ALU.subtract).then_inc(s["scan_done"], 1)

            mod_chunk(dve, 4)
            mod_chunk(dve, 5)
            for first, last in ((0, 1), (1, HP)):
                with dve.Fori(first, last) as p:
                    link.enter(p - first, 3 + 2 * NTILE)
                    dve.wait_ge(s["qhi_done"], p + 1)
                    if first:
                        dve.wait_ge(s["s_done"], p * NTILE)
                    link(V.scalar_tensor_tensor(out=c3(qlo[:, :]), in0=cols(psA), scalar=HD ** -0.5,
                                                in1=c3(qhi[:, :].bitcast(F32)), op0=ALU.mult, op1=ALU.subtract))
                    V.tensor_scalar(q_s[:, bass.ds(p, 1), :], psA[:, 2:3, SC:SC + NS], HD ** -0.5, None, ALU.mult).then_inc(s["ql_done"], 1)
                    if not first:
                        mod_chunk(dve, 6)
                        mod_chunk(dve, 7)
                    dve.wait_ge(s["kv_done"], p + 1)
                    link(V.tensor_copy(khi[:, :], kv[:, :]))
                    link(V.tensor_tensor(klo[:, :], kv[:, :], khi[:, :].bitcast(F32), ALU.subtract))
                    V.tensor_copy(k_s[:, bass.ds(p, 1), :], kv[:, None, NP:TU]).then_inc(s["kl_done"], 1)
                    if not first:
                        dve.wait_ge(s["lfnew_in"], 16 * DB)
                        dve.wait_ge(s["lfp_copied"], 1)
                        V.tensor_tensor_scan(dsamp[:, :], ones[0:NS, 0:1].to_broadcast([NS, LK]), lfall[:, :], 0.0,
                                             ALU.mult, ALU.subtract).then_inc(s["scan_done"], 1)
                        for j in range(8, ADAC):
                            mod_chunk(dve, j)
                        for out_ in ("nds_out", "ndp_out"):
                            dve.wait_ge(s[out_], 16)
                        dve.wait_ge(s["early_out"], 32)
                    dve.wait_ge(s["decay_in"], p * 32 + 32)

                    def scores_max(n):
                        r, i = n % 2, n // 2
                        w = (i + 1) * P
                        dve.wait_ge(s["s_done"], p * NTILE + (n + 1))
                        if n >= 2:
                            dve.wait_ge(s["tr_done"], p * NG + (LAST_GROUP[n - 2] + 1))
                        elif first:
                            dve.wait_ge(s["tr_done"], p * NG)
                        apart(dve)
                        link(V.tensor_tensor_reduce(prob[n % 2][:, 0:w], flat(GP[n % 2])[:, 0:w], decay[:, r, 0:w],
                                                    1.0, NEG, ALU.add, ALU.max, rowmax[:, n % 2:n % 2 + 1]))
                        V.tensor_scalar(negmax[:, n % 2:n % 2 + 1], rowmax[:, n % 2:n % 2 + 1], -1.0, None,
                                        ALU.mult).then_inc(s["mx_done"], 1)

                    def normalise(n):
                        w = (n // 2 + 1) * P
                        dve.wait_ge(s["p_done"], p * NTILE + (n + 1))
                        link(V.reciprocal(rowinv[:, n % 2:n % 2 + 1], rowsum[:, n % 2:n % 2 + 1]))
                        V.tensor_scalar(prob[n % 2][:, 0:w], prob[n % 2][:, 0:w], rowinv[:, n % 2:n % 2 + 1], None,
                                        ALU.mult).then_inc(s["pn_done"], 1)

                    def pt_low(n):
                        for g, (t, blocks) in enumerate(GROUPS):
                            if t == n:
                                m, nb = PAIRS.index((n // 2, blocks[0])), len(blocks)
                                dve.wait_ge(s["pth_done"], p * NG + (g + 1))
                                V.tensor_tensor(ptlo[m % 2][:, 0:nb, n % 2, :],
                                                mi[g % 2][:, 0:nb * P].rearrange("p (a b) -> p a b", a=nb),
                                                pthi[m % 2][:, 0:nb, n % 2, :].bitcast(F32), ALU.subtract).then_inc(s["ptl_done"], 1)

                    def a_low(i):
                        for r in range(2):
                            rows = slice(HD * r, HD * r + HD)
                            dve.wait_ge(s["ah_done"], p * NTILE + (2 * i + r + 1))
                            V.tensor_tensor(alo[rows, bass.ds(p, 1), i * P:(i + 1) * P], GP[i % 2][rows, 2:3, r * P:(r + 1) * P],
                                            ahi[rows, bass.ds(p, 1), i * P:(i + 1) * P].bitcast(F32),
                                            ALU.subtract).then_inc(s["al_done"], 1)

                    for n in range(2):
                        scores_max(n)
                    for n in range(2):
                        normalise(n)
                    for i in range(QT):
                        pt_low(2 * i)
                        if i + 1 < QT:
                            scores_max(2 * i + 2)
                        pt_low(2 * i + 1)
                        if i + 1 < QT:
                            normalise(2 * i + 2)
                            scores_max(2 * i + 3)
                            normalise(2 * i + 3)
                        a_low(i)
                link.leave(last - first)

            dve.wait_ge(s["mod_done"], ADAC)
            link(V.tensor_scalar(mod[:, SC2:SC2 + KD, :], mod[:, SC2:SC2 + KD, :], 1.0, None, ALU.add))
            g1, b1 = (vecs[:, v:v + KD, None].to_broadcast([P, KD, NCOND]) for v in (V_L1G, V_L1B))
            sc2, sh2 = (mod[:, v:v + KD, :] for v in (SC2, SH2))
            link(V.tensor_tensor(scaled[:, :, :], sc2, b1, ALU.mult))
            link(V.tensor_tensor(sh2, sh2, scaled[:, :, :], ALU.add))
            link(V.tensor_tensor(sc2, sc2, g1, ALU.mult))
            link(V.tensor_scalar(aln[:, :], vecs[:, V_L1G:V_L1G + 2 * KD], ALPHA, None, ALU.mult))

            V.tensor_copy(alo[:, :, TU:T], zeros[:, :].rearrange("p (a b) -> p a b", a=NT)).then_inc(s["pad_done"], 1)
            dve.wait_ge(s["qbd_zero"], 1)
            dve.wait_ge(s["kst"], 32 * HP)
            dve.wait_ge(s["vst"], 32 * HP)

            def queries(b):
                for r in range(2):
                    rows = slice(HD * r, HD * r + HD)
                    V.tensor_copy(qbd[rows, :].rearrange("p (a c) -> p a c", c=80)[:, :, r * DS:(r + 1) * DS],
                                  q_s[rows, :, bass.ds(b * DS, DS)]).then_inc(s["qbd_done"], 1)
                V.tensor_copy(kt_s[:, :, PAST:LK], k_s[:, :, bass.ds(b * DS, DS)]).then_inc(s["qbd_done"], 1)

            def keys_t(b, g):
                dve.wait_ge(s["kt_tr"], b * 2 * HP + (g + 1))
                V.tensor_copy(kt_group(g), mi[1][:, :]).then_inc(s["kt_dve"], 1)

            def sample(b, more):
                dve.wait_ge(s["dec_in"], b * 64 + 64)
                link(V.tensor_tensor(decs[:, KH:LR], decs[:, KH:LR], maskn[:, :], ALU.add))
                dve.wait_ge(s["ss_done"], b + 1)
                apart(dve)
                link(V.tensor_tensor_reduce(decs[:, :], flat(psA)[:, 0:LR], decs[:, :], 1.0, NEG, ALU.add, ALU.max,
                                            rowmax[:, 0:1]))
                link(V.tensor_scalar(other[0:NS, :], rowmax[NS:2 * NS, 0:1], -1.0, None, ALU.mult))
                link(V.tensor_scalar(other[NS:2 * NS, :], rowmax[0:NS, 0:1], -1.0, None, ALU.mult))
                V.scalar_tensor_tensor(out=negmax[:, 0:1], in0=rowmax[:, 0:1], scalar=-1.0, in1=other[:, :], op0=ALU.mult,
                                       op1=ALU.min).then_inc(s["sm_done"], 1)
                if more:
                    queries(b + 1)
                    keys_t(b + 1, 1)
                    keys_t(b + 1, 3)
                dve.wait_ge(s["se_done"], b + 1)
                link(V.tensor_copy(other[0:NS, :], rowsum[NS:2 * NS, 0:1]))
                link(V.tensor_copy(other[NS:2 * NS, :], rowsum[0:NS, 0:1]))
                link(V.tensor_tensor(other[:, :], other[:, :], rowsum[:, 0:1], ALU.add))
                link(V.reciprocal(rowinv[:, 0:1], other[:, :]))
                V.tensor_scalar(decs[:, :], decs[:, :], rowinv[:, 0:1], None, ALU.mult).then_inc(s["sp_done"], 1)
                dve.wait_ge(s["pt_tr"], b * 2 + 2)
                V.tensor_copy(ptrs[0:DS, NPG // 2, :], psB[0:DS, 1, 0:P]).then_inc(s["pt_dve"], 1)
                if more:
                    keys_t(b + 1, 5)
                dve.wait_ge(s["ov_done"], b + 1)
                V.tensor_tensor(om[:, :].rearrange("p (h d) -> p h d", h=H), psB[:, 2, :].rearrange("p (h d) -> p h d", h=H),
                                blockmask[:, :, None].to_broadcast([P, H, HD]), ALU.mult).then_inc(s["om_done"], 1)
                if more:
                    keys_t(b + 1, 7)
                dve.wait_ge(s["sah_done"], b + 1)
                V.tensor_tensor(alo[:, :, bass.ds(b * DS + NP, DS)], att_s,
                                ahi[:, :, bass.ds(b * DS + NP, DS)].bitcast(F32), ALU.subtract).then_inc(s["sal_done"], 1)

            queries(0)
            for g in range(1, 2 * HP, 2):
                keys_t(0, g)
            with dve.Fori(0, DB - 1) as b:
                link.enter(b, 8)
                sample(b, True)
            link.leave(DB - 1)
            sample(DB - 1, False)

            def branch(j):
                if j == 1:
                    dve.wait_ge(s["ul_out"], 32 * NT)
                if j == 2:
                    dve.wait_ge(s["pt2_out"], 32 * NT)
                with dve.Fori(0, 4) as i:
                    link.enter(i, 2 if j else 0)
                    for k, x in enumerate("AB"):
                        dve.wait_ge(s[f"b{x}"], i + (4 * j + 1))
                        to = merged[:, bass.ds(2 * i + k, 1), :].rearrange("p o (c n) -> p (o c) n", c=3)
                        g3 = c3(sg[k][:, :])
                        if j == 0:
                            V.tensor_tensor(to, cols(GP[k]), g3, ALU.mult).then_inc(s[f"m{x}"], 1)
                        else:
                            link(V.tensor_tensor(c3(part[k][:, :]), cols(GP[k]), g3, ALU.mult))
                            whole = merged[:, bass.ds(2 * i + k, 1), :]
                            V.tensor_tensor(whole, whole, part[k][:, None, :], ALU.add).then_inc(s[f"m{x}"], 1)
                link.leave(4)

            branch(0)
            dve.wait_ge(s["mA"], 4)
            dve.wait_ge(s["mB"], 4)
            link(V.memset(u[:, 0:2], 0.0))
            link(V.memset(yc[:, TU:T], 0.0))
            with dve.Fori(0, NT) as i:
                link.enter(i, 9)

                def tap(k):
                    return vecs[:, bass.ds(i + (V_CW + 4 * k), 1)]

                dve.wait_ge(s["ch_done"], i + 1)
                dve.wait_ge(s["cc_copied"], i + 1)
                V.tensor_tensor(c3(u[:, 2:2 + T]), cols(psB), c3(cc[:, :]), ALU.mult).then_inc(s["u_done"], 1)
                dve.wait_ge(s["u_done"], i + 1)
                link(V.tensor_copy(us[:, :, 2:2 + DS], u[:, 2 + NP:2 + TU].rearrange("p (b t) -> p b t", b=DB)))
                link(V.tensor_copy(us[:, :, 0:2], cst[:, bass.ds(i, 1), :].rearrange("p o (b t) -> p (o b) t", b=DB)))
                link(V.tensor_copy(ulast[:, 2:18].rearrange("p (b t) -> p b t", b=DB), us[:, :, DS:DS + 2]))
                V.tensor_copy(ulast[:, 0:2], u[:, NP:NP + 2]).then_inc(s["ul_done"], 1)
                ysmp = yc[:, NP:TU].rearrange("p (b t) -> p b t", b=DB)
                link(V.tensor_scalar(yc[:, 0:NP], u[:, 0:NP], tap(0), None, ALU.mult))
                link(V.tensor_scalar(ysmp, us[:, :, 0:DS], tap(0), None, ALU.mult))
                for k in (1, 2):
                    link(V.scalar_tensor_tensor(out=yc[:, 0:NP], in0=u[:, k:k + NP], scalar=tap(k), in1=yc[:, 0:NP],
                                                op0=ALU.mult, op1=ALU.add))
                    link(V.scalar_tensor_tensor(out=ysmp, in0=us[:, :, k:k + DS], scalar=tap(k), in1=ysmp,
                                                op0=ALU.mult, op1=ALU.add))
                dve.wait_ge(s["cb_done"], i + 1)
                V.tensor_tensor(c3(yc[:, :]), cols(psA), c3(yc[:, :]), ALU.mult).then_inc(s["y_done"], 1)
                dve.wait_ge(s["chi_done"], i + 1)
                V.tensor_tensor(alo[:, bass.ds(i, 1), :], yc[:, None, :], ahi[:, bass.ds(i, 1), :].bitcast(F32),
                                ALU.subtract).then_inc(s["clo_done"], 1)
                dve.wait_ge(s["clo_done"], i + 1)
                dve.wait_ge(s["ul_tr"], i + 1)
            link.leave(NT)
            branch(1)
            dve.wait_ge(s["mA"], 8)
            dve.wait_ge(s["mB"], 8)
            link(V.memset(ps0[:, :, 0:1], 0.0))
            link(V.memset(pb[:, 0:LEAD], 0.0))
            link(V.memset(yp[:, TU:T], 0.0))
            dve.wait_ge(s["consts"], 4 + LEAD)
            for j, g in enumerate(POOL_ORDER):
                win = POOL_WIN[g]
                link(V.tensor_copy(ps0[:, :, 1:1 + PST], pst[:, g, :].rearrange("p (b t) -> p b t", b=DB)))
                dve.wait_ge(s["pcopied"], j + 1)
                new = pb[:, LEAD + NP:LEAD + TU].rearrange("p (b t) -> p b t", b=DB)
                link(V.tensor_copy(ps0[:, :, LEAD:], new))
                x, xs = pb, ps0
                for k, (y, ys) in enumerate(((w1, ps1), (w2, ps2), (w1, ps1), (w2, ps2))[:g + 1]):
                    d = 2 ** k
                    lo = 2 * d - 1
                    link(V.tensor_tensor(y[:, lo:LEAD + NP], x[:, lo:LEAD + NP], x[:, lo - d:LEAD + NP - d], ALU.add))
                    link(V.tensor_tensor(ys[:, :, lo:], xs[:, :, lo:], xs[:, :, lo - d:LEAD + DS - d], ALU.add))
                    x, xs = y, ys
                if j:
                    dve.wait_ge(s["phi_done"], j)
                link(V.scalar_tensor_tensor(out=yp[:, 0:NP], in0=x[:, LEAD:LEAD + NP], scalar=1.0 / win,
                                            in1=pb[:, LEAD:LEAD + NP], op0=ALU.mult, op1=ALU.subtract))
                link(V.tensor_tensor(x[:, LEAD:LEAD + win - 1], x[:, LEAD:LEAD + win - 1], recip[:, 0:win - 1], ALU.mult))
                link(V.tensor_tensor(yp[:, 0:win - 1], x[:, LEAD:LEAD + win - 1], pb[:, LEAD:LEAD + win - 1], ALU.subtract))
                V.scalar_tensor_tensor(out=yp[:, NP:TU].rearrange("p (b t) -> p b t", b=DB), in0=xs[:, :, LEAD:],
                                       scalar=1.0 / win, in1=ps0[:, :, LEAD:], op0=ALU.mult,
                                       op1=ALU.subtract).then_inc(s["pf_done"], 1)
                dve.wait_ge(s["phi_done"], j + 1)
                V.tensor_tensor(alo[:, g, :], yp[:, :], ahi[:, g, :].bitcast(F32), ALU.subtract).then_inc(s["plo_done"], 1)
                dve.wait_ge(s["plo_done"], j + 1)
            for j, g in enumerate(POOL_ORDER):
                dve.wait_ge(s["mhi_done"], j + 1)
                V.scalar_tensor_tensor(out=c3(alo[:, g, :]), in0=cols(GP[j % 2]), scalar=vecs[:, V_PS + g:V_PS + g + 1],
                                       in1=c3(ahi[:, g, :].bitcast(F32)), op0=ALU.mult, op1=ALU.subtract).then_inc(s["mlo_done"], 1)
            branch(2)
            for k in range(KD):
                dve.wait_ge(s["hhi_done"], KD + k + 1)
                V.tensor_tensor(hlo[:, k, :], merged[:, k, :], hhi[:, k, :].bitcast(F32), ALU.subtract).then_inc(s["hlo_done"], 1)
            link(V.memset(mean1[:, :], 1.0 / D))
            dve.wait_ge(s["hlo_done"], 2 * KD)
            for k in range(KD):
                t, x = tmp[k % 2], xr[k % 2]
                dve.wait_ge(s["gemm_done"], 9 + k + 1)
                link(V.tensor_scalar(c3(t[:, :]), cols(GP[k % 2]), mod[:, G1 + k, 0:1], None, ALU.mult))
                link(V.tensor_tensor(t[:, NP:TU].rearrange("p (b t) -> p b t", b=DB),
                                     GP[k % 2][:, 2, SC:SC + NS].rearrange("p (b t) -> p b t", b=DB),
                                     mod[:, G1 + k, 1:NCOND, None].to_broadcast([P, DB, DS]), ALU.mult))
                dve.wait_ge(s[f"xr{k % 2}_in"], 16 * (k // 2 + 1))
                V.scalar_tensor_tensor(out=merged[:, k, :], in0=x[:, :], scalar=ALPHA, in1=t[:, :], op0=ALU.mult,
                                       op1=ALU.add).then_inc(s["wo_ev"], 1)
            dve.wait_ge(s["mean_done"], 1)
            for k in range(KD):
                V.tensor_tensor(c3(merged[:, k, :]), c3(merged[:, k, :]), cols(psA), ALU.subtract).then_inc(s["d_done"], 1)
            dve.wait_ge(s["d_done"], KD)
            dve.wait_ge(s["sd_done"], 1)
            link(V.reciprocal(rstd[:, :], rstd[:, :]))

            def h2_low(k):
                dve.wait_ge(s["hhi_done"], 2 * KD + k + 1)
                V.tensor_tensor(hlo[:, k, :], tmp[k % 2][:, :], hhi[:, k, :].bitcast(F32), ALU.subtract).then_inc(s["hlo_done"], 1)

            for k in range(KD):
                V.tensor_tensor(merged[:, k, :], merged[:, k, :], rstd[:, :], ALU.mult).then_inc(s["xn_done"], 1)
                dve.wait_ge(s["xn_done"], k + 1)
                if k >= 2:
                    dve.wait_ge(s["hlo_done"], 2 * KD + k - 1)
                modulate(k, merged[:, k, :], tmp[k % 2][:, :], SH2, SC2).then_inc(s["hs_done"], 1)
                if k:
                    h2_low(k - 1)
            h2_low(KD - 1)
            dve.wait_ge(s["xa_done"], KD)

            def product(i, k):
                n = 2 * i + (k + 1)
                dve.wait_ge(s["fu_done"], n)
                dve.wait_ge(s["sil_done"], n)
                if not isinstance(i, int) or i:
                    dve.wait_ge(s["flo_done"], n - 2)
                V.tensor_tensor(c3(ft[k][:, :]), cols(psB), c3(sil[k][:, :]), ALU.mult).then_inc(s["ft_done"], 1)

            def f_low(i, k):
                dve.wait_ge(s["fhi_done"], 2 * i + (k + 1))
                V.tensor_tensor(alo[:, k, :], ft[k][:, :], ahi[:, k, :].bitcast(F32), ALU.subtract).then_inc(s["flo_done"], 1)

            def down(i):
                for t in range(KD):
                    ps = GP[t % 2]
                    dve.wait_ge(s["dn_done"], i * KD + (t + 1))
                    acc = merged[:, t, :]
                    g2 = mod[:, G2 + t, 0:1]
                    V.scalar_tensor_tensor(out=acc[:, 0:2 * CH].rearrange("p (c n) -> p c n", c=2), in0=ps[:, 0:2, 0:CH], scalar=g2,
                                           in1=acc[:, 0:2 * CH].rearrange("p (c n) -> p c n", c=2),
                                           op0=ALU.mult, op1=ALU.add).then_inc(s["dn_part"], 1)
                    V.scalar_tensor_tensor(out=acc[:, 2 * CH:NP], in0=ps[:, 2, 0:SC], scalar=g2, in1=acc[:, 2 * CH:NP],
                                           op0=ALU.mult, op1=ALU.add).then_inc(s["dn_part"], 1)
                    V.tensor_tensor(t64[:, t % 2, :].rearrange("p (b t) -> p b t", b=DB),
                                    ps[:, 2, SC:SC + NS].rearrange("p (b t) -> p b t", b=DB),
                                    mod[:, G2 + t, 1:NCOND, None].to_broadcast([P, DB, DS]), ALU.mult).then_inc(s["dn_ev"], 1)
                    dve.wait_ge(s["dn_ev"], i * KD + (t + 1))
                    V.tensor_tensor(acc[:, NP:TU], acc[:, NP:TU], t64[:, t % 2, :], ALU.add).then_inc(s["dn_part"], 1)

            product(0, 0)
            f_low(0, 0)
            product(0, 1)
            f_low(0, 1)
            with dve.Fori(1, FFIT) as i:
                product(i, 0)
                down(i - 1)
                f_low(i, 0)
                product(i, 1)
                f_low(i, 1)
                dve.wait_ge(s["dn_part"], i * (3 * KD))
            down(FFIT - 1)
            dve.wait_ge(s["dn_part"], 3 * KD * FFIT)
            def scale(t):
                n = P if t < QT else NS
                dve.wait_ge(s["yn_done"], t + 1)
                V.tensor_tensor(yo[t % 3][0:n, :], yo[t % 3][0:n, :], gb[0:n, 0, :], ALU.mult).then_inc(s["ym_done"], 1)

            dve.wait_ge(s["gb_in"], 32)
            for t in range(QT + 1):
                n = P if t < QT else NS
                m = mv[0:n, t % 2, :]
                dve.wait_ge(s["yt_done"], t + 1)
                for j in range(2):
                    link(V.bn_stats(bst[0:n, t % 2, j, :], GP[t % 2][0:n, j, :]))
                V.bn_aggr(m[:, 0:2], bst[0:n, t % 2, :, :].rearrange("p a b -> p (a b)")).then_inc(s["yv_done"], 1)
                if t:
                    scale(t - 1)
                dve.wait_ge(s["ysd_done"], t + 1)
                link(V.reciprocal(m[:, 3:4], m[:, 2:3]))
                V.scalar_tensor_tensor(out=m[:, 4:5], in0=m[:, 0:1], scalar=-1.0, in1=m[:, 3:4], op0=ALU.mult,
                                       op1=ALU.mult).then_inc(s["yr_done"], 1)
            scale(QT)

        @block.tensor
        def _(pe):
            mm, tr = nc.tensor.matmul, nc.tensor.transpose

            def gemm(slot, ps, blocks, hi=None, lo=None, done=None, begin=True, free=(), ready=None):
                hi, lo = hi or hhi, lo or hlo
                for sem_, n in free:
                    pe.wait_ge(sem_, n)
                for j, (b, k) in enumerate(blocks):
                    first, last = j == 0, j == len(blocks) - 1
                    if ready:
                        pe.wait_ge(ready[0], ready[1] + k + 1)
                    for c in range(3):
                        m = mm(ps[:, c, 0:CH], whi[slot][:, b, :], hi[:, k, c * CH:(c + 1) * CH], start=first, stop=False)
                        if begin and first and c == 0:
                            m.then_inc(s["w_begun"], 1)
                    for c in range(3):
                        mm(ps[:, c, 0:CH], whi[slot][:, b, :], lo[:, k, c * CH:(c + 1) * CH], start=False, stop=False)
                    for c in range(3):
                        m = mm(ps[:, c, 0:CH], wlo[slot][:, b, :], hi[:, k, c * CH:(c + 1) * CH], start=False, stop=last)
                m.then_inc(done, 1)
                return m

            all_k = [(k, k) for k in range(KD)]

            def unit(u):
                pe.wait_ge(s["w_split"], u + 1)

            pe.wait_ge(s["eye"], 2)
            pe.wait_ge(s["c_silu"], 1)
            for k in range(KD):
                m = tr(mi[0][:, k * NCOND:(k + 1) * NCOND], c9s[:, k * P:(k + 1) * P], ident[0:NCOND, 0:NCOND])
            m.then_inc(s["setup_tr"], 1)
            pe.wait_ge(s["vec_in"], 80)
            tr(mi[1][:, 0:NVEC], vtab[:, :], ident[0:NVEC, 0:NVEC]).then_inc(s["setup_tr"], 1)
            pe.wait_ge(s["st_in"], 48)
            for k in range(NT):
                m = tr(psA[:, 0, k * DB * PST:(k + 1) * DB * PST], stok[:, k * P:(k + 1) * P], ident[0:DB * PST, 0:DB * PST])
            m.then_inc(s["setup_tr"], 1)
            for k in range(NT):
                m = tr(psA[:, 1, k * 2 * DB:(k + 1) * 2 * DB], ctok[:, k * P:(k + 1) * P], ident[0:2 * DB, 0:2 * DB])
            m.then_inc(s["setup_tr"], 1)
            pe.wait_ge(s["x_in"], 48)
            for g in range(18):
                if g >= 3:
                    pe.wait_ge(s["x_act" if (g - 3) % 2 else "x_dve"], (g - 3) // 2 + 1)
                for j in range(4):
                    if g < 16:
                        m = tr(psB[:, g % 3, j * P:(j + 1) * P], xtok[:, 4 * (g % 2) + j, (g // 2) * P:(g // 2 + 1) * P], ident[:, :])
                    else:
                        k = 4 * (g - 16) + j
                        m = tr(psB[:, g % 3, j * NS:(j + 1) * NS], xtok[0:NS, QT, k * P:(k + 1) * P], ident[0:NS, 0:NS])
                m.then_inc(s["x_tr"], 1)
            pe.wait_ge(s["setup_copied"], 3)

            def ada_mm(j):
                pe.wait_ge(ada_in[j % 2], 16 * (j // 2 + 1))
                if j >= 2:
                    pe.wait_ge(s["mod_done"], j - 1)
                for k in range(KD):
                    for g in range(4):
                        m = mm(mi[j % 2][32 * g:32 * g + 32, 0:P], ct[:, k, :], ada[j % 2][:, k, g * P:(g + 1) * P],
                               start=k == 0, stop=k == KD - 1)
                m.then_inc(s["ada_used"], 1)

            def ada_tr(j):
                pe.wait_ge(s["modrow_done"], j + 1)
                tr(mi[j % 2][:, P:2 * P], modrow[:, j % 2, :], ident[:, :]).then_inc(s["mod_tr"], 1)

            for j in range(4):
                ada_mm(j)
                if j:
                    ada_tr(j - 1)
            ada_tr(3)
            pe.wait_ge(s["setup_copied"], 3)
            unit(U_F)
            gemm(0, psA, all_k, done=s["gemm_done"], ready=(s["hlo_done"], 0))
            pe.wait_ge(s["lfp_in"], 16 * (DB - 3) * NPG)
            pe.wait_ge(s["lfq_in"], 16 * 3 * NPG)
            pe.wait_ge(s["x_dve"], 9)
            pe.wait_ge(s["x_act"], 9)
            for j in range(2):
                for g in range(4 * j, 4 * j + 4):
                    m = tr(psB[0:NS, j, (g % 4) * P:(g % 4 + 1) * P], lfpast[:, g, :, :].rearrange("p b h -> p (b h)"), ident[:, :])
                m.then_inc(s["lfp_tr"], 1)
            ada_mm(4)
            ada_mm(5)

            def lf_transposes():
                pe.wait_ge(s["lf_done"], 1)
                tr(psB[0:NS, 2, P:P + H], nl8[:, NP:TU], ident[0:H, 0:H])
                for g in range(QT):
                    m = tr(psB[:, 2, g * H:(g + 1) * H], nl8[:, g * P:(g + 1) * P], ident[0:H, 0:H])
                m.then_inc(s["lf_tr"], 1)

            for first, last in ((0, 1), (1, HP)):
                with pe.Fori(first, last) as p:
                    if first:
                        pe.wait_ge(s["al_done"], p * NTILE - 2)
                    unit(p * 3 + U_QKV)
                    if not first:
                        pe.wait_ge(s["z_done"], 1)
                    gemm(1, psA, all_k, done=s["q_done"])
                    if not first:
                        lf_transposes()
                        for j in (4, 5):
                            ada_tr(j)
                        for j in (6, 7):
                            ada_mm(j)
                        pe.wait_ge(s["lfp_copied"], 1)
                        pe.wait_ge(s["lf_copied"], 2)
                    unit(p * 3 + (U_QKV + 1))
                    gemm(2, psB, all_k, done=s["k_done"], free=((s["al_done"], p * NTILE),) if first else ())
                    if not first:
                        for j in (6, 7):
                            ada_tr(j)
                        for j in (8, 9):
                            ada_mm(j)
                    unit(p * 3 + (U_QKV + 2))
                    gemm(0, psA, all_k, done=s["v_done"], free=((s["ql_done"], p + 1),))

                    def token_major(ps, which):
                        for n in range(QT):
                            m = tr(ps[:, n // 4, (n % 4) * P:(n % 4 + 1) * P], kv[:, n * P:(n + 1) * P], ident[:, :])
                        m.then_inc(s["tok_tr"], 1)
                        tr(ps[0:NS, 2, 0:P], kv[:, NP:TU], ident[:, :]).then_inc(s["tok_tr"], 1)

                    if not first:
                        for j in (8, 9):
                            ada_tr(j)
                        for j in (10, 11):
                            ada_mm(j)
                    pe.wait_ge(s["kv_done"], p + 1)
                    token_major(psB, 0)
                    if not first:
                        for j in (10, 11):
                            ada_tr(j)
                    pe.wait_ge(s["vf_done"], p + 1)
                    token_major(psA, 1)

                    def scores(n):
                        r, i = n % 2, n // 2
                        rows = slice(HD * r, HD * r + HD)
                        q = slice(i * P, (i + 1) * P)
                        if n < 2:
                            pe.wait_ge(s["tok_copied"], p * 2 + (2 - n))
                            pe.wait_ge(s["kl_done"], p + 1)
                        else:
                            pe.wait_ge(s["mx_done"], p * NTILE + (n - 1))
                        for c in range(0, (i + 1) * P, 512):
                            k = slice(c, min(c + 512, (i + 1) * P))
                            o = GP[n % 2][:, c // 512, 0:k.stop - c]
                            diag = k.stop == (i + 1) * P
                            mm(o, qhi[rows, q], khi[rows, k], start=True, stop=False)
                            mm(o, qhi[rows, q], klo[rows, k], start=False, stop=False)
                            m = mm(o, qlo[rows, q], khi[rows, k], start=False, stop=not diag)
                        m = mm(GP[n % 2][:, i * P // 512, i * P % 512:i * P % 512 + P], identr[:, :], maskr[:, :],
                               start=False, stop=True)
                        m.then_inc(s["s_done"], 1)

                    def transposes(n):
                        pe.wait_ge(s["pn_done"], p * NTILE + (n + 1))
                        for g, (t, blocks) in enumerate(GROUPS):
                            if t != n:
                                continue
                            if g >= 2:
                                pe.wait_ge(s["ptl_done"], p * NG + (g - 1))
                            for j, kb in enumerate(blocks):
                                m = tr(mi[g % 2][:, j * P:(j + 1) * P], prob[n % 2][:, kb * P:(kb + 1) * P], ident[:, :])
                            m.then_inc(s["tr_done"], 1)

                    def values(i):
                        o = GP[i % 2][:, 2, 0:2 * P]
                        if i >= 2:
                            pe.wait_ge(s["al_done"], p * NTILE + 2 * (i - 1))
                        if i == 0:
                            pe.wait_ge(s["vl_done"], p + 1)
                        for m, (t, j0) in enumerate(PAIRS):
                            if t != i:
                                continue
                            blocks = range(j0, min(j0 + 4, i + 1))
                            pe.wait_ge(s["ptl_done"], p * NG + (GROUPS.index((2 * i + 1, list(blocks))) + 1))
                            for j, kb in enumerate(blocks):
                                ph, pl = (x[m % 2][:, j, :, :].rearrange("p r q -> p (r q)") for x in (pthi, ptlo))
                                mm(o, vhi[:, kb, :], ph, start=kb == 0, stop=False)
                                mm(o, vhi[:, kb, :], pl, start=False, stop=False)
                                mo = mm(o, vlo[:, kb, :], ph, start=False, stop=kb == i)
                        mo.then_inc(s["o_done"], 1)

                    scores(0)
                    scores(1)
                    for i in range(QT):
                        for n in (2 * i, 2 * i + 1):
                            transposes(n)
                            if n + 2 < NTILE:
                                scores(n + 2)
                        values(i)

            pe.wait_ge(s["al_done"], NTILE * HP)

            def keys_t(b, groups):
                for g in groups:
                    if g % HP == 0:
                        pe.wait_ge(s["kpg_in"], b * (16 * NPG) + 16 * NPG)
                    if g >= 2:
                        pe.wait_ge(s["kt_dve" if g % 2 else "kt_act"], b * HP + g // 2)
                    for j in range(4):
                        m = tr(mi[g % 2][:, j * P:(j + 1) * P], kpage[:, 4 * (g // HP) + j, (g % HP) * P:(g % HP + 1) * P], ident[:, :])
                    m.then_inc(s["kt_tr"], 1)

            def sample(b, more):
                pe.wait_ge(s["qbd_done"], b * 3 + 3)
                pe.wait_ge(s["kt_act"], b * HP + HP)
                pe.wait_ge(s["kt_dve"], b * HP + HP)
                for bank, w in ((0, KH), (1, DS)):
                    for k in range(HP):
                        for half in range(2):
                            c = PAST if bank else half * KH
                            m = mm(psA[half * NS:(half + 1) * NS, bank, 0:w], qbd[:, k * NS:(k + 1) * NS], kt_s[:, k, c:c + w],
                                   start=k == 0, stop=k == HP - 1)
                m.then_inc(s["ss_done"], 1)
                if more:
                    keys_t(b + 1, range(5))
                pe.wait_ge(s["sp_done"], b + 1)
                apart(pe)
                for g in range(NPG // 2):
                    m = tr(psB[:, 0, g * P:(g + 1) * P], decs[:, g * P:(g + 1) * P], ident[:, :])
                m.then_inc(s["pt_tr"], 1)
                tr(psB[0:DS, 1, 0:P], decs[:, KH:LR], ident[:, :]).then_inc(s["pt_tr"], 1)
                if more:
                    keys_t(b + 1, [5])
                pe.wait_ge(s["vpg_in"], b * (16 * NPG) + 16 * NPG)
                pe.wait_ge(s["vnew_in"], b * 16 + 16)
                pe.wait_ge(s["pt_act"], b + 1)
                pe.wait_ge(s["pt_dve"], b + 1)
                hpg = NPG // 2
                for g in range(hpg):
                    for half in range(2):
                        rows = slice(half * NS, (half + 1) * NS)
                        mm(psB[rows, 2, :], ptrs[:, g, rows], vpage[:, half * hpg + g, :], start=g == 0, stop=half == 0 and g == hpg - 1)
                mm(psB[rows, 2, :], ptrs[0:DS, hpg, rows], vpage[0:DS, NPG, :], start=False, stop=True).then_inc(s["ov_done"], 1)
                if more:
                    keys_t(b + 1, [6, 7])
                pe.wait_ge(s["om_done"], b + 1)
                for k in range(HP):
                    m = mm(att_s[:, k, :], om[:, k * P:(k + 1) * P], fold[:, :], start=True, stop=True)
                m.then_inc(s["fold_done"], 1)

            keys_t(0, range(2 * HP))
            with pe.Fori(0, DB - 1) as b:
                sample(b, True)
            sample(DB - 1, False)

            def branch(j, u0, free_a, free_b, ready):
                for first, last in ((0, 1), (1, 4)):
                    with pe.Fori(first, last) as i:
                        for k, x in enumerate("AB"):
                            unit(i * 3 + (u0 + k))
                            free = (s[f"m{x}"], i + 4 * j) if first else (free_a, free_b)[k]
                            gemm((u0 + k) % RING, GP[k], all_k, done=s[f"g{x}"], free=(free,))
                        if not first:
                            for sem_, n in ready:
                                pe.wait_ge(sem_, n)
                        unit(i * 3 + (u0 + 2))
                        for k, x in enumerate("AB"):
                            gemm((u0 + 2) % RING, GP[k], [(2 * t + k, t) for t in range(NT)], ahi, alo, done=s[f"b{x}"],
                                 begin=k == 0, free=((s[f"sg{x}"], i + (4 * j + 1)),))

            branch(0, U_BRA, (s["ss_done"], DB), (s["sal_done"], DB), ((s["sal_done"], DB), (s["pad_done"], 2)))
            pe.wait_ge(s["mA"], 4)
            pe.wait_ge(s["mB"], 4)
            with pe.Fori(0, NT) as i:
                unit(i * 3 + U_CONV)
                gemm(U_CONV % RING, psA, all_k, done=s["cc_done"])
                unit(i * 3 + (U_CONV + 1))
                gemm((U_CONV + 1) % RING, psB, all_k, done=s["ch_done"])
                unit(i * 3 + (U_CONV + 2))
                gemm((U_CONV + 2) % RING, psA, all_k, done=s["cb_done"], free=((s["cc_copied"], i + 1),))
                pe.wait_ge(s["ul_done"], i + 1)
                tr(mi[0][0:18, 0:P], ulast[:, :], ident[:, :]).then_inc(s["ul_tr"], 1)
                pe.wait_ge(s["y_done"], i + 1)
            branch(1, U_BRC, (s["y_done"], NT), (s["u_done"], NT), ((s["clo_done"], NT),))
            for g in range(NT):
                u0 = U_POOL + g
                unit(u0)
                pe.wait_ge(s["mB" if g else "mA"], 8)
                if g >= 2:
                    pe.wait_ge(s["pcopied"], g - 1)
                gemm(u0 % RING, GP[g % 2], all_k, done=s["gemm_done"])
                pe.wait_ge(s["pcopied"], g + 1)
                if g:
                    pe.wait_ge(s["pt2_copied"], g)
                tr(mi[0][0:PST, 0:P], pb[:, LEAD + NP - PST:LEAD + NP], ident[:, :])
                tr(mi[0][0:NS, P:2 * P], pb[:, LEAD + NP:LEAD + TU], ident[:, :]).then_inc(s["pt2_tr"], 1)
            unit(U_POOL + NT)
            for j, g in enumerate(POOL_ORDER):
                if j >= 2:
                    pe.wait_ge(s["mlo_done"], j - 1)
                pe.wait_ge(s["plo_done"], j + 1)
                gemm((U_POOL + NT) % RING, GP[j % 2], [(g, g)], ahi, alo, done=s["gemm_done"],
                     begin=j == 0)
            branch(2, U_BRP, (s["mlo_done"], NT), (s["mlo_done"], NT), ((s["mlo_done"], NT),))
            for k in range(KD):
                unit(U_WO + k)
                pe.wait_ge(s["mB" if k else "mA"], 12)
                if k >= 2:
                    pe.wait_ge(s["wo_ev"], k - 1)
                gemm((U_WO + k) % RING, GP[k % 2], all_k, done=s["gemm_done"],
                     ready=(s["hlo_done"], KD) if k == 0 else None)
            pe.wait_ge(s["ysum_done"], KD - 2)
            for x, n in ((ysum[:, :], KD - 1), (merged[:, KD - 1, :], KD)):
                pe.wait_ge(s["wo_ev"], n)
                for c in range(3):
                    m = mm(psA[:, c, 0:CH], mean1[:, :], x[:, c * CH:(c + 1) * CH], start=n == KD - 1, stop=n == KD)
            m.then_inc(s["mean_done"], 1)
            pe.wait_ge(s["wo_ev"], KD)
            for k in range(KD):
                pe.wait_ge(s["sq_done"], k + 1)
                for c in range(3):
                    m = mm(psB[:, c, 0:CH], mean1[:, :], tmp[k % 2][:, c * CH:(c + 1) * CH], start=k == 0, stop=k == KD - 1)
                m.then_inc(s["var_done"], 1)

            def hidden(u0, slot, free_a=(), free_b=(), ready=None):
                unit(u0)
                gemm(slot % RING, psA, all_k, done=s["fg_done"], free=free_a, ready=ready)
                unit(u0 + 1)
                gemm((slot + 1) % RING, psB, all_k, done=s["fu_done"], free=free_b)

            def downs(i, u0, slot):
                for h in range(2):
                    unit(u0 + h)
                    for t in range(4 * h, 4 * h + 4):
                        if t < 2:
                            pe.wait_ge(s["sil_done" if t == 0 else "ft_done"], 2 * FFIT if isinstance(i, int) else 2 * i + 3)
                        else:
                            pe.wait_ge(s["dn_ev"], i * KD + (t - 1))
                        if t == 0:
                            pe.wait_ge(s["flo_done"], 2 * i + 2)
                        gemm((slot + h) % RING, GP[t % 2], [(k * 4 + t % 4, k) for k in range(2)], ahi, alo, done=s["dn_done"],
                             begin=t == 4 * h)

            pe.wait_ge(s["d_done"], KD)
            hidden(U_FF0, U_FF0, free_b=[(s["sd_done"], 1)], ready=(s["hlo_done"], 2 * KD))
            hidden(U_FF0 + 2, U_FF0 + 2, [(s["sil_done"], 1)], [(s["ft_done"], 1)])
            with pe.Fori(1, FFIT) as i:
                u0 = i * 6 + (U_FF - 6)
                hidden(u0, U_FF, [(s["sil_done"], 2 * i)], [(s["ft_done"], 2 * i)])
                downs(i - 1, u0 + 2, U_FF + 2)
                hidden(u0 + 4, U_FF + 4, [(s["dn_ev"], i * KD - 1)], [(s["dn_ev"], i * KD)])
            downs(FFIT - 1, U_FFE, U_FFE)
            pe.wait_ge(s["dn_part"], 3 * KD * FFIT)
            for t in range(QT + 1):
                n = P if t < QT else NS
                if t >= 2:
                    pe.wait_ge(s["yn_done"], t - 1)
                for k in range(KD):
                    m = tr(GP[t % 2][0:n, k // 4, (k % 4) * P:(k % 4 + 1) * P], merged[:, k, t * P:t * P + n], ident[:, :])
                m.then_inc(s["yt_done"], 1)


_INS = ["x_prompt", "x_sample", "cache_k", "cache_v", "cache_logf", "state_conv", "state_pool", "page_table", "c_prompt",
        "c_sample", "ada_w", "ada_b", "w_in", "b_forget", "conv_w", "pool_w", "pool_scale", "w_br_attn", "w_br_conv",
        "w_br_pool", "w_o", "ln1_g", "ln1_b", "w_gate_up", "w_down", "ln2_g", "ln2_b"]
_OUTS = {
    "y_prompt": (1, NP, D), "y_sample": (DB, DS, D),
    "k_prompt": (1, 1, NP, H, HD), "v_prompt": (1, 1, NP, H, HD), "logf_prompt": (1, 1, NP, H),
    "conv_prompt": (1, 1, 2, HALF), "pool_prompt": (1, 1, PST, HALF),
    "k_sample": (1, DB, DS, H, HD), "v_sample": (1, DB, DS, H, HD), "logf_sample": (1, DB, DS, H),
    "conv_sample": (1, DB, 2, HALF), "pool_sample": (1, DB, PST, HALF),
}


def kernel(**inputs):
    import concourse.bacc as bacc
    from concourse.bass_utils import run_bass_kernel_spmd

    nc = bacc.Bacc("TRN2", target_bir_lowering=False, num_devices=1, dynamic_dma_scratch_size=8192)
    arrays, a = {}, {}
    for name in _INS:
        x = np.ascontiguousarray(inputs[name])
        arrays[f"in_{name}"] = x
        a[name] = nc.dram_tensor(f"in_{name}", x.shape, mybir.dt.from_np(x.dtype), kind="ExternalInput").ap()
    out = {n: nc.dram_tensor(f"out_{n}", sh, F32, kind="ExternalOutput").ap() for n, sh in _OUTS.items()}
    build(nc, a, out)
    r = run_bass_kernel_spmd(nc, [arrays], core_ids=[0])
    return tuple(r.results[0][f"out_{n}"] for n in _OUTS)
```
